# Optimizing a Trainium2 kernel written in Bass

```python
import math
import jax, jax.numpy as jnp
from jax import lax
import numpy as np

D_MODEL = 1024
BATCH = 1
SEQ = 256
DEPTH = 1
DEC_BATCH = 1
DEC_SEQ = 1024
PAST_LEN = 128

A_HEADS = 8
A_HEAD_DIM = 64
A_WIDTH = A_HEADS * A_HEAD_DIM
A_CONV = 5
A_CHUNK = 64
B_GROUPS = ((128, 1), (512, 4), (2048, 16))
B_HEADS_PER_GROUP = 4
B_HEADS = B_HEADS_PER_GROUP * len(B_GROUPS)
B_HEAD_DIM = 64
B_WIDTH = B_HEADS * B_HEAD_DIM
B_OUT_WIDTH = B_HEADS_PER_GROUP * B_HEAD_DIM
B_BLOCK = 64
N_EXPERTS = 16
D_EXPERT = 1024
CAPACITY_FACTOR = 2
EPS = 1e-6
NEG = -1e30
SPLIT_POINTS = (3 * A_WIDTH,
                4 * A_WIDTH,
                4 * A_WIDTH + 2 * A_HEADS,
                4 * A_WIDTH + 4 * A_HEADS,
                4 * A_WIDTH + 4 * A_HEADS + 3 * B_WIDTH)
IN_WIDTH = 4 * A_WIDTH + 4 * A_HEADS + 3 * B_WIDTH + 2 * D_MODEL

kernel_name = "hybrid_deltanet_dilated_attn_ec_moe_encoder"

def rmsnorm(x, g):
    xf = x.astype(jnp.float32)
    y = xf * lax.rsqrt(jnp.mean(xf * xf, axis=-1, keepdims=True) + EPS)
    return (y * g.astype(jnp.float32)).astype(x.dtype)

def l2norm(x):
    xf = x.astype(jnp.float32)
    return xf * lax.rsqrt(jnp.sum(xf * xf, axis=-1, keepdims=True) + EPS)

def alibi_slopes():
    return jnp.asarray(2.0 ** (-8.0 * np.arange(1, B_HEADS + 1) / B_HEADS), dtype=jnp.float32)

def centred_depthwise_conv(x, w):
    c = x.shape[-1]
    pad = (A_CONV - 1) // 2
    return lax.conv_general_dilated(x, w.astype(x.dtype)[:, None, :], window_strides=(1,),
                                    padding=[(pad, pad)], dimension_numbers=('NWC', 'WIO', 'NWC'),
                                    feature_group_count=c)

def gated_delta_chunked(q, k, v, g, beta):
    bn, s, h, dk = q.shape
    dv = v.shape[-1]
    n = s // A_CHUNK
    f32 = jnp.float32

    def to_chunks(t):
        return t.astype(f32).reshape(bn, n, A_CHUNK, h, -1).transpose(1, 0, 3, 2, 4)

    qc = to_chunks(q) * (dk ** -0.5)
    kc, vc = to_chunks(k), to_chunks(v)
    gc = g.astype(f32).reshape(bn, n, A_CHUNK, h).transpose(1, 0, 3, 2)
    bc = beta.astype(f32).reshape(bn, n, A_CHUNK, h).transpose(1, 0, 3, 2)
    gcum = jnp.cumsum(gc, axis=-1)
    idx = jnp.arange(A_CHUNK)
    causal = idx[:, None] >= idx[None, :]
    strict = idx[:, None] > idx[None, :]
    decay = jnp.where(causal, jnp.exp(jnp.minimum(gcum[..., :, None] - gcum[..., None, :], 0.0)), 0.0)
    kb = kc * bc[..., None]
    lower = jnp.where(strict, jnp.einsum('nbhcd,nbhed->nbhce', kb, kc) * decay, 0.0)
    tmat = lower + jnp.eye(A_CHUNK, dtype=f32)
    rhs = jnp.concatenate([vc * bc[..., None], kb * jnp.exp(gcum)[..., None]], axis=-1)
    sol = lax.linalg.triangular_solve(tmat, rhs, left_side=True, lower=True, unit_diagonal=True)
    u, w = sol[..., :dv], sol[..., dv:]
    attn_intra = jnp.where(causal, jnp.einsum('nbhcd,nbhed->nbhce', qc, kc) * decay, 0.0)

    def step(state, inp):
        q_i, k_i, u_i, w_i, a_i, g_i = inp
        v_new = u_i - jnp.einsum('bhcd,bhdv->bhcv', w_i, state)
        o = (jnp.einsum('bhcd,bhdv->bhcv', q_i * jnp.exp(g_i)[..., None], state)
             + jnp.einsum('bhce,bhev->bhcv', a_i, v_new))
        g_last = g_i[..., -1]
        state = (state * jnp.exp(g_last)[..., None, None]
                 + jnp.einsum('bhcd,bhcv->bhdv', k_i * jnp.exp(g_last[..., None] - g_i)[..., None], v_new))
        return state, o

    state0 = jnp.zeros((bn, h, dk, dv), f32)
    _, o = lax.scan(step, state0, (qc, kc, u, w, attn_intra, gcum))
    return o.transpose(1, 0, 3, 2, 4).reshape(bn, s, h, dv)

def dilated_window_attention(q, k, v, window, dilation, slopes):
    bn, s, h, dh = q.shape
    side = window // (2 * dilation)
    length = s // dilation
    nb = -(-length // B_BLOCK)
    lp = nb * B_BLOCK
    bd = bn * dilation

    def to_phases(t):
        t = t.astype(jnp.float32).reshape(bn, length, dilation, h, dh).transpose(0, 2, 1, 3, 4)
        return jnp.pad(t.reshape(bd, length, h, dh), ((0, 0), (0, lp - length), (0, 0), (0, 0)))

    def neighbours(t):
        tb = jnp.pad(t, ((0, 0), (B_BLOCK, B_BLOCK), (0, 0), (0, 0))).reshape(bd, nb + 2, B_BLOCK, h, dh)
        return jnp.concatenate([tb[:, :-2], tb[:, 1:-1], tb[:, 2:]], axis=2)

    qb = to_phases(q).reshape(bd, nb, B_BLOCK, h, dh)
    kb = neighbours(to_phases(k))
    vb = neighbours(to_phases(v))
    qpos = jnp.arange(nb)[:, None] * B_BLOCK + jnp.arange(B_BLOCK)[None, :]
    kpos = (jnp.arange(nb)[:, None] - 1) * B_BLOCK + jnp.arange(3 * B_BLOCK)[None, :]
    delta = kpos[:, None, :] - qpos[:, :, None]
    valid = (jnp.abs(delta) <= side) & (kpos[:, None, :] >= 0) & (kpos[:, None, :] < length)
    dist = (jnp.abs(delta) * dilation).astype(jnp.float32)
    scores = (jnp.einsum('bnqhd,bnkhd->bhnqk', qb, kb) * (dh ** -0.5)
              - slopes[:, None, None, None] * dist)
    scores = jnp.where(valid, scores, NEG)
    lse = jax.nn.logsumexp(scores, axis=-1)
    p = jnp.exp(scores - lse[..., None])
    o = jnp.einsum('bhnqk,bnkhd->bnqhd', p, vb).reshape(bd, lp, h, dh)[:, :length]
    lse = lse.transpose(0, 2, 3, 1).reshape(bd, lp, h)[:, :length]
    o = o.reshape(bn, dilation, length, h, dh).transpose(0, 2, 1, 3, 4).reshape(bn, s, h, dh)
    lse = lse.reshape(bn, dilation, length, h).transpose(0, 2, 1, 3).reshape(bn, s, h)
    return o, lse

def token_mixer(hn, w_in, conv_w, a_log, dt_bias, a_norm, w_proj_a, w_proj_b, w_out):
    bn, s, _ = hn.shape
    dt = hn.dtype
    proj = jnp.einsum('bsd,dc->bsc', hn, w_in)
    qkv_a, z, beta_raw, alpha_raw, qkv_b, gates = jnp.split(proj, SPLIT_POINTS, axis=-1)

    qkv_a = jax.nn.silu(centred_depthwise_conv(qkv_a, conv_w))
    qa, ka, va = [t.reshape(bn, s, A_HEADS, A_HEAD_DIM) for t in jnp.split(qkv_a, 3, axis=-1)]
    qa, ka = l2norm(qa), l2norm(ka)
    beta = jax.nn.sigmoid(beta_raw.astype(jnp.float32)).reshape(bn, s, 2, A_HEADS)
    g = (-jnp.exp(a_log.astype(jnp.float32))
         * jax.nn.softplus(alpha_raw.astype(jnp.float32).reshape(bn, s, 2, A_HEADS) + dt_bias.astype(jnp.float32)))
    o_fwd = gated_delta_chunked(qa, ka, va, g[:, :, 0], beta[:, :, 0])
    flip = lambda t: jnp.flip(t, axis=1)
    o_bwd = flip(gated_delta_chunked(flip(qa), flip(ka), flip(va), flip(g[:, :, 1]), flip(beta[:, :, 1])))
    oa = rmsnorm(o_fwd + o_bwd, a_norm) * jax.nn.silu(z.astype(jnp.float32).reshape(bn, s, A_HEADS, A_HEAD_DIM))
    ya = jnp.einsum('bsc,cd->bsd', oa.reshape(bn, s, A_WIDTH).astype(dt), w_proj_a)

    qb, kb, vb = [t.reshape(bn, s, B_HEADS, B_HEAD_DIM) for t in jnp.split(qkv_b, 3, axis=-1)]
    slopes = alibi_slopes()
    outs, lses = [], []
    for gi, (window, dilation) in enumerate(B_GROUPS):
        hs = slice(gi * B_HEADS_PER_GROUP, (gi + 1) * B_HEADS_PER_GROUP)
        o_g, lse_g = dilated_window_attention(qb[:, :, hs], kb[:, :, hs], vb[:, :, hs], window, dilation, slopes[hs])
        outs.append(o_g)
        lses.append(lse_g)
    weights = jax.nn.softmax(jnp.stack(lses, axis=0), axis=0)
    ob = jnp.sum(weights[..., None] * jnp.stack(outs, axis=0), axis=0)
    yb = jnp.einsum('bsc,cd->bsd', ob.reshape(bn, s, B_OUT_WIDTH).astype(dt), w_proj_b)

    gate_a, gate_b = jnp.split(jax.nn.sigmoid(gates), 2, axis=-1)
    return jnp.einsum('bsd,de->bse', gate_a * ya + gate_b * yb, w_out)

def expert_choice_ffn(hn, w_router, w_gate, w_up, w_down):
    bn, s, d = hn.shape
    t = bn * s
    cap = (CAPACITY_FACTOR * t) // N_EXPERTS
    xt = hn.reshape(t, d)
    aff = jax.nn.softmax(jnp.einsum('td,de->te', xt, w_router).astype(jnp.float32), axis=-1)
    gate, idx = lax.top_k(aff.T, cap)
    xe = xt[idx]
    hdn = jax.nn.silu(jnp.einsum('ecd,edf->ecf', xe, w_gate)) * jnp.einsum('ecd,edf->ecf', xe, w_up)
    ye = jnp.einsum('ecf,efd->ecd', hdn, w_down) * gate[..., None].astype(hn.dtype)
    y = jnp.zeros_like(xt).at[idx.reshape(-1)].add(ye.reshape(-1, d))
    return y.reshape(bn, s, d)

def run_trunk(x, norm_mix, w_in, conv_w, a_log, dt_bias, a_norm, w_proj_a, w_proj_b, w_out,
              norm_ffn, w_router, w_gate, w_up, w_down, norm_final):
    for l in range(DEPTH):
        x = x + token_mixer(rmsnorm(x, norm_mix[l]), w_in[l], conv_w[l], a_log[l], dt_bias[l], a_norm[l],
                            w_proj_a[l], w_proj_b[l], w_out[l])
        x = x + expert_choice_ffn(rmsnorm(x, norm_ffn[l]), w_router[l], w_gate[l], w_up[l], w_down[l])
    return rmsnorm(x, norm_final)

def setup_inputs(seed: int = 0) -> dict:
    key = jax.random.key(seed)
    ks = jax.random.split(key, 20)
    f32 = jnp.float32
    nrm = lambda k, shape, scale: jax.random.normal(k, shape, f32) * scale
    dt0 = jnp.exp(jax.random.uniform(ks[6], (DEPTH, 2, A_HEADS), f32, math.log(1e-3), math.log(1e-1)))
    return {
        "x_prompt": nrm(ks[0], (BATCH, SEQ, D_MODEL), 1.0),
        "x_sample": nrm(ks[1], (DEC_BATCH, DEC_SEQ, D_MODEL), 1.0),
        "norm_mix": 1.0 + nrm(ks[2], (DEPTH, D_MODEL), 0.02),
        "w_in": nrm(ks[3], (DEPTH, D_MODEL, IN_WIDTH), D_MODEL ** -0.5),
        "conv_w": nrm(ks[4], (DEPTH, A_CONV, 3 * A_WIDTH), A_CONV ** -0.5),
        "a_log": jnp.log(jax.random.uniform(ks[5], (DEPTH, 2, A_HEADS), f32, 1.0, 16.0)),
        "dt_bias": dt0 + jnp.log(-jnp.expm1(-dt0)),
        "a_norm": 1.0 + nrm(ks[7], (DEPTH, A_HEAD_DIM), 0.02),
        "w_proj_a": nrm(ks[8], (DEPTH, A_WIDTH, D_MODEL), A_WIDTH ** -0.5),
        "w_proj_b": nrm(ks[9], (DEPTH, B_OUT_WIDTH, D_MODEL), B_OUT_WIDTH ** -0.5),
        "w_out": nrm(ks[10], (DEPTH, D_MODEL, D_MODEL), D_MODEL ** -0.5),
        "norm_ffn": 1.0 + nrm(ks[11], (DEPTH, D_MODEL), 0.02),
        "w_router": nrm(ks[12], (DEPTH, D_MODEL, N_EXPERTS), D_MODEL ** -0.5),
        "w_gate": nrm(ks[13], (DEPTH, N_EXPERTS, D_MODEL, D_EXPERT), D_MODEL ** -0.5),
        "w_up": nrm(ks[14], (DEPTH, N_EXPERTS, D_MODEL, D_EXPERT), D_MODEL ** -0.5),
        "w_down": nrm(ks[15], (DEPTH, N_EXPERTS, D_EXPERT, D_MODEL), D_EXPERT ** -0.5),
        "norm_final": 1.0 + nrm(ks[16], (D_MODEL,), 0.02),
    }

def reference(x_prompt, x_sample, norm_mix, w_in, conv_w, a_log, dt_bias, a_norm, w_proj_a, w_proj_b,
              w_out, norm_ffn, w_router, w_gate, w_up, w_down, norm_final):
    y_prompt = run_trunk(x_prompt, norm_mix, w_in, conv_w, a_log, dt_bias, a_norm, w_proj_a, w_proj_b, w_out,
                         norm_ffn, w_router, w_gate, w_up, w_down, norm_final)
    y_sample = run_trunk(x_sample, norm_mix, w_in, conv_w, a_log, dt_bias, a_norm, w_proj_a, w_proj_b, w_out,
                         norm_ffn, w_router, w_gate, w_up, w_down, norm_final)
    return (y_prompt, y_sample)


_drawn_inputs = setup_inputs


def setup_inputs(seed=0):
    import zlib

    import numpy as np

    out = dict(_drawn_inputs(seed))
    spreads = {}
    factors = {'norm_mix': 2.969, 'a_norm': 4.656, 'norm_ffn': 3.375, 'norm_final': 2.861}
    for name, (base, spread) in spreads.items():
        noise = np.random.default_rng([zlib.crc32(name.encode()), seed]).standard_normal(out[name].shape)
        drawn = base * np.exp(spread * noise) if base else spread * noise
        out[name] = __import__('jax').numpy.asarray(drawn.astype(out[name].dtype))
    for name, factor in factors.items():
        out[name] = (out[name] * factor).astype(out[name].dtype)
    return out
```

```python
from contextlib import ExitStack, contextmanager
import numpy as np
import concourse.bass as bass
from concourse import mybir

ALU = mybir.AluOpType
ACT = mybir.ActivationFunctionType
F32 = mybir.dt.float32
U32 = mybir.dt.uint32
AX = mybir.AxisListType
P = 128
D = 1024
KT = D // P
TS, TP = 1024, 256
T = TS + TP
NT = T // P
CHUNKS = ((0, 512), (512, 512), (1024, 256))
CONV = 5
RAW = T + 6
EPS = 1e-6
A_TILES = 12
TOK_COLS = 3360
TOK_BLOCK = 420
TOK_BLOCKS = TOK_COLS // TOK_BLOCK


@contextmanager
def signals(nc):
    held = []

    def signal(name):
        held.append(nc.alloc_semaphore(name))
        return held[-1]
    yield signal
    nc.clear_and_free_semaphores(held)
    nc.all_engine_barrier()


def early(count, least):
    return isinstance(count, int) and count < least


def walk(engine, steps, peeled, body):
    for c in range(peeled):
        body(c, c % 2, c // 2)
    with engine.Fori(peeled // 2, steps // 2) as i:
        for b in range(2):
            body(2 * i + b, b, i)


def phase_norm(nc, io, nT, ident):
    with ExitStack() as ctx:
        sb = lambda n, s, d=F32: ctx.enter_context(nc.sbuf_tensor(n, s, d))
        ps = lambda n, s: ctx.enter_context(nc.psum_tensor(n, s, F32))
        sem = ctx.enter_context(signals(nc))

        xall = sb("xall", [P, NT, D])
        gain = sb("gain", [P, D])
        xn = sb("xn", [P, 2, D])
        sq = sb("sq", [P, D])
        ss = sb("ss", [P, 3 * NT])

        px = ps("px", [P, 4, 512])

        x_in = sem("p1_x_in")
        x_hi = sem("p1_x_hi")
        const_in = sem("p1_const_in")
        sumsq = sem("p1_sumsq")
        mean_done = sem("p1_mean")
        inv_done = sem("p1_inv")
        rstd_done = sem("p1_rstd")
        xn_done = sem("p1_xn")
        xt_done = sem("p1_xt")
        xt_act = sem("p1_xt_act")
        xt_dve = sem("p1_xt_dve")

        with nc.Block() as block:
            @block.sync
            def _(sp):
                sp.dma_start(ident[:], io["ident"]).then_inc(const_in, 16)
                sp.dma_start(gain[:], io["norm_mix"].partition_broadcast(P)).then_inc(const_in, 16)
                for t in range(NT):
                    src = io["x"][t * P:(t + 1) * P]
                    sp.dma_start(xall[:, t, :], src).then_inc(x_in if t < 5 else x_hi, 16)

            @block.scalar
            def _(act):
                act.wait_ge(x_in, 16 * 5)
                for t in range(NT):
                    if t == 5:
                        act.wait_ge(x_hi, 16 * 5)
                    if t:
                        act.wait_ge(sumsq, t)
                    act.activation(sq[:], xall[:, t, :], ACT.Square, accum_out=ss[:, t:t + 1]).then_inc(sumsq, 1)
                act.wait_ge(inv_done, 1)
                act.activation(ss[:, 2 * NT:], ss[:, NT:2 * NT], ACT.Sqrt).then_inc(rstd_done, 1)
                with act.Fori(0, NT) as t:
                    act.wait_ge(xt_done, 2 * t + 2)
                    act.copy(nT[:, 4:8, bass.ds(t * P, P)], px[:, 1, :].rearrange("p (k t) -> p k t", k=4)).then_inc(xt_act, 1)

            @block.vector
            def _(dve):
                dve.wait_ge(sumsq, NT)
                dve.tensor_scalar(ss[:, NT:2 * NT], ss[:, 0:NT], 1.0 / D, EPS, ALU.mult, ALU.add).then_inc(mean_done, 1)
                dve.wait_ge(mean_done, 1)
                dve.reciprocal(ss[:, NT:2 * NT], ss[:, NT:2 * NT]).then_inc(inv_done, 1)
                dve.wait_ge(rstd_done, 1)
                dve.wait_ge(const_in, 32)
                dve.sem_inc(xt_act, 0) if False else None
                def normalise(t, b):
                    dve.scalar_tensor_tensor(out=xn[:, b, :], in0=xall[:, t, :] if isinstance(t, int) else xall[:, bass.ds(t, 1), :].rearrange("p a d -> p (a d)"),
                                             scalar=ss[:, 2 * NT + t:2 * NT + t + 1] if isinstance(t, int) else ss[:, bass.ds(t + 2 * NT, 1)],
                                             in1=gain[:], op0=ALU.mult, op1=ALU.mult).then_inc(xn_done, 1)
                normalise(0, 0)
                normalise(1, 1)
                def evacuate(t):
                    dve.wait_ge(xt_done, 2 * t + 1)
                    dve.tensor_copy(nT[:, 0:4, bass.ds(t * P, P)], px[:, 0, :].rearrange("p (k t) -> p k t", k=4)).then_inc(xt_dve, 1)
                with dve.Fori(0, NT // 2 - 1) as i:
                    for b in range(2):
                        evacuate(2 * i + b)
                        dve.wait_ge(xt_done, 2 * (2 * i + b) + 2)
                        normalise(2 * i + b + 2, b)
                for t in (NT - 2, NT - 1):
                    evacuate(t)

            @block.tensor
            def _(pe):
                pe.wait_ge(const_in, 32)
                def transposes(t, b, free):
                    pe.wait_ge(xn_done, t + 1)
                    for h, evacuated in ((0, xt_dve), (1, xt_act)):
                        if free:
                            pe.wait_ge(evacuated, t)
                        for k in range(4):
                            mm = pe.transpose(px[:, h, k * P:(k + 1) * P], xn[:, b, (4 * h + k) * P:(4 * h + k + 1) * P], ident[:])
                        mm.then_inc(xt_done, 1)
                transposes(0, 0, False)
                transposes(1, 1, True)
                with pe.Fori(1, NT // 2) as i:
                    for b in range(2):
                        transposes(2 * i + b, b, True)


CH_TILES = 24
GAP = T + 2
PAD = 64
QK_COLS = PAD + TS + PAD + TP + PAD
GROUPS = (1, 4, 16)


def phase_channels(nc, io, dr, nT, ident):
    with ExitStack() as ctx:
        sb = lambda n, s, d=F32: ctx.enter_context(nc.sbuf_tensor(n, s, d))
        ps = lambda n, s: ctx.enter_context(nc.psum_tensor(n, s, F32))
        sem = ctx.enter_context(signals(nc))

        wbuf = sb("ch_w", [P, 2, KT, P])
        taps = sb("ch_taps", [P, A_TILES, CONV])
        power = sb("ch_power", [P, A_TILES])
        headsum = sb("ch_headsum", [P, P])
        raw = sb("ch_raw", [P, 2, RAW])
        conv = sb("ch_conv", [P, GAP])
        act_out = sb("ch_act", [P, 2, GAP])
        sq = sb("ch_sq", [P, GAP])
        rn = sb("ch_rn", [P, GAP])
        kn = sb("ch_kn", [P, 2, GAP])
        tok = sb("ch_tok", [P, 2, NT, P])
        perm = sb("ch_perm", [P, 2, QK_COLS])
        eps = sb("ch_eps", [P, 1])

        wide = ps("ch_wide", [P, 2, 2, 512])
        tail = ps("ch_tail", [P, 512])
        aux = ps("ch_aux", [P, 3, 512])

        w_ready = [sem(f"ch_w_ready{b}") for b in range(2)]
        const_ready = sem("ch_const_ready")
        pads_ready = sem("ch_pads_ready")
        proj_done = sem("ch_proj_done")
        raw_done = sem("ch_raw_done")
        conv_step = sem("ch_conv_step")
        silu_done = sem("ch_silu_done")
        sq_done = sem("ch_sq_done")
        ss_done = sem("ch_ss_done")
        ln_done = sem("ch_ln_done")
        rn_done = sem("ch_rn_done")
        kn_done = sem("ch_kn_done")
        kn_out = [sem(f"ch_kn_out{b}") for b in range(2)]
        tr_done = sem("ch_tr_done")
        tok_done = sem("ch_tok_done")
        tok_out = [sem(f"ch_tok_out{b}") for b in range(2)]
        perm_out = [sem(f"ch_perm_out{b}") for b in range(2)]

        def region(b, j):
            return wide[:, b, j, :] if j < 2 else tail[:, 0:CHUNKS[2][1]]

        with nc.Block() as block:
            @block.sync
            def _(sp):
                def load(c, b):
                    if not early(c, 2):
                        sp.wait_ge(proj_done, 3 * c - 3)
                    sp.dma_start(wbuf[:, b], io["w_ch"][bass.ds(c, 1)].rearrange("a p k c -> (a p) k c")).then_inc(w_ready[b], 16)
                load(0, 0)
                sp.dma_start(taps[:], io["conv_w"]).then_inc(const_ready, 16)
                sp.dma_start(power[:], io["norm_power"]).then_inc(const_ready, 16)
                sp.dma_start(headsum[:], io["headsum"]).then_inc(const_ready, 16)
                load(1, 1)
                with sp.Fori(1, CH_TILES // 2) as i:
                    for b in range(2):
                        load(2 * i + b, b)

            @block.gpsimd
            def _(pool):
                pool.memset(raw[:], 0.0).then_inc(pads_ready, 1)
                pool.memset(rn[:], 0.0).then_inc(pads_ready, 1)
                pool.memset(eps[:], EPS).then_inc(pads_ready, 1)
                pool.memset(perm[:], 0.0).then_inc(pads_ready, 1)

                def store(c, b, i):
                    pool.wait_ge(kn_done, c + 1)
                    pool.dma_start(dr["qkv_ch"][bass.ds(c * P, P), :], kn[:, b]).then_inc(kn_out[b], 16)
                    pool.wait_ge(tok_done, 3 * c + 3)
                    pool.dma_start(dr["qkv_tok"][:, bass.ds(c * P, P)].rearrange("(t p) c -> p t c", p=P), tok[:, b]).then_inc(tok_out[b], 16)
                walk(pool, A_TILES, 0, store)

                def store_permuted(c, b):
                    pool.wait_ge(raw_done, 3 * c + 3)
                    pool.dma_start(dr["qk_att"][bass.ds((c - A_TILES) * P, P), :], perm[:, b]).then_inc(perm_out[b], 16)
                with pool.Fori(A_TILES // 2, CH_TILES // 2) as i:
                    for b in range(2):
                        store_permuted(2 * i + b, b)
                for b in range(2):
                    pool.wait_ge(kn_out[b], 16 * A_TILES // 2)
                    pool.wait_ge(tok_out[b], 16 * A_TILES // 2)
                    pool.wait_ge(perm_out[b], 16 * (CH_TILES - A_TILES) // 2)

            @block.tensor
            def _(pe):
                def project(c, b, i, j):
                    if j == 0:
                        pe.wait_ge(w_ready[b], 16 * (i + 1))
                    if j < 2 and not early(c, 2):
                        pe.wait_ge(raw_done, 3 * (c - 2) + j + 1)
                    if j == 2 and not early(c, 1):
                        pe.wait_ge(raw_done, 3 * c)
                    at, n = CHUNKS[j]
                    for k in range(KT):
                        mm = pe.matmul(region(b, j)[:, 0:n], wbuf[:, b, k, :], nT[:, k, at:at + n], start=(k == 0), stop=(k == KT - 1))
                    mm.then_inc(proj_done, 1)

                def to_tokens(c, b):
                    pe.wait_ge(kn_done, c + 1)
                    for t in range(NT):
                        at = t * P + (2 if t >= TS // P else 0)
                        mm = pe.transpose(aux[:, t // 4, (t % 4) * P:(t % 4 + 1) * P], kn[:, b, at:at + P], ident[:])
                        if t in (3, 7, NT - 1):
                            mm.then_inc(tr_done, 1)

                def head_sums(c, b):
                    pe.wait_ge(sq_done, c + 1)
                    if not early(c, 1):
                        pe.wait_ge(tok_done, 3 * c)
                    for j, (at, n) in enumerate(CHUNKS):
                        at += 2 if j == 2 else 0
                        mm = pe.matmul(aux[:, j, 0:n], headsum[:], sq[:, at:at + n], start=True, stop=True)
                    mm.then_inc(ss_done, 1)

                def tile(c, b, i, gemm=True):
                    if gemm:
                        project(c, b, i, 0)
                    if not early(c, 2):
                        to_tokens(c - 2, b)
                    if gemm:
                        project(c, b, i, 1)
                    if not early(c, 1) and not (isinstance(c, int) and c > A_TILES):
                        head_sums(c - 1, 1 - b)
                    if gemm:
                        project(c, b, i, 2)
                pe.wait_ge(const_ready, 48)
                walk(pe, A_TILES, 2, tile)
                tile(A_TILES, 0, A_TILES // 2)
                tile(A_TILES + 1, 1, A_TILES // 2)
                with pe.Fori(A_TILES // 2 + 1, CH_TILES // 2) as i:
                    for b in range(2):
                        for j in range(3):
                            project(2 * i + b, b, i, j)

            @block.scalar
            def _(act):
                act.wait_ge(pads_ready, 4)
                act.wait_ge(const_ready, 48)

                def evacuate(c, b, j):
                    act.wait_ge(proj_done, 3 * c + j + 1)
                    if j == 0 and not early(c, 2):
                        act.wait_ge(conv_step, CONV * (c - 1))
                    at, n = CHUNKS[j]
                    at += 2 + (2 if j == 2 else 0)
                    act.copy(raw[:, b, at:at + n], region(b, j)[:, 0:n]).then_inc(raw_done, 1)

                def tokens_out(c, b, i):
                    if not early(c, 2):
                        act.wait_ge(tok_out[b], 16 * i)
                    for j, (lo, hi) in enumerate(((0, 4), (4, 8), (8, NT))):
                        act.wait_ge(tr_done, 3 * c + j + 1)
                        act.copy(tok[:, b, lo:hi, :], aux[:, j, 0:(hi - lo) * P].rearrange("p (t c) -> p t c", c=P)).then_inc(tok_done, 1)

                def inverse_norm(c):
                    act.wait_ge(ss_done, c + 1)
                    if not early(c, 1):
                        act.wait_ge(kn_done, c)
                    act.activation(rn[:, 0:TS], aux[:, 0:2, :], ACT.Ln, bias=eps[:]).then_inc(ln_done, 1)
                    act.activation(rn[:, TS + 2:], aux[:, 2, 0:TP], ACT.Ln, bias=eps[:]).then_inc(ln_done, 1)
                    act.wait_ge(ln_done, 2 * c + 2)
                    act.activation(rn[:], rn[:], ACT.Exp, scale=power[:, bass.ds(c, 1)]).then_inc(rn_done, 1)

                def silu(c, b):
                    act.wait_ge(conv_step, CONV * (c + 1))
                    if not early(c, 2):
                        act.wait_ge(kn_done, c - 1)
                    act.activation(act_out[:, b], conv[:], ACT.Silu).then_inc(silu_done, 1)
                    act.wait_ge(silu_done, c + 1)
                    if not early(c, 1):
                        act.wait_ge(ss_done, c)
                    act.activation(sq[:], act_out[:, b], ACT.Square).then_inc(sq_done, 1)

                def tile(c, b, i):
                    evacuate(c, b, 0)
                    if not early(c, 2):
                        tokens_out(c - 2, b, i - 1)
                    evacuate(c, b, 1)
                    if not early(c, 1):
                        inverse_norm(c - 1)
                    evacuate(c, b, 2)
                    silu(c, b)
                walk(act, A_TILES, 4, tile)

                def permute(c, b, dilation, j):
                    act.wait_ge(proj_done, 3 * c + j + 1)
                    if j == 0 and not early(c, A_TILES + 2):
                        act.wait_ge(perm_out[b], 16 * ((c - A_TILES) // 2))
                    at, n = CHUNKS[j]
                    length = (TS if j < 2 else TP) // dilation
                    base = PAD if j < 2 else 2 * PAD + TS
                    first = at // dilation if j < 2 else 0
                    out = perm[:, b, base:base + length * dilation].rearrange("p (f t) -> p f t", f=dilation)[:, :, first:first + n // dilation]
                    act.copy(out, region(b, j)[:, 0:n].rearrange("p (t f) -> p f t", f=dilation)).then_inc(raw_done, 1)

                c = A_TILES
                for j in range(3):
                    permute(c, 0, GROUPS[0], j)
                    if j == 0:
                        tokens_out(A_TILES - 2, 0, A_TILES // 2 - 1)
                    if j == 1:
                        inverse_norm(A_TILES - 1)
                for j in range(3):
                    permute(c + 1, 1, GROUPS[0], j)
                    if j == 0:
                        tokens_out(A_TILES - 1, 1, A_TILES // 2 - 1)
                for pair in range(1, 6):
                    for b in range(2):
                        for j in range(3):
                            permute(A_TILES + 2 * pair + b, b, GROUPS[pair % 3], j)

            @block.vector
            def _(dve):
                dve.wait_ge(const_ready, 48)

                def normalise(c, b, i):
                    dve.wait_ge(rn_done, c + 1)
                    if not early(c, 2):
                        dve.wait_ge(tr_done, 3 * c - 3)
                        dve.wait_ge(kn_out[b], 16 * i)
                    dve.tensor_tensor(kn[:, b], act_out[:, b], rn[:], ALU.mult).then_inc(kn_done, 1)

                def convolve(c, b):
                    dve.wait_ge(raw_done, 3 * c + 3)
                    if not early(c, 1):
                        dve.wait_ge(silu_done, c)
                    for j in range(CONV):
                        tap = taps[:, bass.ds(c, 1), j:j + 1].rearrange("p a b -> p (a b)")
                        if j == 0:
                            dve.tensor_scalar(conv[:], raw[:, b, 0:GAP], tap, None, ALU.mult).then_inc(conv_step, 1)
                        else:
                            dve.wait_ge(conv_step, CONV * c + j)
                            dve.scalar_tensor_tensor(out=conv[:], in0=raw[:, b, j:j + GAP], scalar=tap, in1=conv[:],
                                                     op0=ALU.mult, op1=ALU.add).then_inc(conv_step, 1)

                def tile(c, b, i):
                    if not early(c, 1):
                        normalise(c - 1, 1 - b, i - (1 - b))
                    convolve(c, b)
                walk(dve, A_TILES, 4, tile)
                normalise(A_TILES - 1, 1, A_TILES // 2 - 1)


Z_AT, BETA_AT, ALPHA_AT, V_AT, GATE_AT = 0, 512, 528, 544, 1312


def phase_tokens(nc, io, dr, nT):
    with ExitStack() as ctx:
        sb = lambda n, s, d=F32: ctx.enter_context(nc.sbuf_tensor(n, s, d))
        ps = lambda n, s: ctx.enter_context(nc.psum_tensor(n, s, F32))
        sem = ctx.enter_context(signals(nc))
        BANKS = 4
        wbuf = sb("tk_w", [P, 2, KT, TOK_BLOCK])
        stage = sb("tk_stage", [P, 2, NT, TOK_BLOCK])
        acc = ps("tk_acc", [P, BANKS, 512])
        w_ready = [sem(f"tk_w_ready{b}") for b in range(2)]
        stored = [sem(f"tk_stored{b}") for b in range(2)]
        mm_done = sem("tk_mm_done")
        copied = {0: sem("tk_copied_act"), 1: sem("tk_copied_dve")}

        with nc.Block() as block:
            @block.sync
            def _(sp):
                def load(c, b, i):
                    if not early(c, 2):
                        sp.wait_ge(mm_done, NT * (c - 1))
                    sp.dma_start(wbuf[:, b], io["w_tok"][bass.ds(c, 1)].rearrange("a p k c -> (a p) k c")).then_inc(w_ready[b], 16)

                def store(c, b, i):
                    sp.wait_ge(copied[0], NT // 2 * (c + 1))
                    sp.wait_ge(copied[1], NT // 2 * (c + 1))
                    sp.dma_start(dr["proj_tok"][:, bass.ds(c * TOK_BLOCK, TOK_BLOCK)].rearrange("(t p) c -> p t c", p=P), stage[:, b]).then_inc(stored[b], 16)

                def turn(c, b, i):
                    load(c, b, i)
                    if not early(c, 1):
                        store(c - 1, 1 - b, i - (1 - b))
                walk(sp, TOK_BLOCKS, 2, turn)
                store(TOK_BLOCKS - 1, 1, TOK_BLOCKS // 2 - 1)
                for b in range(2):
                    sp.wait_ge(stored[b], 16 * TOK_BLOCKS // 2)

            @block.tensor
            def _(pe):
                def multiply(c, b, i):
                    pe.wait_ge(w_ready[b], 16 * (i + 1))
                    for t in range(NT):
                        if not (early(c, 1) and t < BANKS):
                            pe.wait_ge(copied[t % 2], NT // 2 * c + t // 2 - 1)
                        bank = (NT * b + t) % BANKS
                        for k in range(KT):
                            mm = pe.matmul(acc[:, bank, 0:TOK_BLOCK], nT[:, k, t * P:(t + 1) * P], wbuf[:, b, k, :], start=(k == 0), stop=(k == KT - 1))
                        mm.then_inc(mm_done, 1)
                walk(pe, TOK_BLOCKS, 2, multiply)

            def copies(engine, copy, parity):
                def block_out(c, b, i):
                    if not early(c, 2):
                        engine.wait_ge(stored[b], 16 * i)
                    for t in range(parity, NT, 2):
                        engine.wait_ge(mm_done, NT * c + t + 1)
                        copy(stage[:, b, t, :], acc[:, (NT * b + t) % BANKS, 0:TOK_BLOCK]).then_inc(copied[parity], 1)
                walk(engine, TOK_BLOCKS, 2, block_out)

            @block.scalar
            def _(act):
                copies(act, act.copy, 0)

            @block.vector
            def _(dve):
                copies(dve, dve.tensor_copy, 1)


HEADS, HD = 8, 64
COLS = 5 * HEADS


def phase_decay(nc, io, dr, ident):
    with ExitStack() as ctx:
        sb = lambda n, s, d=F32: ctx.enter_context(nc.sbuf_tensor(n, s, d))
        ps = lambda n, s: ctx.enter_context(nc.psum_tensor(n, s, F32))
        sem = ctx.enter_context(signals(nc))
        ba = sb("dc_ba", [P, NT, 4, HEADS])
        bias = sb("dc_bias", [P, 2, HEADS])
        rate = sb("dc_rate", [P, 2, HEADS])
        tri = sb("dc_tri", [P, 3, P])
        beta = sb("dc_beta", [P, NT, 2, HEADS])
        shifted = sb("dc_shifted", [P, NT, 2, HEADS])
        tmp = sb("dc_tmp", [P, NT, 2, HEADS])
        g = sb("dc_g", [P, NT, 2, HEADS])
        cols = sb("dc_cols", [P, NT, 2, 5, HEADS])
        packed = sb("dc_packed", [P, NT, 32])
        rows = sb("dc_rows", [32, NT, P])
        sums = ps("dc_sums", [P, 4, NT * HEADS])
        turned = ps("dc_turned", [P, 3, 512])
        loaded = sem("dc_loaded")
        a_step = sem("dc_act_step")
        v_step = sem("dc_dve_step")
        p_step = sem("dc_pe_step")
        out = sem("dc_out")
        bc = lambda a: a.rearrange("p d h -> p (d h)").unsqueeze(1).to_broadcast([P, NT, 2 * HEADS])
        flat = lambda a: a.rearrange("p t d h -> p t (d h)")

        with nc.Block() as block:
            @block.sync
            def _(sp):
                sp.dma_start(ba[:].rearrange("p t k h -> p t (k h)"), dr["proj_tok"][:, BETA_AT:BETA_AT + 32].rearrange("(t p) c -> p t c", p=P)).then_inc(loaded, 16)
                sp.dma_start(bias[:].rearrange("p d h -> p (d h)"), io["dt_bias"].partition_broadcast(P)).then_inc(loaded, 16)
                sp.dma_start(rate[:].rearrange("p d h -> p (d h)"), io["a_log"].partition_broadcast(P)).then_inc(loaded, 16)
                sp.dma_start(tri[:], io["tri"]).then_inc(loaded, 16)
                sp.wait_ge(a_step, 9)
                sp.dma_start(dr["cols"].rearrange("(t p) c -> p t c", p=P), cols[:].rearrange("p t d k h -> p t (d k h)")).then_inc(out, 16)
                sp.wait_ge(v_step, 15)
                sp.dma_start(dr["rows"], rows[:].rearrange("r t p -> r (t p)")).then_inc(out, 16)
                sp.wait_ge(out, 32)

            @block.scalar
            def _(act):
                act.wait_ge(loaded, 64)
                act.activation(tmp[:], ba[:, :, 0:2, :], ACT.Exp, scale=-1.0).then_inc(a_step, 1)
                act.activation(rate[:], rate[:], ACT.Exp).then_inc(a_step, 1)
                act.wait_ge(v_step, 3)
                act.activation(tmp[:], shifted[:], ACT.Abs).then_inc(a_step, 1)
                act.wait_ge(a_step, 3)
                act.activation(tmp[:], tmp[:], ACT.Exp, scale=-1.0).then_inc(a_step, 1)
                act.wait_ge(a_step, 4)
                act.activation(tmp[:], tmp[:], ACT.Ln, bias=1.0).then_inc(a_step, 1)
                act.wait_ge(v_step, 10)
                act.activation(cols[:, :, :, 2, :], cols[:, :, :, 2, :], ACT.Exp).then_inc(a_step, 1)
                act.activation(cols[:, :, :, 1, :], cols[:, :, :, 4, :], ACT.Exp).then_inc(a_step, 1)
                for d in range(2):
                    act.activation(cols[:, :, d, 3, :], sums[:, 2 + d, :].rearrange("p (t h) -> p t h", h=HEADS), ACT.Exp).then_inc(a_step, 1)

            @block.tensor
            def _(pe):
                pe.wait_ge(loaded, 64)
                pe.wait_ge(v_step, 5)
                for d in range(2):
                    gd = g[:, :, d, :]
                    pe.matmul(sums[:, d, :].rearrange("p (t h) -> p t h", h=HEADS), tri[:, d, :], gd, start=True, stop=True)
                    mm = pe.matmul(sums[:, 2 + d, :].rearrange("p (t h) -> p t h", h=HEADS), tri[:, 2, :], gd, start=True, stop=True)
                mm.then_inc(p_step, 1)
                pe.wait_ge(v_step, 12)
                for t in range(NT):
                    mm = pe.transpose(turned[0:32, t // 4, (t % 4) * P:(t % 4 + 1) * P], packed[:, t, :], ident[:])
                mm.then_inc(p_step, 1)

            @block.vector
            def _(dve):
                def step(ins):
                    ins.then_inc(v_step, 1)
                dve.wait_ge(loaded, 64)
                dve.wait_ge(a_step, 1)
                step(dve.tensor_scalar(beta[:], tmp[:], 1.0, None, ALU.add))
                dve.wait_ge(v_step, 1)
                step(dve.reciprocal(beta[:], beta[:]))
                step(dve.tensor_tensor(flat(shifted[:]), flat(ba[:, :, 2:4, :]), bc(bias[:]), ALU.add))
                dve.wait_ge(a_step, 5)
                dve.wait_ge(v_step, 3)
                step(dve.scalar_tensor_tensor(out=tmp[:], in0=shifted[:], scalar=0.0, in1=tmp[:], op0=ALU.max, op1=ALU.add))
                dve.wait_ge(v_step, 4)
                step(dve.scalar_tensor_tensor(out=flat(g[:]), in0=flat(tmp[:]), scalar=-1.0, in1=bc(rate[:]),
                                              op0=ALU.mult, op1=ALU.mult))
                dve.wait_ge(p_step, 1)
                step(dve.tensor_copy(cols[:, :, :, 0, :], beta[:]))
                for d in range(2):
                    step(dve.tensor_copy(cols[:, :, d, 4, :], sums[:, d, :].rearrange("p (t h) -> p t h", h=HEADS)))
                dve.wait_ge(v_step, 8)
                for d in range(2):
                    step(dve.tensor_tensor(cols[:, :, d, 2, :], sums[:, 2 + d, :].rearrange("p (t h) -> p t h", h=HEADS), cols[:, :, d, 4, :], ALU.subtract))
                for k in range(2):
                    step(dve.tensor_copy(packed[:].rearrange("p t (d k h) -> p t d k h", d=2, k=2)[:, :, :, k, :], cols[:, :, :, 4 * k, :]))
                dve.wait_ge(p_step, 2)
                for j, (lo, hi) in enumerate(((0, 4), (4, 8), (8, NT))):
                    step(dve.tensor_copy(rows[:, lo:hi, :], turned[0:32, j, 0:(hi - lo) * P].rearrange("r (t p) -> r t p", p=P)))


GH = 4
WIN = 2 * P
OUT_W = GH * HD + 2 * GH
V_ROWS = QK_COLS
UNIT_HEADS = [2 * (s % 2) + s // 2 for s in range(GH)]


def back(t, b, i, g, n):
    g -= n
    while g < 0:
        g, t, b, i = g + 3, t - 1, 1 - b, i - (1 - b)
    return t, b, i, g


def phase_attention(nc, io, dr, ident):
    with ExitStack() as ctx:
        sb = lambda n, s, d=F32: ctx.enter_context(nc.sbuf_tensor(n, s, d))
        ps = lambda n, s: ctx.enter_context(nc.psum_tensor(n, s, F32))
        sem = ctx.enter_context(signals(nc))
        zero = sb("at_zero", [PAD, 3, GH * HD])
        q = sb("at_q", [P, 2, 3, 2, P])
        k = sb("at_k", [P, 2, 3, 2, WIN])
        v = sb("at_v", [P, 2, 2, 3, GH * HD])
        bias = sb("at_bias", [P, 2, 3, GH * WIN])
        s = sb("at_s", [P, 2, GH, WIN])
        p = sb("at_p", [P, 2, GH, WIN])
        pt = sb("at_pt", [P, 2, 2, GH, P])
        negmax = sb("at_negmax", [P, 2, GH])
        stage = sb("at_stage", [P, 2, 3, OUT_W])
        scores = ps("at_scores", [P, 2, 2, 2, WIN])
        turned = ps("at_turned", [P, 2, GH, P])
        values = ps("at_values", [P, 2, 512])
        zeroed = sem("at_zeroed")
        v_built = sem("at_v_built")
        loaded = [sem(f"at_loaded{b}") for b in range(2)]
        stored = [sem(f"at_stored{b}") for b in range(2)]
        scored = sem("at_scored")
        biased = sem("at_biased")
        max_done = sem("at_max_done")
        neg_done = sem("at_neg_done")
        exp_done = sem("at_exp_done")
        turned_done = sem("at_turned_done")
        pt_act = sem("at_pt_act")
        pt_dve = sem("at_pt_dve")
        weighed = sem("at_weighed")
        row_done = sem("at_row_done")

        with nc.Block() as block:
            @block.sync
            def _(sp):
                sp.wait_ge(zeroed, 1)
                for r in (0, PAD + TS, 2 * PAD + TS + TP):
                    sp.dma_start(dr["v_att"][:, r:r + PAD, :].rearrange("g p c -> p g c"), zero[:]).then_inc(v_built, 16)
                for g, f in enumerate(GROUPS):
                    for base, at, n in ((PAD, 0, TS), (2 * PAD + TS, TS, TP)):
                        dst = dr["v_att"][g, base:base + n, :].rearrange("(f t) c -> f t c", f=f)
                        src = dr["proj_tok"][at:at + n, V_AT + g * GH * HD:V_AT + (g + 1) * GH * HD].rearrange("(t f) c -> f t c", f=f)
                        sp.dma_start(dst, src).then_inc(v_built, 16)
                sp.wait_ge(v_built, 16 * 9)
                rows = dr["qk_att"].rearrange("(s g p) c -> p s g c", s=2, p=P)
                vrows = dr["v_att"].rearrange("g r c -> r g c")

                def load(t, b, i):
                    if not early(t, 2):
                        sp.wait_ge(weighed, 3 * (t - 1))
                    q0 = P * t + PAD + (PAD if isinstance(t, int) and t >= TS // P else 0)
                    sp.dma_start(q[:, b].rearrange("p g j c -> p (g j) c"), rows[:, 0, :, bass.ds(q0, P)]).then_inc(loaded[b], 16)
                    sp.dma_start(k[:, b].rearrange("p g j c -> p (g j) c"), rows[:, 1, :, bass.ds(q0 - PAD, WIN)]).then_inc(loaded[b], 16)
                    for h in range(2):
                        sp.dma_start(v[:, b, h], vrows[bass.ds(q0 - PAD + h * P, P)]).then_inc(loaded[b], 16)
                    sp.dma_start(bias[:, b].rearrange("p g c -> p (g c)"), io["att_bias"][bass.ds(t, 1)].rearrange("a p c -> (a p) c")).then_inc(loaded[b], 16)
                walk(sp, TS // P, 2, load)
                for t in (TS // P, TS // P + 1):
                    load(t, t % 2, t // 2)

            @block.gpsimd
            def _(pool):
                pool.memset(zero[:], 0.0).then_inc(zeroed, 1)

                def store(t, b, i):
                    pool.wait_ge(row_done, 3 * t + 3)
                    prompt = isinstance(t, int) and t >= TS // P
                    first, n = (TS, TP) if prompt else (0, TS)
                    tile = t - first // P
                    parts = 0
                    for g, f in enumerate(GROUPS):
                        length = n // f
                        rows = dr["att_out"][first:first + n, g * OUT_W:(g + 1) * OUT_W].rearrange("(t f) c -> f t c", f=f)
                        if length >= P:
                            per = length // P
                            phase = tile if per == 1 else (0 if f == 1 else i)
                            at = (t * P - first) if f == 1 else b * P
                            pool.dma_start(rows[bass.ds(phase, 1), bass.ds(at, P), :].rearrange("f t c -> (f t) c"), stage[:, b, g, :]).then_inc(stored[b], 16)
                            parts += 1
                        else:
                            for x in range(P // length):
                                pool.dma_start(rows[bass.ds(tile * (P // length) + x, 1)].rearrange("f t c -> (f t) c"),
                                               stage[x * length:(x + 1) * length, b, g, :]).then_inc(stored[b], 16)
                                parts += 1
                    return parts
                walk(pool, TS // P, 0, store)
                parts = [store(t, t % 2, t // 2) for t in (TS // P, TS // P + 1)]
                for b in range(2):
                    pool.wait_ge(stored[b], 16 * (4 * TS // P // 2 + parts[b]))

            @block.tensor
            def _(pe):
                def score(t, b, i, g):
                    u = 3 * t + g
                    r = (3 * b + g) % 2
                    if g == 0:
                        pe.wait_ge(loaded[b], 80 * (i + 1))
                    if not early(u, 2):
                        pe.wait_ge(biased, u - 1)
                    for slot, h in enumerate(UNIT_HEADS):
                        rows = slice(HD * (h % 2), HD * (h % 2) + HD)
                        mm = pe.matmul(scores[:, r, h % 2, h // 2, :], q[rows, b, g, h // 2, :], k[rows, b, g, h // 2, :], start=True, stop=True)
                    mm.then_inc(scored, 1)

                def turn(t, b, i, g):
                    u = 3 * t + g
                    r = (3 * b + g) % 2
                    pe.wait_ge(exp_done, u + 1)
                    if not early(u, 1):
                        pe.wait_ge(pt_act, u)
                        pe.wait_ge(pt_dve, u)
                    for half in range(2):
                        for slot in range(GH):
                            mm = pe.transpose(turned[:, half, slot, :], p[:, r, slot, half * P:(half + 1) * P], ident[:])
                    mm.then_inc(turned_done, 1)

                def weigh(t, b, i, g):
                    u = 3 * t + g
                    r = (3 * b + g) % 2
                    pe.wait_ge(pt_act, u + 1)
                    pe.wait_ge(pt_dve, u + 1)
                    if not early(u, 2):
                        pe.wait_ge(row_done, u - 1)
                    for slot, h in enumerate(UNIT_HEADS):
                        for half in range(2):
                            mm = pe.matmul(values[:, r, h * HD:(h + 1) * HD], pt[:, r, half, slot, :], v[:, b, half, g, h * HD:(h + 1) * HD],
                                           start=(half == 0), stop=(half == 1))
                    mm.then_inc(weighed, 1)

                def tile(t, b, i):
                    for g in range(3):
                        score(t, b, i, g)
                        if not early(3 * t + g, 1):
                            turn(*back(t, b, i, g, 1))
                        if not early(3 * t + g, 2):
                            weigh(*back(t, b, i, g, 2))
                walk(pe, NT, 2, tile)
                last = (NT, 0, NT // 2, 0)
                turn(*back(*last, 1))
                weigh(*back(*last, 2))
                weigh(*back(*last, 1))

            @block.scalar
            def _(act):
                def exponentials(t, b, i, g):
                    u = 3 * t + g
                    r = (3 * b + g) % 2
                    act.wait_ge(neg_done, u + 1)
                    if not early(u, 2):
                        act.wait_ge(turned_done, u - 1)
                    for slot, h in enumerate(UNIT_HEADS):
                        e = act.activation(p[:, r, slot, :], s[:, r, slot, :], ACT.Exp, bias=negmax[:, r, h:h + 1],
                                           accum_out=stage[:, b, g, GH * HD + GH + h:GH * HD + GH + h + 1])
                    e.then_inc(exp_done, 1)

                def turned_out(t, b, i, g):
                    u = 3 * t + g
                    act.wait_ge(turned_done, u + 1)
                    if not early(u, 2):
                        act.wait_ge(weighed, u - 1)
                    act.copy(pt[:, (3 * b + g) % 2, 0], turned[:, 0]).then_inc(pt_act, 1)

                def tile(t, b, i):
                    for g in range(3):
                        exponentials(t, b, i, g)
                        if not early(3 * t + g, 1):
                            turned_out(*back(t, b, i, g, 1))
                walk(act, NT, 2, tile)
                turned_out(*back(NT, 0, NT // 2, 0, 1))

            @block.vector
            def _(dve):
                def maxima(t, b, i, g):
                    u = 3 * t + g
                    r = (3 * b + g) % 2
                    dve.wait_ge(scored, u + 1)
                    if g == 0:
                        dve.wait_ge(loaded[b], 80 * (i + 1))
                        if not early(t, 2):
                            dve.wait_ge(stored[b], 64 * i)
                    if not early(u, 2):
                        dve.wait_ge(exp_done, u - 1)
                    dve.scalar_tensor_tensor(out=s[:, r].rearrange("p h c -> p (h c)"), in0=scores[:, r].rearrange("p a j c -> p (a j c)"), scalar=HD ** -0.5,
                                             in1=bias[:, b, g, :], op0=ALU.mult, op1=ALU.add).then_inc(biased, 1)
                    dve.wait_ge(biased, u + 1)
                    top = stage[:, b, g, GH * HD:GH * HD + GH]
                    dve.tensor_reduce(top.rearrange("p (j r) -> p r j", r=2), s[:, r].rearrange("p (r j) c -> p r j c", r=2), AX.X, ALU.max).then_inc(max_done, 1)
                    dve.wait_ge(max_done, u + 1)
                    dve.tensor_scalar(negmax[:, r, :], top, -1.0, None, ALU.mult).then_inc(neg_done, 1)

                def turned_out(t, b, i, g):
                    u = 3 * t + g
                    dve.wait_ge(turned_done, u + 1)
                    if not early(u, 2):
                        dve.wait_ge(weighed, u - 1)
                    dve.tensor_copy(pt[:, (3 * b + g) % 2, 1], turned[:, 1]).then_inc(pt_dve, 1)

                def rows_out(t, b, i, g):
                    u = 3 * t + g
                    dve.wait_ge(weighed, u + 1)
                    dve.tensor_copy(stage[:, b, g, 0:GH * HD], values[:, (3 * b + g) % 2, 0:GH * HD]).then_inc(row_done, 1)

                def tile(t, b, i):
                    for g in range(3):
                        maxima(t, b, i, g)
                        if not early(3 * t + g, 1):
                            turned_out(*back(t, b, i, g, 1))
                        if not early(3 * t + g, 2):
                            rows_out(*back(t, b, i, g, 2))
                walk(dve, NT, 2, tile)
                last = (NT, 0, NT // 2, 0)
                turned_out(*back(*last, 1))
                rows_out(*back(*last, 2))
                rows_out(*back(*last, 1))


def attention_bias():
    slopes = (2.0 ** (-8.0 * np.arange(1, 13) / 12)).astype(np.float32)
    out = np.full((NT, P, 3, GH, WIN), -1e30, np.float32)
    qi = np.arange(P)[:, None]
    delta = np.arange(WIN)[None, :] - PAD - qi
    for t in range(NT):
        n, tile = (TS, t) if t < TS // P else (TP, t - TS // P)
        for g, f in enumerate(GROUPS):
            length = n // f
            qpos = tile * P + qi
            kpos = qpos + delta
            valid = (np.abs(delta) <= 64) & (kpos >= 0) & (kpos < n) & (kpos // length == qpos // length)
            for slot, h in enumerate(UNIT_HEADS):
                b = -slopes[g * GH + h] * (np.abs(delta) * f).astype(np.float32)
                out[t, :, g, slot, :] = np.where(valid, b, np.float32(-1e30))
    return out.reshape(NT, P, 3 * GH * WIN)


CH = 64
STEPS = T // CH
S_STEPS = TS // CH
BLK = 16
NH = HEADS


def chunk_tokens(s, d):
    if d == 0:
        return CH * s
    prompt = isinstance(s, tuple)
    raise ValueError


def places(s, prompt):
    fwd = s * CH
    bwd = (2 * S_STEPS + (STEPS - S_STEPS) - 1) * CH - s * CH if prompt else (S_STEPS - 1) * CH - s * CH
    gap = GAP - T if prompt else 0
    return (fwd, fwd + gap), (bwd, bwd + gap)


def steps(engine, body):
    for c in range(2):
        body(c, c % 2, 0, False)
    with engine.Fori(1, S_STEPS // 2) as i:
        for b in range(2):
            body(2 * i + b, b, i, False)
    for c in range(S_STEPS, S_STEPS + 2):
        body(c, c % 2, c // 2, True)
    with engine.Fori(S_STEPS // 2 + 1, STEPS // 2) as i:
        for b in range(2):
            body(2 * i + b, b, i, True)


def bc_head(a, n=HD):
    return a.unsqueeze(2).to_broadcast([P, NH, n])


def phase_scores(nc, io, dr):
    with ExitStack() as ctx:
        sb = lambda n, s, d=F32: ctx.enter_context(nc.sbuf_tensor(n, s, d))
        ps = lambda n, s: ctx.enter_context(nc.psum_tensor(n, s, F32))
        sem = ctx.enter_context(signals(nc))
        kbd = sb("sc_kbd", [P, 2, NH, P])
        qk = sb("sc_qk", [P, 2, 2 * NH, CH])
        rows = sb("sc_rows", [P, 2, 2 * NH, CH])
        cols = sb("sc_cols", [P, 2, 5, NH])
        diff = sb("sc_diff", [P, 2, NH, CH])
        decay = sb("sc_decay", [P, 2, NH, CH])
        bdecay = sb("sc_bdecay", [P, 2, NH, CH])
        growth = sb("sc_growth", [P, 2, NH, CH])
        laq = sb("sc_laq", [P, 2, 3, NH, CH])
        picked = sb("sc_picked", [P, 2, NH, CH])
        diag = sb("sc_diag", [P, 2, NH, BLK])
        causal = sb("sc_causal", [P, CH])
        own = sb("sc_own", [P, CH])
        prod = ps("sc_prod", [P, 2, NH, P])
        const_in = sem("sc_const_in")
        zeroed = sem("sc_zeroed")
        loaded = [sem(f"sc_loaded{b}") for b in range(2)]
        stored = [sem(f"sc_stored{b}") for b in range(2)]
        prod_done = sem("sc_prod_done")
        diff_done = sem("sc_diff_done")
        capped = sem("sc_capped")
        decay_done = sem("sc_decay_done")
        growth_done = sem("sc_growth_done")
        bdecay_done = sem("sc_bdecay_done")
        qt_done = sem("sc_qt_done")
        at_done = sem("sc_at_done")
        lt_done = sem("sc_lt_done")
        picked_done = sem("sc_picked_done")
        diag_done = sem("sc_diag_done")
        LOADS = 8

        with nc.Block() as block:
            @block.sync
            def _(sp):
                sp.dma_start(causal[:], io["causal"]).then_inc(const_in, 16)
                sp.dma_start(own[:], io["own_block"]).then_inc(const_in, 16)
                sp.wait_ge(zeroed, 1)

                def load(s, b, i, prompt):
                    if not early(s, 2):
                        sp.wait_ge(prod_done, s - 1)
                        sp.wait_ge(qt_done, s - 1)
                        sp.wait_ge(bdecay_done, s - 1)
                    for d, (tok, col) in enumerate(places(s, prompt)):
                        half = slice(HD * d, HD * d + HD)
                        sp.dma_start(kbd[half, b, :, HD * d:HD * d + HD], dr["qkv_ch"][NH * HD:2 * NH * HD, bass.ds(col, CH)].rearrange("(h d) t -> d h t", d=HD)).then_inc(loaded[b], 16)
                        sp.dma_start(qk[half, b], dr["qkv_ch"][0:2 * NH * HD, bass.ds(col, CH)].rearrange("(h d) t -> d h t", d=HD)).then_inc(loaded[b], 16)
                        sp.dma_start(rows[half, b], dr["rows"][16 * d:16 * d + 16, bass.ds(tok, CH)].partition_broadcast(HD)).then_inc(loaded[b], 16)
                        sp.dma_start(cols[half, b].rearrange("p k h -> p (k h)"), dr["cols"][bass.ds(tok, CH), COLS * d:COLS * d + COLS]).then_inc(loaded[b], 16)

                def store(s, b, i):
                    sp.wait_ge(lt_done, s + 1)
                    sp.dma_start(dr["laq"][bass.ds(s, 1)].rearrange("a p c -> (a p) c"), laq[:, b].rearrange("p k h c -> p (k h c)")).then_inc(stored[b], 16)
                    sp.wait_ge(diag_done, s + 1)
                    sp.dma_start(dr["diag"][:, bass.ds(s, 1)].rearrange("h s r c -> r (h s) c"), diag[:, b]).then_inc(stored[b], 16)

                def turn(s, b, i, prompt):
                    load(s, b, i, prompt)
                    if not early(s, 1):
                        store(s - 1, 1 - b, i - (1 - b))
                steps(sp, turn)
                store(STEPS - 1, 1, STEPS // 2 - 1)
                for b in range(2):
                    sp.wait_ge(stored[b], 32 * STEPS // 2)

            @block.tensor
            def _(pe):
                def products(s, b, i, prompt):
                    pe.wait_ge(loaded[b], 16 * LOADS * (i + 1))
                    if not early(s, 2):
                        pe.wait_ge(lt_done, s - 1)
                    both = qk[:, b].rearrange("p (s h) t -> p s h t", s=2)
                    for h in range(NH):
                        mm = pe.matmul(prod[:, b, h, :].rearrange("p (s t) -> p s t", s=2), kbd[:, b, h, :], both[:, :, h, :], start=True, stop=True)
                    mm.then_inc(prod_done, 1)
                steps(pe, products)

            @block.scalar
            def _(act):
                def exponentials(s, b, i, prompt):
                    act.wait_ge(capped, s + 1)
                    if not early(s, 2):
                        act.wait_ge(lt_done, s - 1)
                    act.activation(decay[:, b], diff[:, b], ACT.Exp).then_inc(decay_done, 1)
                    act.activation(growth[:, b], rows[:, b, NH:, :], ACT.Exp).then_inc(growth_done, 1)
                steps(act, exponentials)

            @block.gpsimd
            def _(pool):
                pool.memset(kbd[:], 0.0).then_inc(zeroed, 1)
                pool.wait_ge(const_in, 32)

                def scaled(s, b, i, prompt):
                    pool.wait_ge(decay_done, s + 1)
                    pool.tensor_tensor(bdecay[:, b], decay[:, b], rows[:, b, 0:NH, :], ALU.mult).then_inc(bdecay_done, 1)
                    pool.wait_ge(lt_done, s + 1)
                    if not early(s, 2):
                        pool.wait_ge(diag_done, s - 1)
                    pool.tensor_tensor(picked[:, b], laq[:, b, 0], own[:].unsqueeze(1).to_broadcast([P, NH, CH]), ALU.mult).then_inc(picked_done, 1)
                steps(pool, scaled)

            @block.vector
            def _(dve):
                dve.wait_ge(const_in, 32)
                def tile(s, b, i, prompt):
                    dve.wait_ge(loaded[b], 16 * LOADS * (i + 1))
                    if not early(s, 2):
                        dve.wait_ge(decay_done, s - 1)
                    dve.tensor_tensor(diff[:, b], rows[:, b, NH:, :], bc_head(cols[:, b, 4, :]), ALU.subtract).then_inc(diff_done, 1)
                    dve.wait_ge(diff_done, s + 1)
                    dve.scalar_tensor_tensor(out=diff[:, b], in0=diff[:, b], scalar=0.0, in1=causal[:].unsqueeze(1).to_broadcast([P, NH, CH]),
                                             op0=ALU.min, op1=ALU.add).then_inc(capped, 1)
                    if not early(s, 2):
                        dve.wait_ge(stored[b], 32 * i)
                    dve.wait_ge(growth_done, s + 1)
                    dve.scalar_tensor_tensor(out=laq[:, b, 2], in0=qk[:, b, 0:NH, :], scalar=HD ** -0.5, in1=growth[:, b],
                                             op0=ALU.mult, op1=ALU.mult).then_inc(qt_done, 1)
                    dve.wait_ge(prod_done, s + 1)
                    dve.wait_ge(decay_done, s + 1)
                    dve.scalar_tensor_tensor(out=laq[:, b, 1], in0=prod[:, b, :, 0:CH], scalar=HD ** -0.5, in1=decay[:, b],
                                             op0=ALU.mult, op1=ALU.mult).then_inc(at_done, 1)
                    dve.wait_ge(bdecay_done, s + 1)
                    dve.tensor_tensor(laq[:, b, 0], prod[:, b, :, CH:], bdecay[:, b], ALU.mult).then_inc(lt_done, 1)
                    dve.wait_ge(picked_done, s + 1)
                    dve.tensor_reduce(diag[:, b], picked[:, b].rearrange("p h (k c) -> p h c k", c=BLK), AX.X, ALU.add).then_inc(diag_done, 1)
                steps(dve, tile)


INV_P = 80
PROBLEMS = 2 * CH // BLK


def phase_invert(nc, io, dr):
    with ExitStack() as ctx:
        sb = lambda n, s, d=F32: ctx.enter_context(nc.sbuf_tensor(n, s, d))
        sem = ctx.enter_context(signals(nc))
        u = sb("iv_u", [INV_P, 2, PROBLEMS, BLK, BLK])
        x = sb("iv_x", [INV_P, 2, PROBLEMS, BLK, BLK])
        xt = sb("iv_xt", [INV_P, 2, PROBLEMS, BLK, BLK])
        term = sb("iv_term", [INV_P, 2, PROBLEMS * BLK * BLK])
        loaded = sem("iv_loaded")
        negated = sem("iv_negated")
        terms_done = sem("iv_terms_done")
        rows_done = sem("iv_rows_done")
        turned = sem("iv_turned")
        out = sem("iv_out")
        pairs = dr["diag"].rearrange("h s r c -> (h s) (r c)").rearrange("(p n) (d m) -> p d n m", n=2, d=2)
        merged = lambda a: a.rearrange("p d q r c -> p d (q r c)").rearrange("p d (n m) -> p d n m", n=2)

        with nc.Block() as block:
            @block.sync
            def _(sp):
                for d in range(2):
                    sp.dma_start(merged(u[:])[:, d], pairs[:, d]).then_inc(loaded, 16)
                sp.dma_start(x[:].rearrange("p d q r c -> p (d q) (r c)"), io["blk_ident"].partition_broadcast(INV_P)).then_inc(loaded, 16)
                sp.wait_ge(turned, 1)
                for form, src in ((0, xt), (1, x)):
                    dst = dr["blocks"][form].rearrange("h s r c -> (h s) (r c)").rearrange("(p n) (d m) -> p d n m", n=2, d=2)
                    for d in range(2):
                        sp.dma_start(dst[:, d], merged(src[:])[:, d]).then_inc(out, 16)
                sp.wait_ge(out, 64)

            @block.vector
            def _(dve):
                dve.wait_ge(loaded, 48)
                dve.tensor_scalar(u[:], u[:], -1.0, None, ALU.mult).then_inc(negated, 1)
                dve.wait_ge(negated, 1)
                for n in range(1, BLK):
                    for d in range(2):
                        row = BLK - 1 - n if d == 0 else n
                        known = slice(row + 1, BLK) if d == 0 else slice(0, row)
                        if n > 1:
                            dve.wait_ge(rows_done, 2 * (n - 2) + d + 1)
                        t = term[:, d, 0:PROBLEMS * n * n].rearrange("p (q c m) -> p q c m", q=PROBLEMS, c=n)
                        dve.tensor_tensor(t, u[:, d, :, row, known].unsqueeze(2).to_broadcast([INV_P, PROBLEMS, n, n]),
                                          x[:, d, :, known, known].rearrange("p q m c -> p q c m"), ALU.mult).then_inc(terms_done, 1)
                    for d in range(2):
                        row = BLK - 1 - n if d == 0 else n
                        known = slice(row + 1, BLK) if d == 0 else slice(0, row)
                        t = term[:, d, 0:PROBLEMS * n * n].rearrange("p (q c m) -> p q c m", q=PROBLEMS, c=n)
                        dve.wait_ge(terms_done, 2 * (n - 1) + d + 1)
                        dve.tensor_reduce(x[:, d, :, row, known], t, AX.X, ALU.add).then_inc(rows_done, 1)
                dve.wait_ge(rows_done, 2 * (BLK - 1))
                dve.tensor_copy(xt[:].rearrange("p d q r c -> p (d q) r c"), x[:].rearrange("p d q r c -> p (d q) c r")).then_inc(turned, 1)


def phase_delta(nc, io, dr):
    with ExitStack() as ctx:
        sb = lambda n, s, d=F32: ctx.enter_context(nc.sbuf_tensor(n, s, d))
        ps = lambda n, s: ctx.enter_context(nc.psum_tensor(n, s, F32))
        sem = ctx.enter_context(signals(nc))
        ltb = sb("dl_ltb", [P, 2, NH, P])
        atb = sb("dl_atb", [P, 2, NH, P])
        ka = sb("dl_ka", [P, 2, NH, 2, CH])
        qt = sb("dl_qt", [P, 2, NH, CH])
        blk = sb("dl_blk", [P, 2, 2, NH, BLK])
        kv = sb("dl_kv", [P, 2, 2, NH, HD])
        cols = sb("dl_cols", [P, 2, 5, NH])
        x = sb("dl_x", [P, 2, NH, P])
        xt = sb("dl_xt", [P, 2, NH, P])
        rhs = sb("dl_rhs", [P, 2, NH, 2, HD])
        kdb = sb("dl_kdb", [P, 2, NH, P])
        bg = sb("dl_bg", [P, 2, NH])
        ei = sb("dl_ei", [P, 2, NH, HD])
        prod = sb("dl_prod", [P, NH, P])
        ub = sb("dl_u", [P, NH, HD])
        wb = sb("dl_wb", [P, NH, P])
        mtb = sb("dl_mtb", [P, NH, P])
        qeb = sb("dl_qeb", [P, NH, P])
        state = sb("dl_state", [P, NH, HD])
        ostage = sb("dl_ostage", [P, 2, NH, HD])
        mask16 = sb("dl_mask16", [P, P])
        mask32 = sb("dl_mask32", [P, P])
        spread = sb("dl_spread", [P, P])
        eye64 = sb("dl_eye64", [P, HD])
        halves = sb("dl_halves", [P, P])
        bank = [ps(f"dl_bank{n}", [P, 4, P]) for n in range(8)]
        const_in = sem("dl_const_in")
        zeroed = sem("dl_zeroed")
        loaded = [sem(f"dl_loaded{b}") for b in range(2)]
        stored = [sem(f"dl_stored{b}") for b in range(2)]
        bg_done = sem("dl_bg_done")
        kdec_done = sem("dl_kdec_done")
        prepared = sem("dl_prepared")
        y1, a1, b1, y2, b2, uw_done, mq_done, o_done, s_done = (sem(f"dl_{n}_done") for n in ("y1", "a1", "b1", "y2", "b2", "uw", "mq", "o", "s"))
        p1_out, x1_out, xt1_out, p2_out, xt2_out, mq_out, state_out = (sem(f"dl_{n}_out") for n in ("p1", "x1", "xt1", "p2", "xt2", "mq", "state"))
        uw_out, o_out = sem("dl_uw_out"), sem("dl_o_out")
        LOADS = 12
        heads = lambda hf: range(4 * hf, 4 * hf + 4)
        four = lambda hf: slice(4 * hf, 4 * hf + 4)
        over = lambda m: m[:].unsqueeze(1).to_broadcast([P, 4, P])

        with nc.Block() as block:
            @block.sync
            def _(sp):
                for dst, name in ((mask16, "mask16"), (mask32, "mask32"), (spread, "spread"), (eye64, "eye64"), (halves, "headsum")):
                    sp.dma_start(dst[:], io[name]).then_inc(const_in, 16)
                sp.wait_ge(zeroed, 1)

                def load(s, b, i, prompt):
                    if not early(s, 2):
                        sp.wait_ge(s_done, 2 * (s - 1))
                    one = dr["laq"][bass.ds(s, 1)].rearrange("a p (k h c) -> (a p) k h c", k=3, h=NH)
                    for d, (tok, col) in enumerate(places(s, prompt)):
                        half = slice(HD * d, HD * d + HD)
                        sp.dma_start(ltb[half, b, :, half], one[half, 0]).then_inc(loaded[b], 16)
                        sp.dma_start(atb[half, b, :, half], one[half, 1]).then_inc(loaded[b], 16)
                        sp.dma_start(kv[half, b].rearrange("p k h c -> p (k h c)"), dr["qkv_tok"][bass.ds(tok, CH), NH * HD:]).then_inc(loaded[b], 16)
                        sp.dma_start(cols[half, b].rearrange("p k h -> p (k h)"), dr["cols"][bass.ds(tok, CH), COLS * d:COLS * d + COLS]).then_inc(loaded[b], 16)
                    sp.dma_start(ka[:, b, :, 1, :], one[:, 1]).then_inc(loaded[b], 16)
                    sp.dma_start(qt[:, b], one[:, 2]).then_inc(loaded[b], 16)
                    for form in range(2):
                        sp.dma_start(blk[:, b, form], dr["blocks"][form, :, bass.ds(s, 1)].rearrange("h s r c -> r (h s) c")).then_inc(loaded[b], 16)

                def store(s, b, i, prompt):
                    sp.wait_ge(o_out, 2 * s + 2)
                    for d, (tok, col) in enumerate(places(s, prompt)):
                        sp.dma_start(dr["o_delta"][d, bass.ds(tok, CH), :], ostage[HD * d:HD * d + HD, b].rearrange("p h c -> p (h c)")).then_inc(stored[b], 16)

                def turn(s, b, i, prompt):
                    load(s, b, i, prompt)
                    if not early(s, 1):
                        store(s - 1, 1 - b, i - (1 - b), prompt and not (isinstance(s, int) and s == S_STEPS))
                steps(sp, turn)
                store(STEPS - 1, 1, STEPS // 2 - 1, True)
                for b in range(2):
                    sp.wait_ge(stored[b], 32 * STEPS // 2)

            @block.gpsimd
            def _(pool):
                for t in (ltb, atb, wb, mtb):
                    pool.memset(t[:], 0.0)
                pool.memset(qeb[:], 0.0).then_inc(zeroed, 1)
                pool.wait_ge(const_in, 80)
                pool.wait_ge(zeroed, 1)

                def prepare(s, b, i, prompt):
                    pool.wait_ge(loaded[b], 16 * LOADS * (i + 1))
                    if not early(s, 2):
                        pool.wait_ge(s_done, 2 * (s - 1))
                    for form, dst in ((0, x), (1, xt)):
                        pool.tensor_tensor(dst[:, b].rearrange("p h (k c) -> p h k c", c=BLK), blk[:, b, form].unsqueeze(2).to_broadcast([P, NH, P // BLK, BLK]),
                                           spread[:].rearrange("p (k c) -> p k c", c=BLK).unsqueeze(1).to_broadcast([P, NH, P // BLK, BLK]), ALU.mult)
                    pool.tensor_tensor(bg[:, b], cols[:, b, 0, :], cols[:, b, 1, :], ALU.mult).then_inc(bg_done, 1)
                    pool.tensor_tensor(rhs[:, b, :, 0, :], kv[:, b, 1], bc_head(cols[:, b, 0, :]), ALU.mult)
                    pool.tensor_tensor(ka[:, b, :, 0, :], kv[:, b, 0], bc_head(cols[:, b, 2, :]), ALU.mult).then_inc(kdec_done, 1)
                    pool.tensor_tensor(ei[:, b], eye64[:].unsqueeze(1).to_broadcast([P, NH, HD]), bc_head(cols[:, b, 3, :]), ALU.mult)
                    pool.wait_ge(kdec_done, s + 1)
                    pool.tensor_tensor(kdb[:, b].rearrange("p h (d c) -> p h d c", d=2), ka[:, b, :, 0, :].unsqueeze(2).to_broadcast([P, NH, 2, HD]),
                                       halves[:].rearrange("p (d c) -> p d c", d=2).unsqueeze(1).to_broadcast([P, NH, 2, HD]), ALU.mult)
                    pool.wait_ge(bg_done, s + 1)
                    pool.tensor_tensor(rhs[:, b, :, 1, :], kv[:, b, 0], bc_head(bg[:, b]), ALU.mult).then_inc(prepared, 1)
                steps(pool, prepare)

            @block.tensor
            def _(pe):
                def stage(out, lhs, rhs_of, hf, done):
                    for h in heads(hf):
                        mm = pe.matmul(out[:, h - 4 * hf, :], lhs(h), rhs_of(h), start=True, stop=True)
                    mm.then_inc(done, 1)

                def step(s, b, i, prompt):
                    first = isinstance(s, int) and s in (0, S_STEPS)
                    pe.wait_ge(prepared, s + 1)
                    X, XT, PR = (lambda h: x[:, b, h, :]), (lambda h: xt[:, b, h, :]), (lambda h: prod[:, h, :])
                    LT = lambda h: ltb[:, b, h, :]
                    n = lambda hf: 2 * s + hf + 1
                    if not early(s, 1):
                        pe.wait_ge(o_out, 2 * s)
                        pe.wait_ge(state_out, 2 * s)
                    for hf in range(2):
                        stage(bank[hf], LT, X, hf, y1)
                    for hf in range(2):
                        pe.wait_ge(p1_out, n(hf))
                        stage(bank[2 + 2 * hf], XT, PR, hf, a1)
                        stage(bank[3 + 2 * hf], PR, XT, hf, b1)
                    for hf in range(2):
                        pe.wait_ge(x1_out, n(hf))
                        stage(bank[6 + hf], LT, X, hf, y2)
                    for hf in range(2):
                        pe.wait_ge(p2_out, n(hf))
                        pe.wait_ge(xt1_out, n(hf))
                        stage(bank[hf], PR, XT, hf, b2)
                    for hf in range(2):
                        pe.wait_ge(xt2_out, n(hf))
                        stage(bank[2 + hf], XT, lambda h: rhs[:, b, h].rearrange("p k c -> p (k c)"), hf, uw_done)
                    for hf in range(2):
                        pe.wait_ge(uw_out, n(hf))
                        stage(bank[4 + hf], lambda h: wb[:, h, :], lambda h: ka[:, b, h].rearrange("p k c -> p (k c)"), hf, mq_done)
                    for hf in range(2):
                        pe.wait_ge(mq_out, n(hf))
                        for out, own_part, state_part, done in ((bank[6 if hf == 0 else 0], atb, qeb, o_done), (bank[7 if hf == 0 else 1], kdb, mtb, s_done)):
                            for h in heads(hf):
                                o = out[:, h - 4 * hf, 0:HD]
                                mm = pe.matmul(o, own_part[:, b, h, :], ub[:, h, :], start=True, stop=first)
                                if not first:
                                    mm = pe.matmul(o, state_part[:, h, :], state[:, h, :], start=False, stop=True)
                            mm.then_inc(done, 1)
                steps(pe, step)

            @block.scalar
            def _(act):
                act.wait_ge(zeroed, 1)

                def step(s, b, i, prompt):
                    for hf in range(2):
                        act.wait_ge(uw_done, 2 * s + hf + 1)
                        uw = bank[2 + hf]
                        act.copy(ub[:, four(hf), :], uw[:, :, 0:HD])
                        act.copy(wb[0:HD, four(hf), 0:HD], uw[0:HD, :, HD:])
                        act.copy(wb[HD:, four(hf), HD:], uw[HD:, :, HD:]).then_inc(uw_out, 1)
                    for hf in range(2):
                        act.wait_ge(o_done, 2 * s + hf + 1)
                        if hf == 0 and not early(s, 2):
                            act.wait_ge(stored[b], 32 * i)
                        act.copy(ostage[:, b, four(hf), :], bank[6 if hf == 0 else 0][:, :, 0:HD]).then_inc(o_out, 1)
                steps(act, step)

            @block.vector
            def _(dve):
                dve.wait_ge(const_in, 80)
                dve.wait_ge(zeroed, 1)

                def step(s, b, i, prompt):
                    n = lambda hf: 2 * s + hf + 1
                    for hf in range(2):
                        dve.wait_ge(y1, n(hf))
                        dve.tensor_tensor(prod[:, four(hf), :], bank[hf][:], over(mask16), ALU.mult).then_inc(p1_out, 1)
                    for hf in range(2):
                        dve.wait_ge(a1, n(hf))
                        dve.tensor_tensor(x[:, b, four(hf), :], bank[2 + 2 * hf][:], x[:, b, four(hf), :], ALU.add).then_inc(x1_out, 1)
                        dve.wait_ge(b1, n(hf))
                        dve.tensor_tensor(xt[:, b, four(hf), :], bank[3 + 2 * hf][:], xt[:, b, four(hf), :], ALU.add).then_inc(xt1_out, 1)
                    for hf in range(2):
                        dve.wait_ge(y2, n(hf))
                        dve.tensor_tensor(prod[:, four(hf), :], bank[6 + hf][:], over(mask32), ALU.mult).then_inc(p2_out, 1)
                    for hf in range(2):
                        dve.wait_ge(b2, n(hf))
                        dve.wait_ge(xt1_out, n(hf))
                        dve.tensor_tensor(xt[:, b, four(hf), :], bank[hf][:], xt[:, b, four(hf), :], ALU.add).then_inc(xt2_out, 1)
                    for hf in range(2):
                        dve.wait_ge(mq_done, n(hf))
                        mq = bank[4 + hf]
                        for d in range(2):
                            half = slice(HD * d, HD * d + HD)
                            dve.tensor_tensor(mtb[half, four(hf), half], ei[half, b, four(hf), :], mq[half, :, 0:HD], ALU.subtract)
                            last = dve.tensor_tensor(qeb[half, four(hf), half], qt[half, b, four(hf), :], mq[half, :, HD:], ALU.subtract)
                        last.then_inc(mq_out, 1)
                    for hf in range(2):
                        dve.wait_ge(s_done, n(hf))
                        dve.tensor_copy(state[:, four(hf), :], bank[7 if hf == 0 else 1][:, :, 0:HD]).then_inc(state_out, 1)
                steps(dve, step)


def delta_constants():
    i = np.arange(P)
    d, r, c = (i[:, None] // CH), i[:, None] % CH, np.arange(CH)[None]
    causal = np.where(np.where(d == 0, c >= r, c <= r), 0.0, -1e30)
    own = r // BLK == c // BLK
    rr, cc = i[:, None], i[None]
    same = rr // CH == cc // CH

    def below(n):
        pair = same & (rr // (2 * n) == cc // (2 * n))
        fwd = pair & (rr // CH == 0) & (rr % (2 * n) >= n) & (cc % (2 * n) < n)
        bwd = pair & (rr // CH == 1) & (rr % (2 * n) < n) & (cc % (2 * n) >= n)
        return -(fwd | bwd).astype(np.float32)
    f = lambda a: np.ascontiguousarray(a, np.float32)
    return dict(causal=f(causal), own_block=f(own), mask16=below(16), mask32=below(32), spread=f(rr // BLK == cc // BLK),
                eye64=f(r == c), blk_ident=f(np.broadcast_to(np.eye(BLK).reshape(1, BLK * BLK), (2 * PROBLEMS, BLK * BLK))))


EXPERTS = 16
CAP_S, CAP_P = 2 * TS // EXPERTS, 2 * TP // EXPERTS
SLOTS = CAP_S + CAP_P


def phase_merge(nc, io, dr, ident):
    with ExitStack() as ctx:
        sb = lambda n, s, d=F32: ctx.enter_context(nc.sbuf_tensor(n, s, d))
        ps = lambda n, s: ctx.enter_context(nc.psum_tensor(n, s, F32))
        sem = ctx.enter_context(signals(nc))
        wa = sb("mg_wa", [P, 4, D])
        wb = sb("mg_wb", [P, 2, D])
        wo = sb("mg_wo", [P, KT, D])
        wr = sb("mg_wr", [P, KT, EXPERTS])
        again = sb("mg_again", [P, HD])
        fgain = sb("mg_fgain", [P, D])
        eps = sb("mg_eps", [P, 1])
        od = sb("mg_od", [P, 2, 2, NH_D := HEADS * HD])
        z = sb("mg_z", [P, 2, NH_D])
        att = sb("mg_att", [P, 2, 3, OUT_W])
        gates = sb("mg_gates", [P, 2, 2 * D])
        xin = sb("mg_x", [P, 2, D])
        on = sb("mg_on", [P, 2, NH_D])
        sq = sb("mg_sq", [P, NH_D])
        st = sb("mg_st", [P, 2, 128])
        wv = sb("mg_wv", [P, 3, GH * HD])
        ob = sb("mg_ob", [P, 2, GH * HD])
        mixin_t = sb("mg_mixin_t", [P, 6, P])
        mix = sb("mg_mix", [P, 2, D])
        gb_part = sb("mg_gb_part", [P, 512])
        mix_t = sb("mg_mix_t", [P, KT, P])
        x2 = sb("mg_x2", [P, 2, D])
        sqx = sb("mg_sqx", [P, D])
        hn = sb("mg_hn", [P, 2, D])
        hn_t = sb("mg_hn_t", [P, KT, P])
        aff = sb("mg_aff", [P, NT, EXPERTS])
        afft = sb("mg_afft", [EXPERTS, T])
        val = sb("mg_val", [EXPERTS, SLOTS])
        idx = sb("mg_idx", [EXPERTS, SLOTS], U32)
        turned = ps("mg_turned", [P, KT, P])
        y = ps("mg_y", [P, 2, 512])
        out = ps("mg_out", [P, 2, 512])
        logit = ps("mg_logit", [P, 512])

        S = {n: sem(f"mg_{n}") for n in (
            "osum", "sq", "sumsq", "ln_on", "rstd_on", "on1", "on2", "silu", "on_done", "m1", "m2", "dm", "eatt", "ed", "den", "rden", "wgt", "wv", "ob_done",
            "sig", "on_turned", "on_t", "y_done", "ga", "gb", "mixed", "mix_turned", "mix_t", "out_done", "x2", "sqx", "ln_x", "rstd_x", "hn", "hn_turned", "hn_t",
            "logits", "lmax", "lneg", "lexp", "lrec", "aff", "aff_turned", "afft", "topk", "const", "eps")}
        inputs = [sem(f"mg_inputs{b}") for b in range(2)]
        x_loaded = [sem(f"mg_x_loaded{b}") for b in range(2)]
        x2_stored = [sem(f"mg_x2_stored{b}") for b in range(2)]
        hn_stored = [sem(f"mg_hn_stored{b}") for b in range(2)]
        chosen_stored = sem("mg_chosen_stored")

        def stages(engine, body):
            for c in range(4):
                body(c, c % 2, c // 2)
            with engine.Fori(2, NT // 2) as i:
                for b in range(2):
                    body(2 * i + b, b, i)
            for c in range(NT, NT + 3):
                body(c, c % 2, c // 2)

        def has(c, lag):
            return not isinstance(c, int) or 0 <= c - lag < NT

        with nc.Block() as block:
            @block.sync
            def _(sp):
                for dst, src in ((wa[:], io["w_proj_a"].rearrange("(k p) c -> p k c", p=P)), (wb[:], io["w_proj_b"].rearrange("(k p) c -> p k c", p=P)),
                                 (again[:], io["a_norm"].partition_broadcast(P)), (fgain[:], io["norm_ffn"].partition_broadcast(P)),
                                 (wr[:], io["w_router"].rearrange("(k p) c -> p k c", p=P)), (wo[:], io["w_out"].rearrange("(k p) c -> p k c", p=P))):
                    sp.dma_start(dst, src).then_inc(S["const"], 16)

                def turn(c, b, i):
                    if has(c, 0):
                        if not early(c, 2):
                            sp.wait_ge(S["mixed"], 2 * (c - 1))
                        r = bass.ds(c * P, P)
                        for d in range(2):
                            sp.dma_start(od[:, b, d], dr["o_delta"][d, r, :]).then_inc(inputs[b], 16)
                        sp.dma_start(z[:, b], dr["proj_tok"][r, Z_AT:Z_AT + NH_D]).then_inc(inputs[b], 16)
                        sp.dma_start(att[:, b].rearrange("p g c -> p (g c)"), dr["att_out"][r, :]).then_inc(inputs[b], 16)
                        sp.dma_start(gates[:, b], dr["proj_tok"][r, GATE_AT:GATE_AT + 2 * D]).then_inc(inputs[b], 16)
                    if has(c, 1):
                        if not early(c, 3):
                            sp.wait_ge(S["x2"], 2 * (c - 2))
                        sp.dma_start(xin[:, 1 - b], io["x"][bass.ds((c - 1) * P, P), :]).then_inc(x_loaded[1 - b], 16)
                    if has(c, 2):
                        r = bass.ds((c - 2) * P, P)
                        sp.wait_ge(S["x2"], 2 * (c - 1))
                        sp.dma_start(dr["x2"][r, :], x2[:, b]).then_inc(x2_stored[b], 16)
                        sp.wait_ge(S["hn"], c - 1)
                        sp.dma_start(dr["hn"][r, :], hn[:, b]).then_inc(hn_stored[b], 16)
                stages(sp, turn)
                sp.wait_ge(S["topk"], 1)
                sp.dma_start(dr["idx"], idx[:]).then_inc(chosen_stored, 16)
                sp.dma_start(dr["gate"], val[:]).then_inc(chosen_stored, 16)
                sp.wait_ge(chosen_stored, 32)
                for b in range(2):
                    sp.wait_ge(x2_stored[b], 16 * NT // 2)
                    sp.wait_ge(hn_stored[b], 16 * NT // 2)

            @block.gpsimd
            def _(pool):
                pool.memset(eps[:], EPS).then_inc(S["eps"], 1)
                pool.wait_ge(S["const"], 96)

                def prepare(c, b, i):
                    if not has(c, 0):
                        return
                    pool.wait_ge(inputs[b], 80 * (i + 1))
                    if not early(c, 2):
                        pool.wait_ge(S["on_turned"], c - 1)
                    pool.tensor_tensor(on[:, b], od[:, b, 0], od[:, b, 1], ALU.add).then_inc(S["osum"], 1)
                    pool.wait_ge(S["osum"], c + 1)
                    pool.tensor_tensor(sq[:], on[:, b], on[:, b], ALU.mult).then_inc(S["sq"], 1)
                    heads = on[:, b].rearrange("p (h c) -> p h c", h=HEADS)
                    pool.wait_ge(S["rstd_on"], c + 1)
                    pool.tensor_tensor(heads, heads, bc_head(st[:, b, 0:HEADS]), ALU.mult).then_inc(S["on1"], 1)
                    pool.wait_ge(S["on1"], c + 1)
                    pool.tensor_tensor(heads, heads, again[:].unsqueeze(1).to_broadcast([P, HEADS, HD]), ALU.mult).then_inc(S["on2"], 1)
                    pool.wait_ge(S["on2"], c + 1)
                    pool.wait_ge(S["silu"], c + 1)
                    pool.tensor_tensor(on[:, b], on[:, b], z[:, b], ALU.mult).then_inc(S["on_done"], 1)
                stages(pool, prepare)

            @block.tensor
            def _(pe):
                pe.wait_ge(S["const"], 96)

                def turn(c, b, i):
                    def half(h):
                        if h == 1 or not early(c, 2):
                            pe.wait_ge(S["ga"], 2 * (c - 1) + h)
                        for k in range(4):
                            mm = pe.matmul(y[:, 0, :], mixin_t[:, k, :], wa[:, k, h * 512:(h + 1) * 512], start=(k == 0), stop=(k == 3))
                        mm.then_inc(S["y_done"], 1)
                        if h == 1 or not early(c, 2):
                            pe.wait_ge(S["gb"], 2 * (c - 1) + h)
                        for k in range(2):
                            mm = pe.matmul(y[:, 1, :], mixin_t[:, 4 + k, :], wb[:, k, h * 512:(h + 1) * 512], start=(k == 0), stop=(k == 1))
                        mm.then_inc(S["y_done"], 1)

                    def project_out(h):
                        if not early(c, 3):
                            pe.wait_ge(S["x2"], 2 * (c - 3) + h + 1)
                        for k in range(KT):
                            mm = pe.matmul(out[:, h, :], mix_t[:, k, :], wo[:, k, h * 512:(h + 1) * 512], start=(k == 0), stop=(k == KT - 1))
                        mm.then_inc(S["out_done"], 1)

                    if has(c, 1):
                        pe.wait_ge(S["on_done"], c)
                        pe.wait_ge(S["ob_done"], c)
                        if not early(c, 4):
                            pe.wait_ge(S["hn_t"], c - 3)
                        for k in range(4):
                            pe.transpose(turned[:, k, :], on[:, 1 - b, k * P:(k + 1) * P], ident[:])
                        for k in range(2):
                            mm = pe.transpose(turned[:, 4 + k, :], ob[:, 1 - b, k * P:(k + 1) * P], ident[:])
                        mm.then_inc(S["on_turned"], 1)
                        pe.wait_ge(S["on_t"], c)
                        half(0)
                    if has(c, 2):
                        pe.wait_ge(S["mixed"], 2 * (c - 1))
                        if not has(c, 1):
                            pe.wait_ge(S["hn_t"], c - 3)
                        for k in range(KT):
                            mm = pe.transpose(turned[:, k, :], mix[:, b, k * P:(k + 1) * P], ident[:])
                        mm.then_inc(S["mix_turned"], 1)
                    if has(c, 1):
                        half(1)
                    if has(c, 2):
                        pe.wait_ge(S["mix_t"], c - 1)
                        project_out(0)
                    if has(c, 3):
                        pe.wait_ge(S["hn"], c - 2)
                        for k in range(KT):
                            mm = pe.transpose(turned[:, k, :], hn[:, 1 - b, k * P:(k + 1) * P], ident[:])
                        mm.then_inc(S["hn_turned"], 1)
                    if has(c, 2):
                        project_out(1)
                    if has(c, 3):
                        pe.wait_ge(S["hn_t"], c - 2)
                        if not early(c, 4):
                            pe.wait_ge(S["lexp"], c - 3)
                        for k in range(KT):
                            mm = pe.matmul(logit[:, 0:EXPERTS], hn_t[:, k, :], wr[:, k, :], start=(k == 0), stop=(k == KT - 1))
                        mm.then_inc(S["logits"], 1)
                stages(pe, turn)
                pe.wait_ge(S["aff"], NT)
                for t in range(NT):
                    dst = turned[0:EXPERTS, t, :] if t < KT else out[0:EXPERTS, 0, (t - KT) * P:(t - KT + 1) * P]
                    mm = pe.transpose(dst, aff[:, t, :], ident[:])
                mm.then_inc(S["aff_turned"], 1)

            @block.scalar
            def _(act):
                act.wait_ge(S["const"], 96)
                act.wait_ge(S["eps"], 1)

                def turn(c, b, i):
                    if has(c, 1):
                        act.wait_ge(S["on_turned"], c)
                        act.copy(mixin_t[:], turned[:, 0:6, :]).then_inc(S["on_t"], 1)
                    if has(c, 2):
                        act.wait_ge(S["mix_turned"], c - 1)
                        act.copy(mix_t[:], turned[:]).then_inc(S["mix_t"], 1)
                    if has(c, 0):
                        act.wait_ge(inputs[b], 80 * (i + 1))
                        act.activation(z[:, b], z[:, b], ACT.Silu).then_inc(S["silu"], 1)
                        act.activation(gates[:, b], gates[:, b], ACT.Sigmoid).then_inc(S["sig"], 1)
                        act.wait_ge(S["sumsq"], c + 1)
                        act.activation(st[:, b, 8:16], st[:, b, 8:16], ACT.Ln, bias=eps[:], scale=1.0 / HD).then_inc(S["ln_on"], 1)
                        act.wait_ge(S["ln_on"], c + 1)
                        act.activation(st[:, b, 0:8], st[:, b, 8:16], ACT.Exp, scale=-0.5).then_inc(S["rstd_on"], 1)
                        act.wait_ge(S["dm"], c + 1)
                        act.activation(st[:, b, 16:28], st[:, b, 16:28], ACT.Exp).then_inc(S["eatt"], 1)
                    if has(c, 3):
                        act.wait_ge(S["hn_turned"], c - 2)
                        act.copy(hn_t[:], turned[:]).then_inc(S["hn_t"], 1)
                    if has(c, 2):
                        act.wait_ge(S["x2"], 2 * (c - 1))
                        if not early(c, 3):
                            act.wait_ge(S["sqx"], c - 2)
                        act.activation(sqx[:], x2[:, b], ACT.Square, accum_out=st[:, b, 64:65]).then_inc(S["sqx"], 1)
                        act.wait_ge(S["sqx"], c - 1)
                        act.activation(st[:, b, 65:66], st[:, b, 64:65], ACT.Ln, bias=eps[:], scale=1.0 / D).then_inc(S["ln_x"], 1)
                        act.wait_ge(S["ln_x"], c - 1)
                        act.activation(st[:, b, 66:67], st[:, b, 65:66], ACT.Exp, scale=-0.5).then_inc(S["rstd_x"], 1)
                    if has(c, 3):
                        act.wait_ge(S["lneg"], c - 2)
                        act.activation(st[:, 1 - b, 72:88], logit[:, 0:EXPERTS], ACT.Exp, bias=st[:, 1 - b, 69:70], accum_out=st[:, 1 - b, 70:71]).then_inc(S["lexp"], 1)
                stages(act, turn)

            @block.vector
            def _(dve):
                dve.wait_ge(S["const"], 96)

                def one(name, at, ins):
                    ins.then_inc(S[name], 1)
                    dve.wait_ge(S[name], at)

                def turn(c, b, i):
                    if has(c, 1):
                        o = 1 - b
                        if not early(c, 3):
                            dve.wait_ge(S["mix_turned"], c - 2)
                        dve.wait_ge(S["sig"], c)
                        for h in range(2):
                            cols = slice(h * 512, h * 512 + 512)
                            n = 2 * (c - 1) + h + 1
                            dve.wait_ge(S["y_done"], 2 * n - 1)
                            dve.tensor_tensor(mix[:, o, cols], y[:, 0, :], gates[:, o, cols], ALU.mult).then_inc(S["ga"], 1)
                            dve.wait_ge(S["y_done"], 2 * n)
                            dve.tensor_tensor(gb_part[:], y[:, 1, :], gates[:, o, D + h * 512:D + h * 512 + 512], ALU.mult).then_inc(S["gb"], 1)
                            dve.wait_ge(S["gb"], n)
                            one("mixed", n, dve.tensor_tensor(mix[:, o, cols], mix[:, o, cols], gb_part[:], ALU.add))
                    if has(c, 0):
                        s = lambda lo, n: st[:, b, lo:lo + n]
                        dve.wait_ge(S["sq"], c + 1)
                        dve.tensor_reduce(s(8, 8), sq[:].rearrange("p (h c) -> p h c", h=HEADS), AX.X, ALU.add).then_inc(S["sumsq"], 1)
                        dve.wait_ge(inputs[b], 80 * (i + 1))
                        m = att[:, b, :, GH * HD:GH * HD + GH]
                        den = att[:, b, :, GH * HD + GH:OUT_W]
                        one("m1", c + 1, dve.tensor_tensor(s(28, 4), m[:, 0, :], m[:, 1, :], ALU.max))
                        one("m2", c + 1, dve.tensor_tensor(s(28, 4), s(28, 4), m[:, 2, :], ALU.max))
                        e = s(16, 12).rearrange("p (g h) -> p g h", g=3)
                        dve.tensor_tensor(e, m, s(28, 4).unsqueeze(1).to_broadcast([P, 3, GH]), ALU.subtract).then_inc(S["dm"], 1)
                        dve.wait_ge(S["eatt"], c + 1)
                        ed = s(32, 12).rearrange("p (g h) -> p g h", g=3)
                        one("ed", c + 1, dve.tensor_tensor(ed, e, den, ALU.mult))
                        one("den", c + 1, dve.tensor_reduce(s(44, 4), ed.rearrange("p g h -> p h g"), AX.X, ALU.add))
                        one("rden", c + 1, dve.reciprocal(s(44, 4), s(44, 4)))
                        one("wgt", c + 1, dve.tensor_tensor(ed, e, s(44, 4).unsqueeze(1).to_broadcast([P, 3, GH]), ALU.mult))
                        for g in range(3):
                            last = dve.tensor_tensor(wv[:, g].rearrange("p (h c) -> p h c", h=GH), att[:, b, g, 0:GH * HD].rearrange("p (h c) -> p h c", h=GH),
                                                     s(32 + GH * g, GH).unsqueeze(2).to_broadcast([P, GH, HD]), ALU.mult)
                        one("wv", c + 1, last)
                        if not early(c, 2):
                            dve.wait_ge(S["on_turned"], c - 1)
                        dve.tensor_reduce(ob[:, b], wv[:].rearrange("p g c -> p c g"), AX.X, ALU.add).then_inc(S["ob_done"], 1)
                        dve.wait_ge(S["ob_done"], c + 1)
                    if has(c, 2):
                        if not early(c, 4):
                            dve.wait_ge(x2_stored[b], 16 * (i - 1))
                            dve.wait_ge(hn_stored[b], 16 * (i - 1))
                        dve.wait_ge(x_loaded[b], 16 * i)
                        for h in range(2):
                            cols = slice(h * 512, h * 512 + 512)
                            dve.wait_ge(S["out_done"], 2 * (c - 2) + h + 1)
                            dve.tensor_tensor(x2[:, b, cols], out[:, h, :], xin[:, b, cols], ALU.add).then_inc(S["x2"], 1)
                        dve.wait_ge(S["rstd_x"], c - 1)
                        if not early(c, 4):
                            dve.wait_ge(S["hn_turned"], c - 3)
                        dve.scalar_tensor_tensor(out=hn[:, b], in0=x2[:, b], scalar=st[:, b, 66:67], in1=fgain[:], op0=ALU.mult, op1=ALU.mult).then_inc(S["hn"], 1)
                    if has(c, 3):
                        o = 1 - b
                        dve.wait_ge(S["logits"], c - 2)
                        one("lmax", c - 2, dve.tensor_reduce(st[:, o, 68:69], logit[:, 0:EXPERTS], AX.X, ALU.max))
                        dve.tensor_scalar(st[:, o, 69:70], st[:, o, 68:69], -1.0, None, ALU.mult).then_inc(S["lneg"], 1)
                        dve.wait_ge(S["lexp"], c - 2)
                        one("lrec", c - 2, dve.reciprocal(st[:, o, 71:72], st[:, o, 70:71]))
                        dve.tensor_scalar(aff[:, bass.ds(c - 3, 1), :].rearrange("p a e -> p (a e)"), st[:, o, 72:88], st[:, o, 71:72], None, ALU.mult).then_inc(S["aff"], 1)
                stages(dve, turn)

                dve.wait_ge(S["aff_turned"], 1)
                for n, (dst, src) in enumerate(((afft[:, 0:TS].rearrange("e (t p) -> e t p", p=P), turned[0:EXPERTS]), (afft[:, TS:], out[0:EXPERTS, 0, 0:TP]))):
                    one("afft", n + 1, dve.tensor_copy(dst, src))
                n = 2
                for lo, size, at, cap in ((0, TS, 0, CAP_S), (TS, TP, CAP_S, CAP_P)):
                    seg = afft[:, lo:lo + size]
                    for r in range(cap // 8):
                        cols = slice(at + 8 * r, at + 8 * r + 8)
                        n += 1
                        one("afft", n, dve.max(out=val[:, cols], in_=seg))
                        dve.max_index(out=idx[:, cols], in_max=val[:, cols], in_values=seg)
                        n += 1
                        one("afft", n, dve.match_replace(out=seg, in_to_replace=val[:, cols], in_values=seg, imm_value=-1.0))
                dve.tensor_scalar(idx[:, CAP_S:], idx[:, CAP_S:], TS, None, ALU.add).then_inc(S["topk"], 1)


DE = 1024
FT = DE // P
HALF = 512


def phase_experts(nc, io, dr, ident):
    with ExitStack() as ctx:
        sb = lambda n, s, d=F32: ctx.enter_context(nc.sbuf_tensor(n, s, d))
        ps = lambda n, s: ctx.enter_context(nc.psum_tensor(n, s, F32))
        sem = ctx.enter_context(signals(nc))
        PIECES = ("gate0", "up0", "gate1", "up1", "down0", "down1")
        w = {n: sb(f"ex_{n}", [P, KT, HALF]) for n in PIECES}
        gather_idx = [sb("ex_gidx_s", [CAP_S, 1], U32), sb("ex_gidx_p", [CAP_P, 1], U32)]
        scatter_idx = [sb("ex_sidx_s", [CAP_S, 1], U32), sb("ex_sidx_p", [CAP_P, 1], U32)]
        gain_s = sb("ex_gain_s", [CAP_S, EXPERTS])
        gain_p = sb("ex_gain_p", [CAP_P, EXPERTS])
        xs = sb("ex_xs", [CAP_S, D])
        xp = sb("ex_xp", [CAP_P, D])
        xt = sb("ex_xt", [P, KT, SLOTS])
        sg = sb("ex_sg", [P, 2, SLOTS])
        ht = sb("ex_ht", [P, FT, SLOTS])
        yt = sb("ex_yt", [P, KT, SLOTS])
        ys = sb("ex_ys", [CAP_S, D])
        yp = sb("ex_yp", [CAP_P, D])
        g_acc = ps("ex_g_acc", [P, 2, 512])
        u_acc = ps("ex_u_acc", [P, 2, 512])
        y_acc = ps("ex_y_acc", [P, 2, 512])
        turned = ps("ex_turned", [P, 2, 512])

        w_ready = {n: sem(f"ex_{n}_ready") for n in PIECES}
        gains_ready = sem("ex_gains_ready")
        gidx_ready = sem("ex_gidx_ready")
        sidx_ready = sem("ex_sidx_ready")
        gathered = sem("ex_gathered")
        turns = sem("ex_turns")
        scattered = sem("ex_scattered")
        x_turned = sem("ex_x_turned")
        xt_act, xt_dve = sem("ex_xt_act"), sem("ex_xt_dve")
        g_done, u_done = sem("ex_g_done"), sem("ex_u_done")
        silu_done, h_done = sem("ex_silu_done"), sem("ex_h_done")
        y_done = sem("ex_y_done")
        yt_act, yt_dve = sem("ex_yt_act"), sem("ex_yt_dve")
        y_turned = sem("ex_y_turned")
        ys_act, ys_dve = sem("ex_ys_act"), sem("ex_ys_dve")

        def experts(engine, body):
            body(0)
            with engine.Fori(1, EXPERTS - 1) as e:
                body(e)
            body(EXPERTS - 1)

        def last(e):
            return isinstance(e, int) and e == EXPERTS - 1

        with nc.Block() as block:
            @block.sync
            def _(sp):
                def weights(e):
                    for n, name in enumerate(PIECES):
                        if not early(e, 1):
                            done, tiles = (u_done, FT) if n < 4 else (y_done, KT)
                            sp.wait_ge(done, tiles * (e - 1) + (tiles // 2 if name[-1] == "0" else tiles))
                        kind, h = name[:-1], int(name[-1])
                        src = io[f"w_{kind}"][bass.ds(e, 1), :, h * HALF:(h + 1) * HALF].rearrange("a (k p) c -> p (a k) c", p=P)
                        sp.dma_start(w[name][:], src).then_inc(w_ready[name], 16)

                def indices(e, dst, ready):
                    for buf, (lo, hi) in zip(dst, ((0, CAP_S), (CAP_S, SLOTS))):
                        sp.dma_start(buf[:], dr["idx"][bass.ds(e, 1), lo:hi].rearrange("a n -> n a")).then_inc(ready, 16)

                indices(0, gather_idx, gidx_ready)
                weights(0)
                sp.dma_start(gain_s[:], dr["gate"][:, 0:CAP_S].rearrange("e n -> n e"), allow_slow_non_contiguous=True).then_inc(gains_ready, 16)
                sp.dma_start(gain_p[:], dr["gate"][:, CAP_S:].rearrange("e n -> n e"), allow_slow_non_contiguous=True).then_inc(gains_ready, 16)

                def turn(e):
                    if not last(e):
                        sp.wait_ge(gathered, 32 * (e + 1))
                        indices(e + 1, gather_idx, gidx_ready)
                    if not early(e, 1):
                        if not early(e, 2):
                            sp.wait_ge(scattered, 32 * (e - 1))
                        indices(e - 1, scatter_idx, sidx_ready)
                    if not last(e):
                        weights(e + 1)
                turn(0)
                turn(1)
                with sp.Fori(2, EXPERTS - 1) as e:
                    turn(e)
                turn(EXPERTS - 1)
                sp.wait_ge(scattered, 32 * (EXPERTS - 1))
                indices(EXPERTS - 1, scatter_idx, sidx_ready)

            @block.gpsimd
            def _(pool):
                def gather(e):
                    pool.wait_ge(gidx_ready, 32 * (e + 1))
                    if not early(e, 1):
                        pool.wait_ge(x_turned, 3 * e)
                    pool.sem_inc(turns, 1)
                    for buf, ix in ((xs, gather_idx[0]), (xp, gather_idx[1])):
                        pool.indirect_dma_start(out=buf[:], out_offset=None, in_=dr["hn"], in_offset=bass.IndirectOffsetOnAxis(ap=ix[:, 0:1], axis=0)).then_inc(gathered, 16)

                def scatter(e):
                    pool.wait_ge(sidx_ready, 32 * (e + 1))
                    pool.wait_ge(ys_act, 2 * (e + 1))
                    pool.wait_ge(ys_dve, 2 * (e + 1))
                    if not early(e, 1):
                        pool.wait_ge(scattered, 32 * e)
                    pool.sem_inc(turns, 1)
                    for buf, ix in ((ys, scatter_idx[0]), (yp, scatter_idx[1])):
                        pool.indirect_dma_start(out=dr["x2"], out_offset=bass.IndirectOffsetOnAxis(ap=ix[:, 0:1], axis=0), in_=buf[:], in_offset=None,
                                                compute_op=ALU.add).then_inc(scattered, 16)
                gather(0)
                gather(1)
                gather(2)
                scatter(0)
                with pool.Fori(2, EXPERTS - 1) as e:
                    gather(e + 1)
                    scatter(e - 1)
                scatter(EXPERTS - 2)
                scatter(EXPERTS - 1)
                pool.wait_ge(scattered, 32 * EXPERTS)

            @block.tensor
            def _(pe):
                def turn_in(e):
                    pe.wait_ge(gathered, 32 * (e + 1))
                    for k in range(KT):
                        bank = (turned[:, 0], turned[:, 1], y_acc[:, 1])[k // 3]
                        at = (k % 3) * SLOTS
                        pe.transpose(bank[:, at:at + CAP_S], xs[:, k * P:(k + 1) * P], ident[:])
                        mm = pe.transpose(bank[:, at + CAP_S:at + SLOTS], xp[:, k * P:(k + 1) * P], ident[0:CAP_P, 0:CAP_P])
                        if k in (2, 5, 7):
                            mm.then_inc(x_turned, 1)

                def turn_back(e, n):
                    slots = (slice(0, CAP_S), slice(CAP_S, SLOTS))[n]
                    if n:
                        pe.wait_ge(ys_act, 2 * e + 1)
                        pe.wait_ge(ys_dve, 2 * e + 1)
                    else:
                        pe.wait_ge(yt_act, 4 * (e + 1))
                        pe.wait_ge(yt_dve, 4 * (e + 1))
                    for k in range(KT):
                        mm = pe.transpose(turned[0:slots.stop - slots.start, k // 4, (k % 4) * P:(k % 4 + 1) * P], yt[:, k, slots], ident[:])
                    mm.then_inc(y_turned, 1)

                def turn(e):
                    pe.wait_ge(xt_act, 2 * (e + 1))
                    pe.wait_ge(xt_dve, e + 1)
                    for f in range(FT):
                        if f % 4 == 0:
                            pe.wait_ge(w_ready[f"gate{f // 4}"], 16 * (e + 1))
                        if f >= 2 or not early(e, 1):
                            pe.wait_ge(h_done, FT * e + f - 1)
                        for k in range(KT):
                            mm = pe.matmul(g_acc[:, f % 2, 0:SLOTS], w[f"gate{f // 4}"][:, k, (f % 4) * P:(f % 4 + 1) * P], xt[:, k, :], start=(k == 0), stop=(k == KT - 1))
                        mm.then_inc(g_done, 1)
                        if f % 4 == 0:
                            pe.wait_ge(w_ready[f"up{f // 4}"], 16 * (e + 1))
                        for k in range(KT):
                            mm = pe.matmul(u_acc[:, f % 2, 0:SLOTS], w[f"up{f // 4}"][:, k, (f % 4) * P:(f % 4 + 1) * P], xt[:, k, :], start=(k == 0), stop=(k == KT - 1))
                        mm.then_inc(u_done, 1)
                        if f == 1 and not early(e, 1):
                            turn_back(e - 1, 0)
                        if f == 4 and not early(e, 1):
                            turn_back(e - 1, 1)
                    if not last(e):
                        if not early(e, 1):
                            pe.wait_ge(ys_act, 2 * e)
                            pe.wait_ge(ys_dve, 2 * e)
                        turn_in(e + 1)
                    for d in range(KT):
                        if d % 4 == 0:
                            pe.wait_ge(w_ready[f"down{d // 4}"], 16 * (e + 1))
                        if d == 0:
                            pe.wait_ge(h_done, FT * (e + 1))
                        if d >= 2:
                            pe.wait_ge((yt_act, yt_dve)[d % 2], 4 * e + d // 2)
                        if d == 1:
                            pe.wait_ge(xt_act, 2 * (e + 2) if not last(e) else 2 * (e + 1))
                        for k in range(FT):
                            mm = pe.matmul(y_acc[:, d % 2, 0:SLOTS], w[f"down{d // 4}"][:, k, (d % 4) * P:(d % 4 + 1) * P], ht[:, k, :], start=(k == 0), stop=(k == FT - 1))
                        mm.then_inc(y_done, 1)

                turn_in(0)
                experts(pe, turn)
                turn_back(EXPERTS - 1, 0)
                turn_back(EXPERTS - 1, 1)

            @block.scalar
            def _(act):
                def x_out(e):
                    act.wait_ge(x_turned, 3 * e + 1)
                    act.copy(xt[:, 0:3, :], turned[:, 0, 0:3 * SLOTS].rearrange("p (k n) -> p k n", k=3)).then_inc(xt_act, 1)
                    act.wait_ge(x_turned, 3 * e + 3)
                    act.copy(xt[:, 6:8, :], y_acc[:, 1, 0:2 * SLOTS].rearrange("p (k n) -> p k n", k=2)).then_inc(xt_act, 1)

                def y_out(e, n):
                    act.wait_ge(gains_ready, 32)
                    act.wait_ge(y_turned, 2 * e + n + 1)
                    if n == 0 and not early(e, 1):
                        act.wait_ge(scattered, 32 * e)
                    rows, dst, gain = ((CAP_S, ys, gain_s), (CAP_P, yp, gain_p))[n]
                    act.activation(dst[:, 0:HALF], turned[0:rows, 0, :], ACT.Copy, scale=gain[:, bass.ds(e, 1)]).then_inc(ys_act, 1)

                def turn(e):
                    for f in range(FT):
                        act.wait_ge(g_done, FT * e + f + 1)
                        if f >= 2 or not early(e, 1):
                            act.wait_ge(h_done, FT * e + f - 1)
                        act.activation(sg[:, f % 2], g_acc[:, f % 2, 0:SLOTS], ACT.Silu).then_inc(silu_done, 1)
                        if f in (1, 4) and not early(e, 1):
                            y_out(e - 1, int(f == 4))
                    if not last(e):
                        x_out(e + 1)
                    for d in range(0, KT, 2):
                        act.wait_ge(y_done, KT * e + d + 1)
                        act.copy(yt[:, d, :], y_acc[:, 0, 0:SLOTS]).then_inc(yt_act, 1)
                x_out(0)
                experts(act, turn)
                y_out(EXPERTS - 1, 0)
                y_out(EXPERTS - 1, 1)

            @block.vector
            def _(dve):
                def x_out(e):
                    dve.wait_ge(x_turned, 3 * e + 2)
                    dve.tensor_copy(xt[:, 3:6, :], turned[:, 1, 0:3 * SLOTS].rearrange("p (k n) -> p k n", k=3)).then_inc(xt_dve, 1)

                def y_out(e, n):
                    dve.wait_ge(gains_ready, 32)
                    dve.wait_ge(y_turned, 2 * e + n + 1)
                    if n == 0 and not early(e, 1):
                        dve.wait_ge(scattered, 32 * e)
                    rows, dst, gain = ((CAP_S, ys, gain_s), (CAP_P, yp, gain_p))[n]
                    dve.tensor_scalar(dst[:, HALF:], turned[0:rows, 1, :], gain[:, bass.ds(e, 1)], None, ALU.mult).then_inc(ys_dve, 1)

                def turn(e):
                    for f in range(FT):
                        dve.wait_ge(silu_done, FT * e + f + 1)
                        dve.wait_ge(u_done, FT * e + f + 1)
                        dve.tensor_tensor(ht[:, f, :], u_acc[:, f % 2, 0:SLOTS], sg[:, f % 2], ALU.mult).then_inc(h_done, 1)
                        if f in (1, 4) and not early(e, 1):
                            y_out(e - 1, int(f == 4))
                    if not last(e):
                        x_out(e + 1)
                    for d in range(1, KT, 2):
                        dve.wait_ge(y_done, KT * e + d + 1)
                        dve.tensor_copy(yt[:, d, :], y_acc[:, 1, 0:SLOTS]).then_inc(yt_dve, 1)
                x_out(0)
                experts(dve, turn)
                y_out(EXPERTS - 1, 0)
                y_out(EXPERTS - 1, 1)


def phase_final(nc, io, dr, y):
    with ExitStack() as ctx:
        sb = lambda n, s, d=F32: ctx.enter_context(nc.sbuf_tensor(n, s, d))
        sem = ctx.enter_context(signals(nc))
        xall = sb("fn_x", [P, NT, D])
        sq = sb("fn_sq", [P, D])
        gain = sb("fn_gain", [P, D])
        ss = sb("fn_ss", [P, 3, NT])
        loaded = [sem("fn_loaded_a"), sem("fn_loaded_b")]
        gain_in = sem("fn_gain_in")
        sumsq, mean_done, inv_done, rstd_done, y_done, out = (sem(f"fn_{n}") for n in ("sumsq", "mean", "inv", "rstd", "y", "out"))
        H = NT // 2
        tiles = lambda a, h: a[h * H * P:(h + 1) * H * P].rearrange("(t p) c -> p t c", p=P)
        with nc.Block() as block:
            @block.sync
            def _(sp):
                for h in range(2):
                    sp.dma_start(xall[:, h * H:(h + 1) * H, :], tiles(dr["x2"], h)).then_inc(loaded[h], 16)
                sp.dma_start(gain[:], io["norm_final"].partition_broadcast(P)).then_inc(gain_in, 16)
                for t in range(NT):
                    sp.wait_ge(y_done, t + 1)
                    sp.dma_start(y[t * P:(t + 1) * P, :], xall[:, t, :]).then_inc(out, 16)
                sp.wait_ge(out, 16 * NT)

            @block.scalar
            def _(act):
                for t in range(NT):
                    if t % H == 0:
                        act.wait_ge(loaded[t // H], 16)
                    if t:
                        act.wait_ge(sumsq, t)
                    act.activation(sq[:], xall[:, t, :], ACT.Square, accum_out=ss[:, 0, t:t + 1]).then_inc(sumsq, 1)
                    if t % H == H - 1:
                        act.wait_ge(inv_done, t // H + 1)
                        act.activation(ss[:, 2, t - H + 1:t + 1], ss[:, 1, t - H + 1:t + 1], ACT.Sqrt).then_inc(rstd_done, 1)

            @block.vector
            def _(dve):
                dve.wait_ge(gain_in, 16)
                for h in range(2):
                    cols = slice(h * H, h * H + H)
                    dve.wait_ge(sumsq, H * (h + 1))
                    dve.tensor_scalar(ss[:, 1, cols], ss[:, 0, cols], 1.0 / D, EPS, ALU.mult, ALU.add).then_inc(mean_done, 1)
                    dve.wait_ge(mean_done, h + 1)
                    dve.reciprocal(ss[:, 1, cols], ss[:, 1, cols]).then_inc(inv_done, 1)
                    dve.wait_ge(rstd_done, h + 1)
                    for t in range(h * H, h * H + H):
                        dve.scalar_tensor_tensor(out=xall[:, t, :], in0=xall[:, t, :], scalar=ss[:, 2, t:t + 1], in1=gain[:], op0=ALU.mult, op1=ALU.mult).then_inc(y_done, 1)


def layer(nc, io, y):
    dram = lambda n, s, d=F32: nc.dram_tensor(n, s, d, kind="Internal").ap()
    dr = dict(
        qkv_ch=dram("qkv_ch", [A_TILES * P, GAP]), qkv_tok=dram("qkv_tok", [T, A_TILES * P]),
        qk_att=dram("qk_att", [A_TILES * P, QK_COLS]), proj_tok=dram("proj_tok", [T, TOK_COLS]),
        cols=dram("cols", [T, 2 * COLS]), rows=dram("rows", [32, T]),
        v_att=dram("v_att", [3, V_ROWS, GH * HD]), att_out=dram("att_out", [T, 3 * OUT_W]),
        laq=dram("laq", [STEPS, P, 3 * NH * CH]), diag=dram("diag", [NH, STEPS, P, BLK]), blocks=dram("blocks", [2, NH, STEPS, P, BLK]),
        o_delta=dram("o_delta", [2, T, NH * HD]), x2=dram("x2", [T, D]), hn=dram("hn", [T, D]),
        idx=dram("idx", [EXPERTS, SLOTS], U32), gate=dram("gate", [EXPERTS, SLOTS]),
    )
    with nc.sbuf_tensor("identity", [P, P], F32) as ident:
        with nc.sbuf_tensor("normed", [P, KT, T], F32) as normed:
            phase_norm(nc, io, normed, ident)
            phase_channels(nc, io, dr, normed, ident)
            phase_tokens(nc, io, dr, normed)
        phase_decay(nc, io, dr, ident)
        phase_attention(nc, io, dr, ident)
        phase_scores(nc, io, dr)
        phase_invert(nc, io, dr)
        phase_delta(nc, io, dr)
        phase_merge(nc, io, dr, ident)
        phase_experts(nc, io, dr, ident)
        phase_final(nc, io, dr, y)


def constants():
    i = np.arange(P)
    same = i[:, None] // CH == i[None] // CH
    tri = np.stack([same & (i[:, None] <= i[None]), same & (i[:, None] >= i[None]), same], 1)
    power = np.zeros((P, A_TILES))
    power[:, :2 * NH * HD // P] = -0.5
    f = lambda a: np.ascontiguousarray(a, np.float32)
    return dict(ident=f(np.eye(P)), tri=f(tri), norm_power=f(power), headsum=f(same), att_bias=attention_bias(), **delta_constants())


def laid_out(inputs):
    a = {n: np.asarray(v) for n, v in inputs.items()}
    tiled = lambda w, width: np.ascontiguousarray(w.reshape(KT, P, -1, width).transpose(2, 1, 0, 3))
    w_in = a["w_in"][0]
    qkv_a = A_TILES * P
    qk_b = 2 * 3 * GH * HD
    z_end = qkv_a + TOK_COLS - (3 * GH * HD + 2 * D)
    return dict(
        x=np.concatenate([a["x_sample"][0], a["x_prompt"][0]]),
        norm_mix=a["norm_mix"], norm_ffn=a["norm_ffn"], norm_final=a["norm_final"].reshape(1, D), a_norm=a["a_norm"],
        w_ch=tiled(np.concatenate([w_in[:, :qkv_a], w_in[:, z_end:z_end + qk_b]], 1), P),
        w_tok=tiled(np.concatenate([w_in[:, qkv_a:z_end], w_in[:, z_end + qk_b:]], 1), TOK_BLOCK),
        conv_w=np.ascontiguousarray(a["conv_w"][0].T.reshape(A_TILES, P, CONV).transpose(1, 0, 2)),
        a_log=a["a_log"].reshape(1, 2 * HEADS), dt_bias=a["dt_bias"].reshape(1, 2 * HEADS),
        w_proj_a=a["w_proj_a"][0], w_proj_b=a["w_proj_b"][0], w_out=a["w_out"][0], w_router=a["w_router"][0],
        w_gate=a["w_gate"][0], w_up=a["w_up"][0], w_down=a["w_down"][0],
    )


def kernel(**inputs):
    import concourse.bacc as bacc
    from concourse.bass_utils import run_bass_kernel_spmd

    nc = bacc.Bacc("TRN2", target_bir_lowering=False, num_devices=1)
    arrays = {f"in_{n}": np.ascontiguousarray(v) for n, v in {**laid_out(inputs), **constants()}.items()}
    io = {n[3:]: nc.dram_tensor(n, a.shape, mybir.dt.from_np(a.dtype), kind="ExternalInput").ap() for n, a in arrays.items()}
    y = nc.dram_tensor("y", [T, D], F32, kind="ExternalOutput").ap()
    layer(nc, io, y)
    got = run_bass_kernel_spmd(nc, [arrays], core_ids=[0]).results[0]["y"]
    return got[TS:].reshape(1, TP, D), got[:TS].reshape(1, TS, D)
```

```python
from contextlib import ExitStack, contextmanager
import numpy as np
import concourse.bass as bass
from concourse import mybir

ALU = mybir.AluOpType
ACT = mybir.ActivationFunctionType
F32 = mybir.dt.float32
U32 = mybir.dt.uint32
AX = mybir.AxisListType
P = 128
D = 1024
KT = D // P
TS, TP = 1024, 256
T = TS + TP
NT = T // P
CHUNKS = ((0, 512), (512, 512), (1024, 256))
CONV = 5
RAW = T + 6
EPS = 1e-6
A_TILES = 12
TOK_COLS = 3360
TOK_BLOCK = 336
TOK_BLOCKS = TOK_COLS // TOK_BLOCK


@contextmanager
def signals(nc):
    held = []

    def signal(name):
        held.append(nc.alloc_semaphore(name))
        return held[-1]
    yield signal
    nc.clear_and_free_semaphores(held)
    nc.all_engine_barrier()


HEADS, HD = 8, 64
CH = 64
STEPS = T // CH
S_STEPS = TS // CH


def early(count, least):
    return isinstance(count, int) and count < least


def walk(engine, steps, peeled, body):
    for c in range(peeled):
        body(c, c % 2, c // 2)
    with engine.Fori(peeled // 2, steps // 2) as i:
        for b in range(2):
            body(2 * i + b, b, i)


F32R = mybir.dt.float32r


def rest(dve, out, whole, rounded):
    return dve.tensor_tensor(out, whole, rounded.bitcast(F32), ALU.subtract)


def multiply_split(pe, out, stationary, moving, first, last):
    pairs = ((0, 0), (0, 1), (1, 0))
    for n, (a, b) in enumerate(pairs):
        mm = pe.matmul(out, stationary[a], moving[b], start=(first and n == 0), stop=(last and n == len(pairs) - 1))
    return mm


def phase_norm(nc, io, nT, nT_lo, ident):
    with ExitStack() as ctx:
        sb = lambda n, s, d=F32: ctx.enter_context(nc.sbuf_tensor(n, s, d))
        ps = lambda n, s: ctx.enter_context(nc.psum_tensor(n, s, F32))
        sem = ctx.enter_context(signals(nc))

        xall = sb("xall", [P, NT, D])
        gain = sb("gain", [P, D])
        xn = sb("xn", [P, 2, D])
        sq = sb("sq", [P, D])
        ss = sb("ss", [P, 3, NT])

        px = ps("px", [P, 2, 2, 512])
        SPANS = ((0, 2), (2, 5), (5, NT))

        x_in = [sem(f"p1_x_in{g}") for g in range(len(SPANS))]
        const_in = sem("p1_const_in")
        sumsq = sem("p1_sumsq")
        mean_done = sem("p1_mean")
        inv_done = sem("p1_inv")
        rstd_done = sem("p1_rstd")
        xn_done = sem("p1_xn")
        xt_done = sem("p1_xt")
        rounded = sem("p1_rounded")
        rest_done = sem("p1_rest_done")

        with nc.Block() as block:
            @block.sync
            def _(sp):
                for g, (lo, hi) in enumerate(SPANS):
                    for t in range(lo, hi):
                        sp.dma_start(xall[:, t, :], io["x"][t * P:(t + 1) * P]).then_inc(x_in[g], 16)
                    if g == 0:
                        sp.dma_start(ident[:], io["ident"]).then_inc(const_in, 16)
                        sp.dma_start(gain[:], io["norm_mix"].partition_broadcast(P)).then_inc(const_in, 16)

            @block.scalar
            def _(act):
                for g, (lo, hi) in enumerate(SPANS):
                    act.wait_ge(x_in[g], 16 * (hi - lo))
                    for t in range(lo, hi):
                        if t:
                            act.wait_ge(sumsq, t)
                        act.activation(sq[:], xall[:, t, :], ACT.Square, accum_out=ss[:, 0, t:t + 1]).then_inc(sumsq, 1)
                    act.wait_ge(inv_done, g + 1)
                    act.activation(ss[:, 2, lo:hi], ss[:, 1, lo:hi], ACT.Sqrt).then_inc(rstd_done, 1)
                for t in range(NT):
                    for h in range(2):
                        act.wait_ge(xt_done, 2 * t + h + 1)
                        act.copy(nT[:, 4 * h:4 * h + 4, bass.ds(t * P, P)], px[:, t % 2, h, :].rearrange("p (k t) -> p k t", k=4)).then_inc(rounded, 1)

            @block.vector
            def _(dve):
                def inverse(g):
                    lo, hi = SPANS[g]
                    dve.wait_ge(sumsq, hi)
                    dve.tensor_scalar(ss[:, 1, lo:hi], ss[:, 0, lo:hi], 1.0 / D, EPS, ALU.mult, ALU.add).then_inc(mean_done, 1)
                    dve.wait_ge(mean_done, g + 1)
                    dve.reciprocal(ss[:, 1, lo:hi], ss[:, 1, lo:hi]).then_inc(inv_done, 1)

                def normalise(t):
                    if t >= 2:
                        dve.wait_ge(xt_done, 2 * (t - 2) + 2)
                    dve.scalar_tensor_tensor(out=xn[:, t % 2, :], in0=xall[:, t, :], scalar=ss[:, 2, t:t + 1], in1=gain[:], op0=ALU.mult, op1=ALU.mult).then_inc(xn_done, 1)

                def split(t):
                    for h in range(2):
                        here = lambda a: a[:, 4 * h:4 * h + 4, bass.ds(t * P, P)]
                        dve.wait_ge(rounded, 2 * t + h + 1)
                        rest(dve, here(nT_lo), px[:, t % 2, h, :].rearrange("p (k t) -> p k t", k=4), here(nT)).then_inc(rest_done, 1)

                for g in range(len(SPANS)):
                    inverse(g)
                dve.wait_ge(rstd_done, len(SPANS))
                dve.wait_ge(const_in, 32)
                normalise(0)
                normalise(1)
                for t in range(NT):
                    if t + 2 < NT:
                        normalise(t + 2)
                    split(t)

            @block.tensor
            def _(pe):
                pe.wait_ge(const_in, 32)
                for t in range(NT):
                    pe.wait_ge(xn_done, t + 1)
                    for h in range(2):
                        if t >= 2:
                            pe.wait_ge(rest_done, 2 * t + h - 3)
                        for k in range(4):
                            mm = pe.transpose(px[:, t % 2, h, k * P:(k + 1) * P], xn[:, t % 2, (4 * h + k) * P:(4 * h + k + 1) * P], ident[:])
                        mm.then_inc(xt_done, 1)


CH_TILES = 24
GAP = T + 2
PAD = 64
QK_COLS = PAD + TS + PAD + TP + PAD
GROUPS = (1, 4, 16)


def phase_channels(nc, io, dr, nT, nT_lo, ident):
    with ExitStack() as ctx:
        sb = lambda n, s, d=F32: ctx.enter_context(nc.sbuf_tensor(n, s, d))
        ps = lambda n, s: ctx.enter_context(nc.psum_tensor(n, s, F32))
        sem = ctx.enter_context(signals(nc))

        wbuf = sb("ch_w", [P, 2, KT, P])
        w_hi = sb("ch_w_rounded", [P, 2, KT, P], F32R)
        w_lo = sb("ch_w_rest", [P, 2, KT, P], F32R)
        taps = sb("ch_taps", [P, A_TILES, CONV])
        power = sb("ch_power", [P, A_TILES])
        headsum = sb("ch_headsum", [P, P])
        raw = sb("ch_raw", [P, 2, RAW])
        conv = sb("ch_conv", [P, GAP])
        act_out = sb("ch_act", [P, 2, GAP])
        sq = sb("ch_sq", [P, GAP])
        rn = sb("ch_rn", [P, GAP])
        kn = sb("ch_kn", [P, 2, GAP])
        tok = sb("ch_tok", [P, 2, NT, P])
        perm = sb("ch_perm", [P, 2, QK_COLS])
        eps = sb("ch_eps", [P, 1])

        wide = ps("ch_wide", [P, 2, 2, 512])
        tail = ps("ch_tail", [P, 512])
        aux = ps("ch_aux", [P, 3, 512])

        w_ready = [sem(f"ch_w_ready{b}") for b in range(2)]
        w_rounded = sem("ch_w_rounded")
        w_split = sem("ch_w_split")
        const_ready = sem("ch_const_ready")
        pads_ready = sem("ch_pads_ready")
        proj_done = sem("ch_proj_done")
        raw_done = sem("ch_raw_done")
        conv_step = sem("ch_conv_step")
        silu_done = sem("ch_silu_done")
        sq_done = sem("ch_sq_done")
        ss_done = sem("ch_ss_done")
        ln_done = sem("ch_ln_done")
        rn_done = sem("ch_rn_done")
        kn_done = sem("ch_kn_done")
        kn_out = [sem(f"ch_kn_out{b}") for b in range(2)]
        tr_done = sem("ch_tr_done")
        tok_done = sem("ch_tok_done")
        tok_out = [sem(f"ch_tok_out{b}") for b in range(2)]
        perm_out = [sem(f"ch_perm_out{b}") for b in range(2)]

        KN_STORES = 4

        def region(b, j):
            return wide[:, b, j, :] if j < 2 else tail[:, 0:CHUNKS[2][1]]

        with nc.Block() as block:
            @block.sync
            def _(sp):
                def load(c, b):
                    if not early(c, 2):
                        sp.wait_ge(w_split, c - 1)
                    sp.dma_start(wbuf[:, b], io["w_ch"][bass.ds(c, 1)].rearrange("a p k c -> (a p) k c")).then_inc(w_ready[b], 16)
                load(0, 0)
                sp.dma_start(taps[:], io["conv_w"]).then_inc(const_ready, 16)
                sp.dma_start(power[:], io["norm_power"]).then_inc(const_ready, 16)
                sp.dma_start(headsum[:], io["headsum"]).then_inc(const_ready, 16)
                load(1, 1)

                def store(c, b):
                    sp.wait_ge(kn_done, c + 1)
                    for h in range(2):
                        part = slice(HD * h, HD * h + HD)
                        for lo, hi, at in ((0, S_STEPS, 0), (S_STEPS, STEPS, GAP - T)):
                            dst = dr["qkv_ch"][lo:hi, :, bass.ds(2 * c + h, 1), :].rearrange("n d h t -> d (n h) t")
                            sp.dma_start(dst, kn[part, b, lo * CH + at:hi * CH + at].rearrange("p (n t) -> p n t", t=CH)).then_inc(kn_out[b], 16)
                with sp.Fori(1, A_TILES // 2 + 1) as i:
                    for b in range(2):
                        load(2 * i + b, b)
                        store(2 * i + b - 2, b)
                with sp.Fori(A_TILES // 2 + 1, CH_TILES // 2) as i:
                    for b in range(2):
                        load(2 * i + b, b)
                for b in range(2):
                    sp.wait_ge(kn_out[b], KN_STORES * 16 * A_TILES // 2)

            @block.gpsimd
            def _(pool):
                pool.memset(raw[:], 0.0).then_inc(pads_ready, 1)
                pool.memset(rn[:], 0.0).then_inc(pads_ready, 1)
                pool.memset(eps[:], EPS).then_inc(pads_ready, 1)
                pool.memset(perm[:], 0.0).then_inc(pads_ready, 1)

                def store(c, b, i):
                    pool.wait_ge(tok_done, 3 * c + 3)
                    pool.dma_start(dr["qkv_tok"][:, bass.ds(c * P, P)].rearrange("(t p) c -> p t c", p=P), tok[:, b]).then_inc(tok_out[b], 16)
                walk(pool, A_TILES, 0, store)

                def store_permuted(c, b):
                    pool.wait_ge(raw_done, 3 * c + 3)
                    pool.dma_start(dr["qk_att"][bass.ds((c - A_TILES) * P, P), :], perm[:, b]).then_inc(perm_out[b], 16)
                with pool.Fori(A_TILES // 2, CH_TILES // 2) as i:
                    for b in range(2):
                        store_permuted(2 * i + b, b)
                for b in range(2):
                    pool.wait_ge(tok_out[b], 16 * A_TILES // 2)
                    pool.wait_ge(perm_out[b], 16 * (CH_TILES - A_TILES) // 2)

            @block.tensor
            def _(pe):
                def project(c, b, i, j):
                    if j == 0:
                        pe.wait_ge(w_split, c + 1)
                    if j < 2 and not early(c, 2):
                        pe.wait_ge(raw_done, 3 * (c - 2) + j + 1)
                    if j == 2 and not early(c, 1):
                        pe.wait_ge(raw_done, 3 * c)
                    at, n = CHUNKS[j]
                    for k in range(KT):
                        mm = multiply_split(pe, region(b, j)[:, 0:n], (w_hi[:, b, k, :], w_lo[:, b, k, :]),
                                            (nT[:, k, at:at + n], nT_lo[:, k, at:at + n]), k == 0, k == KT - 1)
                    mm.then_inc(proj_done, 1)

                def to_tokens(c, b):
                    pe.wait_ge(kn_done, c + 1)
                    for t in range(NT):
                        at = t * P + (2 if t >= TS // P else 0)
                        mm = pe.transpose(aux[:, t // 4, (t % 4) * P:(t % 4 + 1) * P], kn[:, b, at:at + P], ident[:])
                        if t in (3, 7, NT - 1):
                            mm.then_inc(tr_done, 1)

                def head_sums(c, b):
                    pe.wait_ge(sq_done, c + 1)
                    if not early(c, 1):
                        pe.wait_ge(tok_done, 3 * c)
                    for j, (at, n) in enumerate(CHUNKS):
                        at += 2 if j == 2 else 0
                        mm = pe.matmul(aux[:, j, 0:n], headsum[:], sq[:, at:at + n], start=True, stop=True)
                    mm.then_inc(ss_done, 1)

                def tile(c, b, i, gemm=True):
                    if gemm:
                        project(c, b, i, 0)
                    if not early(c, 2):
                        to_tokens(c - 2, b)
                    if gemm:
                        project(c, b, i, 1)
                    if not early(c, 1) and not (isinstance(c, int) and c > A_TILES):
                        head_sums(c - 1, 1 - b)
                    if gemm:
                        project(c, b, i, 2)
                pe.wait_ge(const_ready, 48)
                walk(pe, A_TILES, 2, tile)
                tile(A_TILES, 0, A_TILES // 2)
                tile(A_TILES + 1, 1, A_TILES // 2)
                with pe.Fori(A_TILES // 2 + 1, CH_TILES // 2) as i:
                    for b in range(2):
                        for j in range(3):
                            project(2 * i + b, b, i, j)

            @block.scalar
            def _(act):
                act.wait_ge(pads_ready, 4)
                act.wait_ge(const_ready, 48)

                def evacuate(c, b, j):
                    act.wait_ge(proj_done, 3 * c + j + 1)
                    if j == 0 and not early(c, 2):
                        act.wait_ge(conv_step, CONV * (c - 1))
                    at, n = CHUNKS[j]
                    at += 2 + (2 if j == 2 else 0)
                    act.copy(raw[:, b, at:at + n], region(b, j)[:, 0:n]).then_inc(raw_done, 1)

                def tokens_out(c, b, i):
                    if not early(c, 2):
                        act.wait_ge(tok_out[b], 16 * i)
                    for j, (lo, hi) in enumerate(((0, 4), (4, 8), (8, NT))):
                        act.wait_ge(tr_done, 3 * c + j + 1)
                        act.copy(tok[:, b, lo:hi, :], aux[:, j, 0:(hi - lo) * P].rearrange("p (t c) -> p t c", c=P)).then_inc(tok_done, 1)

                def inverse_norm(c):
                    act.wait_ge(ss_done, c + 1)
                    if not early(c, 1):
                        act.wait_ge(kn_done, c)
                    act.activation(rn[:, 0:TS], aux[:, 0:2, :], ACT.Ln, bias=eps[:]).then_inc(ln_done, 1)
                    act.activation(rn[:, TS + 2:], aux[:, 2, 0:TP], ACT.Ln, bias=eps[:]).then_inc(ln_done, 1)
                    act.wait_ge(ln_done, 2 * c + 2)
                    act.activation(rn[:], rn[:], ACT.Exp, scale=power[:, bass.ds(c, 1)]).then_inc(rn_done, 1)

                def silu(c, b):
                    act.wait_ge(conv_step, CONV * (c + 1))
                    if not early(c, 2):
                        act.wait_ge(kn_done, c - 1)
                    act.activation(act_out[:, b], conv[:], ACT.Silu).then_inc(silu_done, 1)
                    act.wait_ge(silu_done, c + 1)
                    if not early(c, 1):
                        act.wait_ge(ss_done, c)
                    act.activation(sq[:], act_out[:, b], ACT.Square).then_inc(sq_done, 1)

                def tile(c, b, i):
                    evacuate(c, b, 0)
                    if not early(c, 2):
                        tokens_out(c - 2, b, i - 1)
                    evacuate(c, b, 1)
                    if not early(c, 1):
                        inverse_norm(c - 1)
                    evacuate(c, b, 2)
                    silu(c, b)
                walk(act, A_TILES, 4, tile)

                def permute(c, b, dilation, j):
                    act.wait_ge(proj_done, 3 * c + j + 1)
                    if j == 0 and not early(c, A_TILES + 2):
                        act.wait_ge(perm_out[b], 16 * ((c - A_TILES) // 2))
                    at, n = CHUNKS[j]
                    length = (TS if j < 2 else TP) // dilation
                    base = PAD if j < 2 else 2 * PAD + TS
                    first = at // dilation if j < 2 else 0
                    out = perm[:, b, base:base + length * dilation].rearrange("p (f t) -> p f t", f=dilation)[:, :, first:first + n // dilation]
                    act.copy(out, region(b, j)[:, 0:n].rearrange("p (t f) -> p f t", f=dilation)).then_inc(raw_done, 1)

                c = A_TILES
                for j in range(3):
                    permute(c, 0, GROUPS[0], j)
                    if j == 0:
                        tokens_out(A_TILES - 2, 0, A_TILES // 2 - 1)
                    if j == 1:
                        inverse_norm(A_TILES - 1)
                for j in range(3):
                    permute(c + 1, 1, GROUPS[0], j)
                    if j == 0:
                        tokens_out(A_TILES - 1, 1, A_TILES // 2 - 1)
                for pair in range(1, 6):
                    for b in range(2):
                        for j in range(3):
                            permute(A_TILES + 2 * pair + b, b, GROUPS[pair % 3], j)

            @block.vector
            def _(dve):
                dve.wait_ge(const_ready, 48)

                def split(c, b, i):
                    dve.wait_ge(w_ready[b], 16 * (i + 1))
                    if not early(c, 2):
                        dve.wait_ge(proj_done, 3 * c - 3)
                    dve.tensor_copy(w_hi[:, b], wbuf[:, b]).then_inc(w_rounded, 1)
                    dve.wait_ge(w_rounded, c + 1)
                    rest(dve, w_lo[:, b], wbuf[:, b], w_hi[:, b]).then_inc(w_split, 1)

                def normalise(c, b, i):
                    dve.wait_ge(rn_done, c + 1)
                    if not early(c, 2):
                        dve.wait_ge(tr_done, 3 * c - 3)
                        dve.wait_ge(kn_out[b], KN_STORES * 16 * i)
                    dve.tensor_tensor(kn[:, b], act_out[:, b], rn[:], ALU.mult).then_inc(kn_done, 1)

                def convolve(c, b):
                    dve.wait_ge(raw_done, 3 * c + 3)
                    if not early(c, 1):
                        dve.wait_ge(silu_done, c)
                    for j in range(CONV):
                        tap = taps[:, bass.ds(c, 1), j:j + 1].rearrange("p a b -> p (a b)")
                        if j == 0:
                            dve.tensor_scalar(conv[:], raw[:, b, 0:GAP], tap, None, ALU.mult).then_inc(conv_step, 1)
                        else:
                            dve.wait_ge(conv_step, CONV * c + j)
                            dve.scalar_tensor_tensor(out=conv[:], in0=raw[:, b, j:j + GAP], scalar=tap, in1=conv[:],
                                                     op0=ALU.mult, op1=ALU.add).then_inc(conv_step, 1)

                def tile(c, b, i):
                    split(c + 1, 1 - b, i + b)
                    if not early(c, 1):
                        normalise(c - 1, 1 - b, i - (1 - b))
                    convolve(c, b)
                split(0, 0, 0)
                walk(dve, A_TILES, 4, tile)
                split(A_TILES + 1, 1, A_TILES // 2)
                normalise(A_TILES - 1, 1, A_TILES // 2 - 1)
                with dve.Fori(A_TILES // 2 + 1, CH_TILES // 2) as i:
                    for b in range(2):
                        split(2 * i + b, b, i)


Z_AT, BETA_AT, ALPHA_AT, V_AT, GATE_AT = 0, 512, 528, 544, 1312


def phase_tokens(nc, io, dr, nT, nT_lo):
    with ExitStack() as ctx:
        sb = lambda n, s, d=F32: ctx.enter_context(nc.sbuf_tensor(n, s, d))
        ps = lambda n, s: ctx.enter_context(nc.psum_tensor(n, s, F32))
        sem = ctx.enter_context(signals(nc))
        BANKS = 4
        PARTS = 4
        wbuf = sb("tk_w", [P, KT, TOK_BLOCK])
        w_hi = sb("tk_w_rounded", [P, 2, KT, TOK_BLOCK], F32R)
        w_lo = sb("tk_w_rest", [P, 2, KT, TOK_BLOCK], F32R)
        stage = sb("tk_stage", [P, 2, NT, TOK_BLOCK])
        acc = ps("tk_acc", [P, BANKS, 512])
        w_ready = sem("tk_w_ready")
        w_rounded = sem("tk_w_rounded")
        w_split = sem("tk_w_split")
        stored = [sem(f"tk_stored{b}") for b in range(2)]
        mm_done = sem("tk_mm_done")
        copied = {0: sem("tk_copied_act"), 1: sem("tk_copied_dve")}

        with nc.Block() as block:
            @block.sync
            def _(sp):
                def load(c):
                    if not early(c, 1):
                        sp.wait_ge(w_split, PARTS * c)
                    sp.dma_start(wbuf[:], io["w_tok"][bass.ds(c, 1)].rearrange("a p k c -> (a p) k c")).then_inc(w_ready, 16)

                def store(c, b, i):
                    sp.wait_ge(copied[0], NT // 2 * (c + 1))
                    sp.wait_ge(copied[1], NT // 2 * (c + 1))
                    sp.dma_start(dr["proj_tok"][:, bass.ds(c * TOK_BLOCK, TOK_BLOCK)].rearrange("(t p) c -> p t c", p=P), stage[:, b]).then_inc(stored[b], 16)

                def turn(c, b, i):
                    load(c + 1)
                    if not early(c, 1):
                        store(c - 1, 1 - b, i - (1 - b))
                load(0)
                walk(sp, TOK_BLOCKS - 2, 2, turn)
                turn(TOK_BLOCKS - 2, 0, TOK_BLOCKS // 2 - 1)
                for c in (TOK_BLOCKS - 2, TOK_BLOCKS - 1):
                    store(c, c % 2, c // 2)
                for b in range(2):
                    sp.wait_ge(stored[b], 16 * TOK_BLOCKS // 2)

            @block.tensor
            def _(pe):
                def multiply(c, b, i):
                    pe.wait_ge(w_split, PARTS * (c + 1))
                    for t in range(NT):
                        if not (early(c, 1) and t < BANKS):
                            pe.wait_ge(copied[t % 2], NT // 2 * c + t // 2 - 1)
                        bank = (NT * b + t) % BANKS
                        for k in range(KT):
                            mm = multiply_split(pe, acc[:, bank, 0:TOK_BLOCK], (nT[:, k, t * P:(t + 1) * P], nT_lo[:, k, t * P:(t + 1) * P]),
                                                (w_hi[:, b, k, :], w_lo[:, b, k, :]), k == 0, k == KT - 1)
                        mm.then_inc(mm_done, 1)
                walk(pe, TOK_BLOCKS, 2, multiply)

            def copy_out(engine, copy, c, b, t):
                engine.wait_ge(mm_done, NT * c + t + 1)
                copy(stage[:, b, t, :], acc[:, (NT * b + t) % BANKS, 0:TOK_BLOCK]).then_inc(copied[t % 2], 1)

            @block.scalar
            def _(act):
                def block_out(c, b, i):
                    if not early(c, 2):
                        act.wait_ge(stored[b], 16 * i)
                    for t in range(0, NT, 2):
                        copy_out(act, act.copy, c, b, t)
                walk(act, TOK_BLOCKS, 2, block_out)

            @block.vector
            def _(dve):
                def split(c, b, i, part):
                    ks = slice(part * KT // PARTS, (part + 1) * KT // PARTS)
                    if part == 0:
                        dve.wait_ge(w_ready, 16 * (c + 1))
                        if not early(c, 2):
                            dve.wait_ge(mm_done, NT * (c - 1))
                    dve.tensor_copy(w_hi[:, b, ks], wbuf[:, ks]).then_inc(w_rounded, 1)
                    dve.wait_ge(w_rounded, PARTS * c + part + 1)
                    rest(dve, w_lo[:, b, ks], wbuf[:, ks], w_hi[:, b, ks]).then_inc(w_split, 1)

                def block_out(c, b, i, more=True):
                    if not early(c, 2):
                        dve.wait_ge(stored[b], 16 * i)
                    for t in range(1, NT, 2):
                        copy_out(dve, dve.tensor_copy, c, b, t)
                        if more and t // 2 < PARTS:
                            split(c + 1, 1 - b, i + b, t // 2)
                for part in range(PARTS):
                    split(0, 0, 0, part)
                for c in range(2):
                    block_out(c, c, 0)
                with dve.Fori(1, TOK_BLOCKS // 2 - 1) as i:
                    for b in range(2):
                        block_out(2 * i + b, b, i)
                block_out(TOK_BLOCKS - 2, 0, TOK_BLOCKS // 2 - 1)
                block_out(TOK_BLOCKS - 1, 1, TOK_BLOCKS // 2 - 1, more=False)


COLS = 5 * HEADS


def phase_decay(nc, io, dr, ident):
    with ExitStack() as ctx:
        sb = lambda n, s, d=F32: ctx.enter_context(nc.sbuf_tensor(n, s, d))
        ps = lambda n, s: ctx.enter_context(nc.psum_tensor(n, s, F32))
        sem = ctx.enter_context(signals(nc))
        ba = sb("dc_ba", [P, NT, 4, HEADS])
        bias = sb("dc_bias", [P, 2, HEADS])
        rate = sb("dc_rate", [P, 2, HEADS])
        tri = sb("dc_tri", [P, 3, P])
        beta = sb("dc_beta", [P, NT, 2, HEADS])
        shifted = sb("dc_shifted", [P, NT, 2, HEADS])
        tmp = sb("dc_tmp", [P, NT, 2, HEADS])
        g = sb("dc_g", [P, NT, 2, HEADS])
        cols = sb("dc_cols", [P, NT, 2, 5, HEADS])
        packed = sb("dc_packed", [P, NT, 32])
        rows = sb("dc_rows", [32, NT, P])
        sums = ps("dc_sums", [P, 4, NT * HEADS])
        turned = ps("dc_turned", [P, 3, 512])
        loaded = sem("dc_loaded")
        a_step = sem("dc_act_step")
        v_step = sem("dc_dve_step")
        p_step = sem("dc_pe_step")
        out = sem("dc_out")
        bc = lambda a: a.rearrange("p d h -> p (d h)").unsqueeze(1).to_broadcast([P, NT, 2 * HEADS])
        flat = lambda a: a.rearrange("p t d h -> p t (d h)")

        with nc.Block() as block:
            @block.sync
            def _(sp):
                sp.dma_start(ba[:].rearrange("p t k h -> p t (k h)"), dr["proj_tok"][:, BETA_AT:BETA_AT + 32].rearrange("(t p) c -> p t c", p=P)).then_inc(loaded, 16)
                sp.dma_start(bias[:].rearrange("p d h -> p (d h)"), io["dt_bias"].partition_broadcast(P)).then_inc(loaded, 16)
                sp.dma_start(rate[:].rearrange("p d h -> p (d h)"), io["a_log"].partition_broadcast(P)).then_inc(loaded, 16)
                sp.dma_start(tri[:], io["tri"]).then_inc(loaded, 16)
                sp.wait_ge(a_step, 9)
                sp.dma_start(dr["cols"].rearrange("(t p) c -> p t c", p=P), cols[:].rearrange("p t d k h -> p t (d k h)")).then_inc(out, 16)
                sp.wait_ge(v_step, 15)
                for d in range(2):
                    sp.dma_start(dr["rows"][d].rearrange("n r t -> r n t"), rows[16 * d:16 * d + 16].rearrange("r t (h c) -> r (t h) c", c=CH)).then_inc(out, 16)
                sp.wait_ge(out, 48)

            @block.scalar
            def _(act):
                act.wait_ge(loaded, 64)
                act.activation(tmp[:], ba[:, :, 0:2, :], ACT.Exp, scale=-1.0).then_inc(a_step, 1)
                act.activation(rate[:], rate[:], ACT.Exp).then_inc(a_step, 1)
                act.wait_ge(v_step, 3)
                act.activation(tmp[:], shifted[:], ACT.Abs).then_inc(a_step, 1)
                act.wait_ge(a_step, 3)
                act.activation(tmp[:], tmp[:], ACT.Exp, scale=-1.0).then_inc(a_step, 1)
                act.wait_ge(a_step, 4)
                act.activation(tmp[:], tmp[:], ACT.Ln, bias=1.0).then_inc(a_step, 1)
                act.wait_ge(v_step, 10)
                act.activation(cols[:, :, :, 2, :], cols[:, :, :, 2, :], ACT.Exp).then_inc(a_step, 1)
                act.activation(cols[:, :, :, 1, :], cols[:, :, :, 4, :], ACT.Exp).then_inc(a_step, 1)
                for d in range(2):
                    act.activation(cols[:, :, d, 3, :], sums[:, 2 + d, :].rearrange("p (t h) -> p t h", h=HEADS), ACT.Exp).then_inc(a_step, 1)

            @block.tensor
            def _(pe):
                pe.wait_ge(loaded, 64)
                pe.wait_ge(v_step, 5)
                for d in range(2):
                    gd = g[:, :, d, :]
                    pe.matmul(sums[:, d, :].rearrange("p (t h) -> p t h", h=HEADS), tri[:, d, :], gd, start=True, stop=True)
                    mm = pe.matmul(sums[:, 2 + d, :].rearrange("p (t h) -> p t h", h=HEADS), tri[:, 2, :], gd, start=True, stop=True)
                mm.then_inc(p_step, 1)
                pe.wait_ge(v_step, 12)
                for t in range(NT):
                    mm = pe.transpose(turned[0:32, t // 4, (t % 4) * P:(t % 4 + 1) * P], packed[:, t, :], ident[:])
                mm.then_inc(p_step, 1)

            @block.vector
            def _(dve):
                def step(ins):
                    ins.then_inc(v_step, 1)
                dve.wait_ge(loaded, 64)
                dve.wait_ge(a_step, 1)
                step(dve.tensor_scalar(beta[:], tmp[:], 1.0, None, ALU.add))
                dve.wait_ge(v_step, 1)
                step(dve.reciprocal(beta[:], beta[:]))
                step(dve.tensor_tensor(flat(shifted[:]), flat(ba[:, :, 2:4, :]), bc(bias[:]), ALU.add))
                dve.wait_ge(a_step, 5)
                dve.wait_ge(v_step, 3)
                step(dve.scalar_tensor_tensor(out=tmp[:], in0=shifted[:], scalar=0.0, in1=tmp[:], op0=ALU.max, op1=ALU.add))
                dve.wait_ge(v_step, 4)
                step(dve.scalar_tensor_tensor(out=flat(g[:]), in0=flat(tmp[:]), scalar=-1.0, in1=bc(rate[:]),
                                              op0=ALU.mult, op1=ALU.mult))
                dve.wait_ge(p_step, 1)
                step(dve.tensor_copy(cols[:, :, :, 0, :], beta[:]))
                for d in range(2):
                    step(dve.tensor_copy(cols[:, :, d, 4, :], sums[:, d, :].rearrange("p (t h) -> p t h", h=HEADS)))
                dve.wait_ge(v_step, 8)
                for d in range(2):
                    step(dve.tensor_tensor(cols[:, :, d, 2, :], sums[:, 2 + d, :].rearrange("p (t h) -> p t h", h=HEADS), cols[:, :, d, 4, :], ALU.subtract))
                for k in range(2):
                    step(dve.tensor_copy(packed[:].rearrange("p t (d k h) -> p t d k h", d=2, k=2)[:, :, :, k, :], cols[:, :, :, 4 * k, :]))
                dve.wait_ge(p_step, 2)
                for j, (lo, hi) in enumerate(((0, 4), (4, 8), (8, NT))):
                    step(dve.tensor_copy(rows[:, lo:hi, :], turned[0:32, j, 0:(hi - lo) * P].rearrange("r (t p) -> r t p", p=P)))


GH = 4
WIN = 2 * P
OUT_W = GH * HD + 2 * GH
V_ROWS = QK_COLS
UNIT_HEADS = [2 * (s % 2) + s // 2 for s in range(GH)]


def back(t, b, i, g, n):
    g -= n
    while g < 0:
        g, t, b, i = g + 3, t - 1, 1 - b, i - (1 - b)
    return t, b, i, g


def phase_attention(nc, io, dr, ident):
    with ExitStack() as ctx:
        sb = lambda n, s, d=F32: ctx.enter_context(nc.sbuf_tensor(n, s, d))
        ps = lambda n, s: ctx.enter_context(nc.psum_tensor(n, s, F32))
        sem = ctx.enter_context(signals(nc))
        q = sb("at_q", [P, 2, 3, 2, P])
        k = sb("at_k", [P, 2, 3, 2, WIN])
        v = sb("at_v", [P, 2, 2, 3, GH * HD])
        bias = sb("at_bias", [P, 2, 3, GH * WIN])
        s = sb("at_s", [P, 2, GH, WIN])
        p = sb("at_p", [P, 2, GH, WIN])
        pt = sb("at_pt", [P, 2, 2, GH, P])
        negmax = sb("at_negmax", [P, 2, GH])
        stage = sb("at_stage", [P, 2, 3, OUT_W])
        scores = ps("at_scores", [P, 2, 2, 2, WIN])
        turned = ps("at_turned", [P, 2, GH, P])
        values = ps("at_values", [P, 2, 512])
        invert = inversion(nc, ctx, io, dr, sem)
        loaded = [sem(f"at_loaded{b}") for b in range(2)]
        stored = [sem(f"at_stored{b}") for b in range(2)]
        scored = sem("at_scored")
        biased = sem("at_biased")
        max_done = sem("at_max_done")
        neg_done = sem("at_neg_done")
        exp_done = sem("at_exp_done")
        turned_done = sem("at_turned_done")
        pt_act = sem("at_pt_act")
        pt_dve = sem("at_pt_dve")
        weighed = sem("at_weighed")
        row_done = sem("at_row_done")

        def places_of(t, b, i):
            prompt = isinstance(t, int) and t >= TS // P
            first, n = (TS, TP) if prompt else (0, TS)
            tile = t - first // P
            out = []
            for g, f in enumerate(GROUPS):
                length = n // f
                rows = dr["att_out"][first:first + n, g * OUT_W:(g + 1) * OUT_W].rearrange("(t f) c -> f t c", f=f)
                if length >= P:
                    phase = tile if length == P else (0 if f == 1 else i)
                    at = (t * P - first) if f == 1 else b * P
                    out.append((rows[bass.ds(phase, 1), bass.ds(at, P), :].rearrange("f t c -> (f t) c"), (slice(0, P), g)))
                else:
                    for x in range(P // length):
                        out.append((rows[bass.ds(tile * (P // length) + x, 1)].rearrange("f t c -> (f t) c"), (slice(x * length, (x + 1) * length), g)))
            return out

        with nc.Block() as block:
            @block.sync
            def _(sp):
                rows = dr["qk_att"].rearrange("(s g p) c -> p s g c", s=2, p=P)
                vrows = dr["v_att"].rearrange("g r c -> r g c")

                def load(t, b, i):
                    if not early(t, 2):
                        sp.wait_ge(weighed, 3 * (t - 1))
                    q0 = P * t + PAD + (PAD if isinstance(t, int) and t >= TS // P else 0)
                    sp.dma_start(q[:, b].rearrange("p g j c -> p (g j) c"), rows[:, 0, :, bass.ds(q0, P)]).then_inc(loaded[b], 16)
                    sp.dma_start(k[:, b].rearrange("p g j c -> p (g j) c"), rows[:, 1, :, bass.ds(q0 - PAD, WIN)]).then_inc(loaded[b], 16)
                    for h in range(2):
                        sp.dma_start(v[:, b, h], vrows[bass.ds(q0 - PAD + h * P, P)]).then_inc(loaded[b], 16)
                    groups = 3 if isinstance(t, int) else 1
                    src = io["att_bias"][bass.ds(t, 1), :, 0:groups * GH * WIN].rearrange("a p c -> (a p) c")
                    sp.dma_start(bias[:, b, 0:groups].rearrange("p g c -> p (g c)"), src).then_inc(loaded[b], 16)

                def store(t, b, i):
                    sp.wait_ge(row_done, 3 * t + 3)
                    for rows, part in places_of(t, b, i):
                        sp.dma_start(rows, stage[part[0], b, part[1], :]).then_inc(stored[b], 16)

                def turn(t, b, i):
                    load(t, b, i)
                    if not early(t, 2):
                        store(t - 2, b, i - 1)
                walk(sp, TS // P, 2, turn)
                for t in (TS // P, TS // P + 1):
                    turn(t, t % 2, t // 2)
                for t in (TS // P, TS // P + 1):
                    store(t, t % 2, t // 2)
                for b in range(2):
                    sp.wait_ge(stored[b], 16 * (4 * TS // P // 2 + len(places_of(TS // P + b, b, 0))))

            @block.gpsimd
            def _(pool):
                invert(pool)

            @block.tensor
            def _(pe):
                def score(t, b, i, g):
                    u = 3 * t + g
                    r = (3 * b + g) % 2
                    if g == 0:
                        pe.wait_ge(loaded[b], 80 * (i + 1))
                    if not early(u, 2):
                        pe.wait_ge(biased, u - 1)
                    for slot, h in enumerate(UNIT_HEADS):
                        rows = slice(HD * (h % 2), HD * (h % 2) + HD)
                        mm = pe.matmul(scores[:, r, h % 2, h // 2, :], q[rows, b, g, h // 2, :], k[rows, b, g, h // 2, :], start=True, stop=True)
                    mm.then_inc(scored, 1)

                def turn(t, b, i, g):
                    u = 3 * t + g
                    r = (3 * b + g) % 2
                    pe.wait_ge(exp_done, u + 1)
                    if not early(u, 1):
                        pe.wait_ge(pt_act, u)
                        pe.wait_ge(pt_dve, u)
                    for half in range(2):
                        for slot in range(GH):
                            mm = pe.transpose(turned[:, half, slot, :], p[:, r, slot, half * P:(half + 1) * P], ident[:])
                    mm.then_inc(turned_done, 1)

                def weigh(t, b, i, g):
                    u = 3 * t + g
                    r = (3 * b + g) % 2
                    pe.wait_ge(pt_act, u + 1)
                    pe.wait_ge(pt_dve, u + 1)
                    if not early(u, 2):
                        pe.wait_ge(row_done, u - 1)
                    for slot, h in enumerate(UNIT_HEADS):
                        for half in range(2):
                            mm = pe.matmul(values[:, r, h * HD:(h + 1) * HD], pt[:, r, half, slot, :], v[:, b, half, g, h * HD:(h + 1) * HD],
                                           start=(half == 0), stop=(half == 1))
                    mm.then_inc(weighed, 1)

                def tile(t, b, i):
                    for g in range(3):
                        score(t, b, i, g)
                        if not early(3 * t + g, 2):
                            weigh(*back(t, b, i, g, 2))
                        if not early(3 * t + g, 1):
                            turn(*back(t, b, i, g, 1))
                walk(pe, NT, 2, tile)
                last = (NT, 0, NT // 2, 0)
                weigh(*back(*last, 2))
                turn(*back(*last, 1))
                weigh(*back(*last, 1))

            @block.scalar
            def _(act):
                def exponentials(t, b, i, g):
                    u = 3 * t + g
                    r = (3 * b + g) % 2
                    act.wait_ge(neg_done, u + 1)
                    if not early(u, 2):
                        act.wait_ge(turned_done, u - 1)
                    for slot, h in enumerate(UNIT_HEADS):
                        e = act.activation(p[:, r, slot, :], s[:, r, slot, :], ACT.Exp, bias=negmax[:, r, h:h + 1],
                                           accum_out=stage[:, b, g, GH * HD + GH + h:GH * HD + GH + h + 1])
                    e.then_inc(exp_done, 1)

                def turned_out(t, b, i, g):
                    u = 3 * t + g
                    act.wait_ge(turned_done, u + 1)
                    if not early(u, 2):
                        act.wait_ge(weighed, u - 1)
                    act.copy(pt[:, (3 * b + g) % 2, 0], turned[:, 0]).then_inc(pt_act, 1)

                def tile(t, b, i):
                    for g in range(3):
                        exponentials(t, b, i, g)
                        if not early(3 * t + g, 1):
                            turned_out(*back(t, b, i, g, 1))
                walk(act, NT, 2, tile)
                turned_out(*back(NT, 0, NT // 2, 0, 1))

            @block.vector
            def _(dve):
                def maxima(t, b, i, g):
                    u = 3 * t + g
                    r = (3 * b + g) % 2
                    dve.wait_ge(scored, u + 1)
                    if g == 0:
                        dve.wait_ge(loaded[b], 80 * (i + 1))
                        if not early(t, 2):
                            dve.wait_ge(stored[b], 64 * i)
                    if not early(u, 2):
                        dve.wait_ge(exp_done, u - 1)
                    dve.scalar_tensor_tensor(out=s[:, r].rearrange("p h c -> p (h c)"), in0=scores[:, r].rearrange("p a j c -> p (a j c)"), scalar=HD ** -0.5,
                                             in1=bias[:, b, g, :], op0=ALU.mult, op1=ALU.add).then_inc(biased, 1)
                    dve.wait_ge(biased, u + 1)
                    top = stage[:, b, g, GH * HD:GH * HD + GH]
                    dve.tensor_reduce(top.rearrange("p (j r) -> p r j", r=2), s[:, r].rearrange("p (r j) c -> p r j c", r=2), AX.X, ALU.max).then_inc(max_done, 1)
                    dve.wait_ge(max_done, u + 1)
                    dve.tensor_scalar(negmax[:, r, :], top, -1.0, None, ALU.mult).then_inc(neg_done, 1)

                def turned_out(t, b, i, g):
                    u = 3 * t + g
                    dve.wait_ge(turned_done, u + 1)
                    if not early(u, 2):
                        dve.wait_ge(weighed, u - 1)
                    dve.tensor_copy(pt[:, (3 * b + g) % 2, 1], turned[:, 1]).then_inc(pt_dve, 1)

                def rows_out(t, b, i, g):
                    u = 3 * t + g
                    dve.wait_ge(weighed, u + 1)
                    dve.tensor_copy(stage[:, b, g, 0:GH * HD], values[:, (3 * b + g) % 2, 0:GH * HD]).then_inc(row_done, 1)

                def tile(t, b, i):
                    for g in range(3):
                        maxima(t, b, i, g)
                        if not early(3 * t + g, 2):
                            rows_out(*back(t, b, i, g, 2))
                        if not early(3 * t + g, 1):
                            turned_out(*back(t, b, i, g, 1))
                walk(dve, NT, 2, tile)
                last = (NT, 0, NT // 2, 0)
                rows_out(*back(*last, 2))
                turned_out(*back(*last, 1))
                rows_out(*back(*last, 1))


def attention_bias():
    slopes = (2.0 ** (-8.0 * np.arange(1, 13) / 12)).astype(np.float32)
    out = np.full((NT, P, 3, GH, WIN), -1e30, np.float32)
    qi = np.arange(P)[:, None]
    delta = np.arange(WIN)[None, :] - PAD - qi
    for t in range(NT):
        n, tile = (TS, t) if t < TS // P else (TP, t - TS // P)
        for g, f in enumerate(GROUPS):
            length = n // f
            qpos = tile * P + qi
            kpos = qpos + delta
            valid = (np.abs(delta) <= 64) & (kpos >= 0) & (kpos < n) & (kpos // length == qpos // length)
            for slot, h in enumerate(UNIT_HEADS):
                b = -slopes[g * GH + h] * (np.abs(delta) * f).astype(np.float32)
                out[t, :, g, slot, :] = np.where(valid, b, np.float32(-1e30))
    return out.reshape(NT, P, 3 * GH * WIN)


BLK = 16
NH = HEADS


def places(s, prompt):
    return s, (S_STEPS + STEPS if prompt else S_STEPS) - 1 - s


def steps(engine, body, peeled=2):
    for c in range(peeled):
        body(c, c % 2, c // 2, False)
    with engine.Fori(peeled // 2, S_STEPS // 2) as i:
        for b in range(2):
            body(2 * i + b, b, i, False)
    for c in range(S_STEPS, STEPS):
        body(c, c % 2, c // 2, True)


def bc_head(a, n=HD):
    return a.unsqueeze(2).to_broadcast([P, NH, n])


def phase_scores(nc, io, dr):
    with ExitStack() as ctx:
        sb = lambda n, s, d=F32: ctx.enter_context(nc.sbuf_tensor(n, s, d))
        ps = lambda n, s: ctx.enter_context(nc.psum_tensor(n, s, F32))
        sem = ctx.enter_context(signals(nc))
        zero = sb("sc_zero", [PAD, 3, GH * HD])
        kbd = sb("sc_kbd", [P, 2, NH, P])
        qk = sb("sc_qk", [P, 2, 2 * NH, CH])
        rows = sb("sc_rows", [P, 2, 2 * NH, CH])
        cols = sb("sc_cols", [P, 2, 5, NH])
        diff = sb("sc_diff", [P, 2, NH, CH])
        decay = sb("sc_decay", [P, 2, NH, CH])
        bdecay = sb("sc_bdecay", [P, 2, NH, CH])
        growth = sb("sc_growth", [P, 2, NH, CH])
        laq = sb("sc_laq", [P, 2, 3, NH, CH])
        picked = sb("sc_picked", [P, 2, NH, CH])
        diag = sb("sc_diag", [P, 2, NH, BLK])
        causal = sb("sc_causal", [P, CH])
        own = sb("sc_own", [P, CH])
        prod = ps("sc_prod", [P, 2, NH, P])
        const_in = sem("sc_const_in")
        zeroed = sem("sc_zeroed")
        loaded = [sem(f"sc_loaded{b}") for b in range(2)]
        laq_stored = [sem(f"sc_laq_stored{b}") for b in range(2)]
        diag_stored = [sem(f"sc_diag_stored{b}") for b in range(2)]
        v_built = sem("sc_v_built")
        kbd_done = sem("sc_kbd_done")
        prod_done = sem("sc_prod_done")
        diff_done = sem("sc_diff_done")
        capped = sem("sc_capped")
        decay_done = sem("sc_decay_done")
        growth_done = sem("sc_growth_done")
        bdecay_done = sem("sc_bdecay_done")
        qt_done = sem("sc_qt_done")
        at_done = sem("sc_at_done")
        lt_done = sem("sc_lt_done")
        picked_done = sem("sc_picked_done")
        diag_done = sem("sc_diag_done")
        LOADS = 6

        def attention_values(engine):
            engine.wait_ge(zeroed, 2)
            for r in (0, PAD + TS, 2 * PAD + TS + TP):
                engine.dma_start(dr["v_att"][:, r:r + PAD, :].rearrange("g p c -> p g c"), zero[:]).then_inc(v_built, 16)
            for g, f in enumerate(GROUPS):
                for base, at, n in ((PAD, 0, TS), (2 * PAD + TS, TS, TP)):
                    dst = dr["v_att"][g, base:base + n, :].rearrange("(f t) c -> f t c", f=f)
                    src = dr["proj_tok"][at:at + n, V_AT + g * GH * HD:V_AT + (g + 1) * GH * HD].rearrange("(t f) c -> f t c", f=f)
                    engine.dma_start(dst, src).then_inc(v_built, 16)

        with nc.Block() as block:
            @block.sync
            def _(sp):
                sp.dma_start(causal[:], io["causal"]).then_inc(const_in, 16)
                sp.dma_start(own[:], io["own_block"]).then_inc(const_in, 16)

                def load(s, b, i, prompt):
                    if not early(s, 2):
                        sp.wait_ge(prod_done, s - 1)
                        sp.wait_ge(qt_done, s - 1)
                        sp.wait_ge(bdecay_done, s - 1)
                        sp.wait_ge(growth_done, s - 1)
                    for d, chunk in enumerate(places(s, prompt)):
                        half = slice(HD * d, HD * d + HD)
                        one = bass.ds(chunk, 1)
                        sp.dma_start(qk[half, b], dr["qkv_ch"][one, :, 0:2 * NH, :].rearrange("n d h t -> (n d) h t")).then_inc(loaded[b], 16)
                        sp.dma_start(rows[half, b], dr["rows"][d, one].rearrange("n r t -> (n r) t").partition_broadcast(HD)).then_inc(loaded[b], 16)
                        sp.dma_start(cols[half, b].rearrange("p k h -> p (k h)"), dr["cols"][bass.ds(chunk * CH, CH), COLS * d:COLS * d + COLS]).then_inc(loaded[b], 16)

                def store(s, b, i):
                    sp.wait_ge(diag_done, s + 1)
                    sp.dma_start(dr["diag"][:, bass.ds(s, 1)].rearrange("h s r c -> r (h s) c"), diag[:, b]).then_inc(diag_stored[b], 16)

                def turn(s, b, i, prompt):
                    load(s, b, i, prompt)
                    if not early(s, 3):
                        store(s - 3, 1 - b, i - 2 + b)
                steps(sp, turn, peeled=4)
                for s in range(STEPS - 3, STEPS):
                    store(s, s % 2, s // 2)
                for b in range(2):
                    sp.wait_ge(diag_stored[b], 16 * STEPS // 2)

            @block.tensor
            def _(pe):
                def products(s, b, i, prompt):
                    pe.wait_ge(kbd_done, 2 * (s + 1))
                    if not early(s, 2):
                        pe.wait_ge(lt_done, s - 1)
                    both = qk[:, b].rearrange("p (s h) t -> p s h t", s=2)
                    for h in range(NH):
                        mm = pe.matmul(prod[:, b, h, :].rearrange("p (s t) -> p s t", s=2), kbd[:, b, h, :], both[:, :, h, :], start=True, stop=True)
                    mm.then_inc(prod_done, 1)
                steps(pe, products)

            @block.scalar
            def _(act):
                act.wait_ge(zeroed, 2)

                def exponentials(s, b, i, prompt):
                    act.wait_ge(loaded[b], 16 * LOADS * (i + 1))
                    if not early(s, 2):
                        act.wait_ge(prod_done, s - 1)
                    for d in range(2):
                        half = slice(HD * d, HD * d + HD)
                        act.copy(kbd[half, b, :, half], qk[half, b, NH:, :]).then_inc(kbd_done, 1)
                    if not early(s, 2):
                        act.wait_ge(qt_done, s - 1)
                    act.activation(growth[:, b], rows[:, b, NH:, :], ACT.Exp).then_inc(growth_done, 1)
                    act.wait_ge(capped, s + 1)
                    if not early(s, 2):
                        act.wait_ge(lt_done, s - 1)
                    act.activation(decay[:, b], diff[:, b], ACT.Exp).then_inc(decay_done, 1)
                steps(act, exponentials)

            @block.gpsimd
            def _(pool):
                pool.memset(kbd[:], 0.0).then_inc(zeroed, 1)
                pool.memset(zero[:], 0.0).then_inc(zeroed, 1)
                attention_values(pool)
                pool.wait_ge(const_in, 32)

                def scaled(s, b, i, prompt):
                    pool.wait_ge(decay_done, s + 1)
                    pool.tensor_tensor(bdecay[:, b], decay[:, b], rows[:, b, 0:NH, :], ALU.mult).then_inc(bdecay_done, 1)
                    pool.wait_ge(lt_done, s + 1)
                    pool.wait_ge(qt_done, s + 1)
                    pool.dma_start(dr["laq"][bass.ds(s, 1)].rearrange("a p c -> (a p) c"), laq[:, b].rearrange("p k h c -> p (k h c)")).then_inc(laq_stored[b], 16)
                    if not early(s, 2):
                        pool.wait_ge(diag_done, s - 1)
                    pool.tensor_tensor(picked[:, b], laq[:, b, 0], own[:].unsqueeze(1).to_broadcast([P, NH, CH]), ALU.mult).then_inc(picked_done, 1)
                steps(pool, scaled)
                pool.wait_ge(v_built, 16 * 9)
                for b in range(2):
                    pool.wait_ge(laq_stored[b], 16 * STEPS // 2)

            @block.vector
            def _(dve):
                dve.wait_ge(const_in, 32)

                def decays(s, b, i):
                    dve.wait_ge(loaded[b], 16 * LOADS * (i + 1))
                    if not early(s, 2):
                        dve.wait_ge(decay_done, s - 1)
                    dve.tensor_tensor(diff[:, b], rows[:, b, NH:, :], bc_head(cols[:, b, 4, :]), ALU.subtract).then_inc(diff_done, 1)
                    dve.wait_ge(diff_done, s + 1)
                    dve.scalar_tensor_tensor(out=diff[:, b], in0=diff[:, b], scalar=0.0, in1=causal[:].unsqueeze(1).to_broadcast([P, NH, CH]),
                                             op0=ALU.min, op1=ALU.add).then_inc(capped, 1)

                def grown_queries(s, b, i):
                    if not early(s, 2):
                        dve.wait_ge(laq_stored[b], 16 * i)
                    dve.wait_ge(growth_done, s + 1)
                    dve.scalar_tensor_tensor(out=laq[:, b, 2], in0=qk[:, b, 0:NH, :], scalar=HD ** -0.5, in1=growth[:, b],
                                             op0=ALU.mult, op1=ALU.mult).then_inc(qt_done, 1)

                def scaled_products(s, b):
                    dve.wait_ge(prod_done, s + 1)
                    dve.wait_ge(decay_done, s + 1)
                    dve.scalar_tensor_tensor(out=laq[:, b, 1], in0=prod[:, b, :, 0:CH], scalar=HD ** -0.5, in1=decay[:, b],
                                             op0=ALU.mult, op1=ALU.mult).then_inc(at_done, 1)
                    dve.wait_ge(bdecay_done, s + 1)
                    dve.tensor_tensor(laq[:, b, 0], prod[:, b, :, CH:], bdecay[:, b], ALU.mult).then_inc(lt_done, 1)

                def diagonal(s, b, i):
                    if not early(s, 2):
                        dve.wait_ge(diag_stored[b], 16 * i)
                    dve.wait_ge(picked_done, s + 1)
                    dve.tensor_reduce(diag[:, b], picked[:, b].rearrange("p h (k c) -> p h c k", c=BLK), AX.X, ALU.add).then_inc(diag_done, 1)

                def tile(s, b, i, prompt):
                    decays(s, b, i)
                    if not early(s, 2):
                        diagonal(s - 2, b, i - 1)
                    if not early(s, 1):
                        scaled_products(s - 1, 1 - b)
                    grown_queries(s, b, i)
                for c in range(4):
                    tile(c, c % 2, c // 2, False)
                with dve.Fori(2, STEPS // 2) as i:
                    for b in range(2):
                        tile(2 * i + b, b, i, False)
                diagonal(STEPS - 2, 0, STEPS // 2 - 1)
                scaled_products(STEPS - 1, 1)
                diagonal(STEPS - 1, 1, STEPS // 2 - 1)


INV_P = 80
PROBLEMS = 2 * CH // BLK


def inversion(nc, ctx, io, dr, sem):
    sb = lambda n, s, d=F32: ctx.enter_context(nc.sbuf_tensor(n, s, d))
    u = sb("iv_u", [INV_P, 2, PROBLEMS, BLK, BLK])
    x = sb("iv_x", [INV_P, 2, PROBLEMS, BLK, BLK])
    xt = sb("iv_xt", [INV_P, 2, PROBLEMS, BLK, BLK])
    term = sb("iv_term", [INV_P, 2, PROBLEMS * BLK * BLK])
    loaded = sem("iv_loaded")
    negated = sem("iv_negated")
    terms_done = sem("iv_terms_done")
    rows_done = sem("iv_rows_done")
    turned = sem("iv_turned")
    out = sem("iv_out")
    pairs = dr["diag"].rearrange("h s r c -> (h s) (r c)").rearrange("(p n) (d m) -> p d n m", n=2, d=2)
    merged = lambda a: a.rearrange("p d q r c -> p d (q r c)").rearrange("p d (n m) -> p d n m", n=2)

    def program(engine):
        for d in range(2):
            engine.dma_start(merged(u[:])[:, d], pairs[:, d]).then_inc(loaded, 16)
        engine.dma_start(x[:].rearrange("p d q r c -> p (d q) (r c)"), io["blk_ident"].partition_broadcast(INV_P)).then_inc(loaded, 16)
        engine.wait_ge(loaded, 48)
        engine.tensor_scalar(u[:], u[:], -1.0, None, ALU.mult).then_inc(negated, 1)
        engine.wait_ge(negated, 1)
        for n in range(BLK - 1):
            updates = []
            for d in range(2):
                m = BLK - 1 - n if d == 0 else n
                rows, known = (slice(0, m), slice(m, BLK)) if d == 0 else (slice(m + 1, BLK), slice(0, m + 1))
                shape = [INV_P, PROBLEMS, BLK - 1 - n, n + 1]
                t = term[:, d, 0:shape[1] * shape[2] * shape[3]].rearrange("p (q r c) -> p q r c", q=shape[1], r=shape[2])
                if n:
                    engine.wait_ge(rows_done, 2 * (n - 1) + d + 1)
                engine.tensor_tensor(t, u[:, d, :, rows, m].unsqueeze(3).to_broadcast(shape), x[:, d, :, m, known].unsqueeze(2).to_broadcast(shape),
                                     ALU.mult).then_inc(terms_done, 1)
                updates.append((x[:, d, :, rows, known], t))
            for d, (dst, t) in enumerate(updates):
                engine.wait_ge(terms_done, 2 * n + d + 1)
                engine.tensor_tensor(dst, dst, t, ALU.add).then_inc(rows_done, 1)
        engine.wait_ge(rows_done, 2 * (BLK - 1))
        engine.tensor_copy(xt[:].rearrange("p d q r c -> p (d q) r c"), x[:].rearrange("p d q r c -> p (d q) c r")).then_inc(turned, 1)
        engine.wait_ge(turned, 1)
        for form, src in ((0, xt), (1, x)):
            dst = dr["blocks"][form].rearrange("h s r c -> (h s) (r c)").rearrange("(p n) (d m) -> p d n m", n=2, d=2)
            for d in range(2):
                engine.dma_start(dst[:, d], merged(src[:])[:, d]).then_inc(out, 16)
        engine.wait_ge(out, 64)
    return program


def phase_delta(nc, io, dr, load_ahead):
    with ExitStack() as ctx:
        sb = lambda n, s, d=F32: ctx.enter_context(nc.sbuf_tensor(n, s, d))
        ps = lambda n, s: ctx.enter_context(nc.psum_tensor(n, s, F32))
        sem = ctx.enter_context(signals(nc))
        ltb = sb("dl_ltb", [P, 2, NH, P])
        atb = sb("dl_atb", [P, 2, NH, P])
        ka = sb("dl_ka", [P, 2, NH, 2, CH])
        qt = sb("dl_qt", [P, 2, NH, CH])
        blk = sb("dl_blk", [P, 2, 2, NH, BLK])
        kv = sb("dl_kv", [P, 2, 2, NH, HD])
        cols = sb("dl_cols", [P, 2, 5, NH])
        x = sb("dl_x", [P, 2, NH, P])
        xt = sb("dl_xt", [P, 2, NH, P])
        rhs = sb("dl_rhs", [P, 2, NH, 2, HD])
        kdb = sb("dl_kdb", [P, 2, NH, P])
        bg = sb("dl_bg", [P, 2, NH])
        ei = sb("dl_ei", [P, 2, NH, HD])
        prod = sb("dl_prod", [P, NH, P])
        ub = sb("dl_u", [P, NH, HD])
        wb = sb("dl_wb", [P, NH, P])
        mtb = sb("dl_mtb", [P, NH, P])
        qeb = sb("dl_qeb", [P, NH, P])
        state = sb("dl_state", [P, NH, HD])
        ostage = sb("dl_ostage", [P, 2, NH, HD])
        mask16 = sb("dl_mask16", [P, P])
        mask32 = sb("dl_mask32", [P, P])
        spread = sb("dl_spread", [P, P])
        eye64 = sb("dl_eye64", [P, HD])
        halves = sb("dl_halves", [P, P])
        bank = [ps(f"dl_bank{n}", [P, 4, P]) for n in range(8)]
        const_in = sem("dl_const_in")
        zeroed = sem("dl_zeroed")
        loaded = [sem(f"dl_loaded{b}") for b in range(2)]
        stored = [sem(f"dl_stored{b}") for b in range(2)]
        bg_done = sem("dl_bg_done")
        kdec_done = sem("dl_kdec_done")
        x_ready, xt_ready, rhs_ready = sem("dl_x_ready"), sem("dl_xt_ready"), sem("dl_rhs_ready")
        prepared = sem("dl_prepared")
        y1, a1, b1, y2, b2, uw_done, mq_done, o_done, s_done = (sem(f"dl_{n}_done") for n in ("y1", "a1", "b1", "y2", "b2", "uw", "mq", "o", "s"))
        p1_out, x1_out, xt1_out, p2_out, xt2_out, mq_out, state_out = (sem(f"dl_{n}_out") for n in ("p1", "x1", "xt1", "p2", "xt2", "mq", "state"))
        uw_out, o_out = sem("dl_uw_out"), sem("dl_o_out")
        LOADS = 12
        heads = lambda hf: range(4 * hf, 4 * hf + 4)
        four = lambda hf: slice(4 * hf, 4 * hf + 4)
        over = lambda m: m[:].unsqueeze(1).to_broadcast([P, 4, P])

        with nc.Block() as block:
            @block.sync
            def _(sp):
                for dst, name in ((mask16, "mask16"), (mask32, "mask32"), (spread, "spread"), (eye64, "eye64"), (halves, "headsum")):
                    sp.dma_start(dst[:], io[name]).then_inc(const_in, 16)
                sp.wait_ge(zeroed, 1)

                def load(s, b, i, prompt):
                    if not early(s, 2):
                        sp.wait_ge(s_done, 2 * (s - 1))
                    one = dr["laq"][bass.ds(s, 1)].rearrange("a p (k h c) -> (a p) k h c", k=3, h=NH)
                    for d, chunk in enumerate(places(s, prompt)):
                        half = slice(HD * d, HD * d + HD)
                        tok = chunk * CH
                        sp.dma_start(ltb[half, b, :, half], one[half, 0]).then_inc(loaded[b], 16)
                        sp.dma_start(atb[half, b, :, half], one[half, 1]).then_inc(loaded[b], 16)
                        sp.dma_start(kv[half, b].rearrange("p k h c -> p (k h c)"), dr["qkv_tok"][bass.ds(tok, CH), NH * HD:]).then_inc(loaded[b], 16)
                        sp.dma_start(cols[half, b].rearrange("p k h -> p (k h)"), dr["cols"][bass.ds(tok, CH), COLS * d:COLS * d + COLS]).then_inc(loaded[b], 16)
                    sp.dma_start(ka[:, b, :, 1, :], one[:, 1]).then_inc(loaded[b], 16)
                    sp.dma_start(qt[:, b], one[:, 2]).then_inc(loaded[b], 16)
                    for form in range(2):
                        sp.dma_start(blk[:, b, form], dr["blocks"][form, :, bass.ds(s, 1)].rearrange("h s r c -> r (h s) c")).then_inc(loaded[b], 16)

                def store(s, b, i, prompt):
                    sp.wait_ge(o_out, 2 * s + 2)
                    for d, chunk in enumerate(places(s, prompt)):
                        sp.dma_start(dr["o_delta"][d, bass.ds(chunk * CH, CH), :], ostage[HD * d:HD * d + HD, b].rearrange("p h c -> p (h c)")).then_inc(stored[b], 16)

                def turn(s, b, i, prompt):
                    load(s, b, i, prompt)
                    if isinstance(s, int) and s == S_STEPS:
                        load_ahead(sp)
                    if not early(s, 1):
                        store(s - 1, 1 - b, i - (1 - b), prompt and not (isinstance(s, int) and s == S_STEPS))
                steps(sp, turn)
                store(STEPS - 1, 1, STEPS // 2 - 1, True)
                for b in range(2):
                    sp.wait_ge(stored[b], 32 * STEPS // 2)

            @block.gpsimd
            def _(pool):
                for t in (ltb, atb, wb, mtb):
                    pool.memset(t[:], 0.0)
                pool.memset(qeb[:], 0.0).then_inc(zeroed, 1)
                pool.wait_ge(const_in, 80)
                pool.wait_ge(zeroed, 1)

                def prepare(s, b, i, prompt):
                    pool.wait_ge(loaded[b], 16 * LOADS * (i + 1))
                    if not early(s, 2):
                        pool.wait_ge(s_done, 2 * (s - 1))
                    for form, dst, ready in ((0, x, x_ready), (1, xt, xt_ready)):
                        pool.tensor_tensor(dst[:, b].rearrange("p h (k c) -> p h k c", c=BLK), blk[:, b, form].unsqueeze(2).to_broadcast([P, NH, P // BLK, BLK]),
                                           spread[:].rearrange("p (k c) -> p k c", c=BLK).unsqueeze(1).to_broadcast([P, NH, P // BLK, BLK]), ALU.mult).then_inc(ready, 1)
                    pool.tensor_tensor(bg[:, b], cols[:, b, 0, :], cols[:, b, 1, :], ALU.mult).then_inc(bg_done, 1)
                    pool.tensor_tensor(rhs[:, b, :, 0, :], kv[:, b, 1], bc_head(cols[:, b, 0, :]), ALU.mult)
                    pool.wait_ge(bg_done, s + 1)
                    pool.tensor_tensor(rhs[:, b, :, 1, :], kv[:, b, 0], bc_head(bg[:, b]), ALU.mult).then_inc(rhs_ready, 1)
                    pool.tensor_tensor(ka[:, b, :, 0, :], kv[:, b, 0], bc_head(cols[:, b, 2, :]), ALU.mult).then_inc(kdec_done, 1)
                    pool.tensor_tensor(ei[:, b], eye64[:].unsqueeze(1).to_broadcast([P, NH, HD]), bc_head(cols[:, b, 3, :]), ALU.mult)
                    pool.wait_ge(kdec_done, s + 1)
                    pool.tensor_tensor(kdb[:, b].rearrange("p h (d c) -> p h d c", d=2), ka[:, b, :, 0, :].unsqueeze(2).to_broadcast([P, NH, 2, HD]),
                                       halves[:].rearrange("p (d c) -> p d c", d=2).unsqueeze(1).to_broadcast([P, NH, 2, HD]), ALU.mult).then_inc(prepared, 1)
                steps(pool, prepare)

            @block.tensor
            def _(pe):
                def stage(out, lhs, rhs_of, hf, done):
                    for h in heads(hf):
                        mm = pe.matmul(out[:, h - 4 * hf, :], lhs(h), rhs_of(h), start=True, stop=True)
                    mm.then_inc(done, 1)

                def first_products(s, b, i):
                    pe.wait_ge(loaded[b], 16 * LOADS * (i + 1))
                    pe.wait_ge(x_ready, s + 1)
                    for hf in range(2):
                        stage(bank[2 + hf], lambda h: ltb[:, b, h, :], lambda h: x[:, b, h, :], hf, y1)

                def step(s, b, i, prompt):
                    first = isinstance(s, int) and s in (0, S_STEPS)
                    X, XT, PR = (lambda h: x[:, b, h, :]), (lambda h: xt[:, b, h, :]), (lambda h: prod[:, h, :])
                    LT = lambda h: ltb[:, b, h, :]
                    n = lambda hf: 2 * s + hf + 1
                    pe.wait_ge(p1_out, n(1))
                    pe.wait_ge(xt_ready, s + 1)
                    for hf in range(2):
                        stage(bank[2 + 2 * hf], XT, PR, hf, a1)
                        stage(bank[3 + 2 * hf], PR, XT, hf, b1)
                    if not early(s, 1):
                        pe.wait_ge(o_out, 2 * s)
                        pe.wait_ge(state_out, 2 * s)
                    for hf in range(2):
                        pe.wait_ge(x1_out, n(hf))
                        stage(bank[6 + hf], LT, X, hf, y2)
                    for hf in range(2):
                        pe.wait_ge(p2_out, n(hf))
                        pe.wait_ge(xt1_out, n(hf))
                        stage(bank[hf], PR, XT, hf, b2)
                    pe.wait_ge(rhs_ready, s + 1)
                    for hf in range(2):
                        pe.wait_ge(xt2_out, n(hf))
                        stage(bank[2 + hf], XT, lambda h: rhs[:, b, h].rearrange("p k c -> p (k c)"), hf, uw_done)
                    pe.wait_ge(prepared, s + 1)
                    for hf in range(2):
                        pe.wait_ge(uw_out, n(hf))
                        stage(bank[4 + hf], lambda h: wb[:, h, :], lambda h: ka[:, b, h].rearrange("p k c -> p (k c)"), hf, mq_done)
                    for hf in range(2):
                        pe.wait_ge(mq_out, n(hf))
                        for out, own_part, state_part, done in ((bank[6 if hf == 0 else 0], atb, qeb, o_done), (bank[7 if hf == 0 else 1], kdb, mtb, s_done)):
                            for h in heads(hf):
                                o = out[:, h - 4 * hf, 0:HD]
                                mm = pe.matmul(o, own_part[:, b, h, :], ub[:, h, :], start=True, stop=first)
                                if not first:
                                    mm = pe.matmul(o, state_part[:, h, :], state[:, h, :], start=False, stop=True)
                            mm.then_inc(done, 1)
                    if not (isinstance(s, int) and s == STEPS - 1):
                        first_products(s + 1, 1 - b, i + b)
                first_products(0, 0, 0)
                steps(pe, step)

            @block.scalar
            def _(act):
                act.wait_ge(zeroed, 1)

                def step(s, b, i, prompt):
                    for hf in range(2):
                        act.wait_ge(uw_done, 2 * s + hf + 1)
                        uw = bank[2 + hf]
                        act.copy(ub[:, four(hf), :], uw[:, :, 0:HD])
                        act.copy(wb[0:HD, four(hf), 0:HD], uw[0:HD, :, HD:])
                        act.copy(wb[HD:, four(hf), HD:], uw[HD:, :, HD:]).then_inc(uw_out, 1)
                    for hf in range(2):
                        act.wait_ge(o_done, 2 * s + hf + 1)
                        if hf == 0 and not early(s, 2):
                            act.wait_ge(stored[b], 32 * i)
                        act.copy(ostage[:, b, four(hf), :], bank[6 if hf == 0 else 0][:, :, 0:HD]).then_inc(o_out, 1)
                steps(act, step)

            @block.vector
            def _(dve):
                dve.wait_ge(const_in, 80)
                dve.wait_ge(zeroed, 1)

                def first_products(s):
                    for hf in range(2):
                        dve.wait_ge(y1, 2 * s + hf + 1)
                        dve.tensor_tensor(prod[:, four(hf), :], bank[2 + hf][:], over(mask16), ALU.mult).then_inc(p1_out, 1)

                def step(s, b, i, prompt):
                    n = lambda hf: 2 * s + hf + 1
                    for hf in range(2):
                        dve.wait_ge(a1, n(hf))
                        dve.tensor_tensor(x[:, b, four(hf), :], bank[2 + 2 * hf][:], x[:, b, four(hf), :], ALU.add).then_inc(x1_out, 1)
                        dve.wait_ge(b1, n(hf))
                        dve.tensor_tensor(xt[:, b, four(hf), :], bank[3 + 2 * hf][:], xt[:, b, four(hf), :], ALU.add).then_inc(xt1_out, 1)
                    for hf in range(2):
                        dve.wait_ge(y2, n(hf))
                        dve.tensor_tensor(prod[:, four(hf), :], bank[6 + hf][:], over(mask32), ALU.mult).then_inc(p2_out, 1)
                    for hf in range(2):
                        dve.wait_ge(b2, n(hf))
                        dve.wait_ge(xt1_out, n(hf))
                        dve.tensor_tensor(xt[:, b, four(hf), :], bank[hf][:], xt[:, b, four(hf), :], ALU.add).then_inc(xt2_out, 1)
                    for hf in range(2):
                        dve.wait_ge(mq_done, n(hf))
                        mq = bank[4 + hf]
                        for d in range(2):
                            half = slice(HD * d, HD * d + HD)
                            dve.tensor_tensor(mtb[half, four(hf), half], ei[half, b, four(hf), :], mq[half, :, 0:HD], ALU.subtract)
                            last = dve.tensor_tensor(qeb[half, four(hf), half], qt[half, b, four(hf), :], mq[half, :, HD:], ALU.subtract)
                        last.then_inc(mq_out, 1)
                    for hf in range(2):
                        dve.wait_ge(s_done, n(hf))
                        dve.tensor_copy(state[:, four(hf), :], bank[7 if hf == 0 else 1][:, :, 0:HD]).then_inc(state_out, 1)
                    if not (isinstance(s, int) and s == STEPS - 1):
                        first_products(s + 1)
                first_products(0)
                steps(dve, step)


def delta_constants():
    i = np.arange(P)
    d, r, c = (i[:, None] // CH), i[:, None] % CH, np.arange(CH)[None]
    causal = np.where(np.where(d == 0, c >= r, c <= r), 0.0, -1e30)
    own = r // BLK == c // BLK
    rr, cc = i[:, None], i[None]
    same = rr // CH == cc // CH

    def below(n):
        pair = same & (rr // (2 * n) == cc // (2 * n))
        fwd = pair & (rr // CH == 0) & (rr % (2 * n) >= n) & (cc % (2 * n) < n)
        bwd = pair & (rr // CH == 1) & (rr % (2 * n) < n) & (cc % (2 * n) >= n)
        return -(fwd | bwd).astype(np.float32)
    f = lambda a: np.ascontiguousarray(a, np.float32)
    return dict(causal=f(causal), own_block=f(own), mask16=below(16), mask32=below(32), spread=f(rr // BLK == cc // BLK),
                eye64=f(r == c), blk_ident=f(np.broadcast_to(np.eye(BLK).reshape(1, BLK * BLK), (2 * PROBLEMS, BLK * BLK))))


EXPERTS = 16
CAP_S, CAP_P = 2 * TS // EXPERTS, 2 * TP // EXPERTS
SLOTS = CAP_S + CAP_P
HALF = 512
MIXER_WEIGHTS = 4


def shared_weights(nc, ctx, io):
    pieces = {n: ctx.enter_context(nc.sbuf_tensor(f"weights_{n}", [P, KT, HALF], F32)) for n in ("gate0", "up0", "gate1", "up1")}
    wide = {n: t[:].rearrange("p (k a) c -> p k (a c)", a=2) for n, t in pieces.items()}
    mixer = wide["gate0"], wide["up0"][:, 0:2], (wide["gate1"], wide["up1"])
    mixer_ready = nc.alloc_semaphore("mixer_weights_ready")
    pieces_ready = {n: nc.alloc_semaphore(f"expert_{n}_ready") for n in pieces}

    def load_mixer(engine):
        rows = lambda w: w.rearrange("(k p) c -> p k c", p=P)
        for dst, src in ((mixer[0], rows(io["w_proj_a"])), (mixer[1], rows(io["w_proj_b"])),
                         (mixer[2][0], rows(io["w_out"])[:, 0:4]), (mixer[2][1], rows(io["w_out"])[:, 4:])):
            engine.dma_start(dst, src).then_inc(mixer_ready, 16)

    def load_expert(engine):
        for n, t in pieces.items():
            engine.dma_start(t[:], expert_piece(io, n, 0)).then_inc(pieces_ready[n], 16)
    return mixer, mixer_ready, load_mixer, pieces, pieces_ready, load_expert


def expert_piece(io, name, e):
    kind, h = name[:-1], int(name[-1])
    return io[f"w_{kind}"][bass.ds(e, 1), :, h * HALF:(h + 1) * HALF].rearrange("a (k p) c -> p (a k) c", p=P)


def phase_merge(nc, io, dr, ident, weights, weights_ready, load_ahead):
    with ExitStack() as ctx:
        sb = lambda n, s, d=F32: ctx.enter_context(nc.sbuf_tensor(n, s, d))
        ps = lambda n, s: ctx.enter_context(nc.psum_tensor(n, s, F32))
        sem = ctx.enter_context(signals(nc))
        wa, wb, wo = weights
        wr = sb("mg_wr", [P, KT, EXPERTS])
        again = sb("mg_again", [P, HD])
        fgain = sb("mg_fgain", [P, D])
        eps = sb("mg_eps", [P, 1])
        od = sb("mg_od", [P, 2, 2, NH_D := HEADS * HD])
        z = sb("mg_z", [P, 2, NH_D])
        att = sb("mg_att", [P, 2, 3, OUT_W])
        gates = sb("mg_gates", [P, 2, 2 * D])
        xin = sb("mg_x", [P, 2, D])
        on = sb("mg_on", [P, 2, NH_D])
        sq = sb("mg_sq", [P, NH_D])
        st = sb("mg_st", [P, 2, 128])
        wv = sb("mg_wv", [P, 3, GH * HD])
        ob = sb("mg_ob", [P, 2, GH * HD])
        mixin_t = sb("mg_mixin_t", [P, 6, P])
        mix = sb("mg_mix", [P, 2, D])
        gb_part = sb("mg_gb_part", [P, 512])
        mix_t = sb("mg_mix_t", [P, KT, P])
        x2 = sb("mg_x2", [P, 2, D])
        sqx = sb("mg_sqx", [P, D])
        hn = sb("mg_hn", [P, 2, D])
        hn_t = sb("mg_hn_t", [P, KT, P])
        aff = sb("mg_aff", [P, NT, EXPERTS])
        afft = sb("mg_afft", [EXPERTS, T])
        val = sb("mg_val", [EXPERTS, SLOTS])
        idx = sb("mg_idx", [EXPERTS, SLOTS], U32)
        turned = ps("mg_turned", [P, KT, P])
        y = ps("mg_y", [P, 2, 512])
        out = ps("mg_out", [P, 2, 512])
        logit = ps("mg_logit", [P, 512])

        S = {n: sem(f"mg_{n}") for n in (
            "osum", "sq", "sumsq", "ln_on", "rstd_on", "on1", "on2", "silu", "on_done", "m1", "m2", "dm", "eatt", "ed", "den", "rden", "wgt", "wv", "ob_done",
            "sig", "on_turned", "on_t", "y_done", "ga", "gb", "mixed", "mix_turned", "mix_t", "out_done", "x2", "sqx", "ln_x", "rstd_x", "hn", "hn_turned", "hn_t",
            "logits", "lmax", "lneg", "lexp", "lrec", "aff", "aff_turned", "afft", "topk", "const", "eps")}
        inputs = [sem(f"mg_inputs{b}") for b in range(2)]
        x_loaded = [sem(f"mg_x_loaded{b}") for b in range(2)]
        x2_stored = [sem(f"mg_x2_stored{b}") for b in range(2)]
        hn_stored = [sem(f"mg_hn_stored{b}") for b in range(2)]
        chosen_stored = sem("mg_chosen_stored")

        def stages(engine, body):
            for c in range(4):
                body(c, c % 2, c // 2)
            with engine.Fori(2, NT // 2) as i:
                for b in range(2):
                    body(2 * i + b, b, i)
            for c in range(NT, NT + 3):
                body(c, c % 2, c // 2)

        def has(c, lag):
            return not isinstance(c, int) or 0 <= c - lag < NT

        with nc.Block() as block:
            @block.sync
            def _(sp):
                for dst, src in ((again[:], io["a_norm"].partition_broadcast(P)), (fgain[:], io["norm_ffn"].partition_broadcast(P)),
                                 (wr[:], io["w_router"].rearrange("(k p) c -> p k c", p=P))):
                    sp.dma_start(dst, src).then_inc(S["const"], 16)

                def turn(c, b, i):
                    if has(c, 0):
                        if not early(c, 2):
                            sp.wait_ge(S["mixed"], 2 * (c - 1))
                        r = bass.ds(c * P, P)
                        for d in range(2):
                            sp.dma_start(od[:, b, d], dr["o_delta"][d, r, :]).then_inc(inputs[b], 16)
                        sp.dma_start(z[:, b], dr["proj_tok"][r, Z_AT:Z_AT + NH_D]).then_inc(inputs[b], 16)
                        sp.dma_start(att[:, b].rearrange("p g c -> p (g c)"), dr["att_out"][r, :]).then_inc(inputs[b], 16)
                        sp.dma_start(gates[:, b], dr["proj_tok"][r, GATE_AT:GATE_AT + 2 * D]).then_inc(inputs[b], 16)
                    if has(c, 1):
                        if not early(c, 3):
                            sp.wait_ge(S["x2"], 2 * (c - 2))
                        sp.dma_start(xin[:, 1 - b], io["x"][bass.ds((c - 1) * P, P), :]).then_inc(x_loaded[1 - b], 16)
                    if has(c, 2):
                        r = bass.ds((c - 2) * P, P)
                        sp.wait_ge(S["x2"], 2 * (c - 1))
                        sp.dma_start(dr["x2"][r, :], x2[:, b]).then_inc(x2_stored[b], 16)
                        sp.wait_ge(S["hn"], c - 1)
                        sp.dma_start(dr["hn"][r, :], hn[:, b]).then_inc(hn_stored[b], 16)
                stages(sp, turn)
                sp.wait_ge(S["out_done"], 2 * NT)
                load_ahead(sp)
                sp.wait_ge(S["topk"], 1)
                sp.dma_start(dr["idx"], idx[:]).then_inc(chosen_stored, 16)
                sp.dma_start(dr["gate"], val[:]).then_inc(chosen_stored, 16)
                sp.wait_ge(chosen_stored, 32)
                for b in range(2):
                    sp.wait_ge(x2_stored[b], 16 * NT // 2)
                    sp.wait_ge(hn_stored[b], 16 * NT // 2)

            @block.gpsimd
            def _(pool):
                pool.memset(eps[:], EPS).then_inc(S["eps"], 1)
                pool.wait_ge(S["const"], 48)

                def prepare(c, b, i):
                    if not has(c, 0):
                        return
                    pool.wait_ge(inputs[b], 80 * (i + 1))
                    if not early(c, 2):
                        pool.wait_ge(S["on_turned"], c - 1)
                    pool.tensor_tensor(on[:, b], od[:, b, 0], od[:, b, 1], ALU.add).then_inc(S["osum"], 1)
                    pool.wait_ge(S["osum"], c + 1)
                    pool.tensor_tensor(sq[:], on[:, b], on[:, b], ALU.mult).then_inc(S["sq"], 1)
                    heads = on[:, b].rearrange("p (h c) -> p h c", h=HEADS)
                    pool.wait_ge(S["rstd_on"], c + 1)
                    pool.tensor_tensor(heads, heads, bc_head(st[:, b, 0:HEADS]), ALU.mult).then_inc(S["on1"], 1)
                    pool.wait_ge(S["on1"], c + 1)
                    pool.tensor_tensor(heads, heads, again[:].unsqueeze(1).to_broadcast([P, HEADS, HD]), ALU.mult).then_inc(S["on2"], 1)
                    pool.wait_ge(S["on2"], c + 1)
                    pool.wait_ge(S["silu"], c + 1)
                    pool.tensor_tensor(on[:, b], on[:, b], z[:, b], ALU.mult).then_inc(S["on_done"], 1)
                stages(pool, prepare)

            @block.tensor
            def _(pe):
                pe.wait_ge(S["const"], 48)
                pe.wait_ge(weights_ready, 16 * MIXER_WEIGHTS)

                def turn(c, b, i):
                    def half(h):
                        if h == 1 or not early(c, 2):
                            pe.wait_ge(S["ga"], 2 * (c - 1) + h)
                        for k in range(4):
                            mm = pe.matmul(y[:, 0, :], mixin_t[:, k, :], wa[:, k, h * 512:(h + 1) * 512], start=(k == 0), stop=(k == 3))
                        mm.then_inc(S["y_done"], 1)
                        if h == 1 or not early(c, 2):
                            pe.wait_ge(S["gb"], 2 * (c - 1) + h)
                        for k in range(2):
                            mm = pe.matmul(y[:, 1, :], mixin_t[:, 4 + k, :], wb[:, k, h * 512:(h + 1) * 512], start=(k == 0), stop=(k == 1))
                        mm.then_inc(S["y_done"], 1)

                    def project_out(h):
                        if not early(c, 3):
                            pe.wait_ge(S["x2"], 2 * (c - 3) + h + 1)
                        for k in range(KT):
                            mm = pe.matmul(out[:, h, :], mix_t[:, k, :], wo[k // 4][:, k % 4, h * 512:(h + 1) * 512], start=(k == 0), stop=(k == KT - 1))
                        mm.then_inc(S["out_done"], 1)

                    if has(c, 1):
                        pe.wait_ge(S["on_done"], c)
                        pe.wait_ge(S["ob_done"], c)
                        if not early(c, 4):
                            pe.wait_ge(S["hn_t"], c - 3)
                        for k in range(4):
                            pe.transpose(turned[:, k, :], on[:, 1 - b, k * P:(k + 1) * P], ident[:])
                        for k in range(2):
                            mm = pe.transpose(turned[:, 4 + k, :], ob[:, 1 - b, k * P:(k + 1) * P], ident[:])
                        mm.then_inc(S["on_turned"], 1)
                        pe.wait_ge(S["on_t"], c)
                        half(0)
                    if has(c, 2):
                        pe.wait_ge(S["mixed"], 2 * (c - 1))
                        if not has(c, 1):
                            pe.wait_ge(S["hn_t"], c - 3)
                        for k in range(KT):
                            mm = pe.transpose(turned[:, k, :], mix[:, b, k * P:(k + 1) * P], ident[:])
                        mm.then_inc(S["mix_turned"], 1)
                    if has(c, 1):
                        half(1)
                    if has(c, 2):
                        pe.wait_ge(S["mix_t"], c - 1)
                        project_out(0)
                    if has(c, 3):
                        pe.wait_ge(S["hn"], c - 2)
                        for k in range(KT):
                            mm = pe.transpose(turned[:, k, :], hn[:, 1 - b, k * P:(k + 1) * P], ident[:])
                        mm.then_inc(S["hn_turned"], 1)
                    if has(c, 2):
                        project_out(1)
                    if has(c, 3):
                        pe.wait_ge(S["hn_t"], c - 2)
                        if not early(c, 4):
                            pe.wait_ge(S["lexp"], c - 3)
                        for k in range(KT):
                            mm = pe.matmul(logit[:, 0:EXPERTS], hn_t[:, k, :], wr[:, k, :], start=(k == 0), stop=(k == KT - 1))
                        mm.then_inc(S["logits"], 1)
                stages(pe, turn)
                pe.wait_ge(S["aff"], NT)
                for t in range(NT):
                    dst = turned[0:EXPERTS, t, :] if t < KT else out[0:EXPERTS, 0, (t - KT) * P:(t - KT + 1) * P]
                    mm = pe.transpose(dst, aff[:, t, :], ident[:])
                mm.then_inc(S["aff_turned"], 1)

            @block.scalar
            def _(act):
                act.wait_ge(S["const"], 48)
                act.wait_ge(S["eps"], 1)

                def turn(c, b, i):
                    if has(c, 1):
                        act.wait_ge(S["on_turned"], c)
                        act.copy(mixin_t[:], turned[:, 0:6, :]).then_inc(S["on_t"], 1)
                    if has(c, 2):
                        act.wait_ge(S["mix_turned"], c - 1)
                        act.copy(mix_t[:], turned[:]).then_inc(S["mix_t"], 1)
                    if has(c, 0):
                        act.wait_ge(inputs[b], 80 * (i + 1))
                        act.activation(z[:, b], z[:, b], ACT.Silu).then_inc(S["silu"], 1)
                        act.activation(gates[:, b], gates[:, b], ACT.Sigmoid).then_inc(S["sig"], 1)
                        act.wait_ge(S["sumsq"], c + 1)
                        act.activation(st[:, b, 8:16], st[:, b, 8:16], ACT.Ln, bias=eps[:], scale=1.0 / HD).then_inc(S["ln_on"], 1)
                        act.wait_ge(S["ln_on"], c + 1)
                        act.activation(st[:, b, 0:8], st[:, b, 8:16], ACT.Exp, scale=-0.5).then_inc(S["rstd_on"], 1)
                        act.wait_ge(S["dm"], c + 1)
                        act.activation(st[:, b, 16:28], st[:, b, 16:28], ACT.Exp).then_inc(S["eatt"], 1)
                    if has(c, 3):
                        act.wait_ge(S["hn_turned"], c - 2)
                        act.copy(hn_t[:], turned[:]).then_inc(S["hn_t"], 1)
                    if has(c, 2):
                        act.wait_ge(S["x2"], 2 * (c - 1))
                        if not early(c, 3):
                            act.wait_ge(S["sqx"], c - 2)
                        act.activation(sqx[:], x2[:, b], ACT.Square, accum_out=st[:, b, 64:65]).then_inc(S["sqx"], 1)
                        act.wait_ge(S["sqx"], c - 1)
                        act.activation(st[:, b, 65:66], st[:, b, 64:65], ACT.Ln, bias=eps[:], scale=1.0 / D).then_inc(S["ln_x"], 1)
                        act.wait_ge(S["ln_x"], c - 1)
                        act.activation(st[:, b, 66:67], st[:, b, 65:66], ACT.Exp, scale=-0.5).then_inc(S["rstd_x"], 1)
                    if has(c, 3):
                        act.wait_ge(S["lneg"], c - 2)
                        act.activation(st[:, 1 - b, 72:88], logit[:, 0:EXPERTS], ACT.Exp, bias=st[:, 1 - b, 69:70], accum_out=st[:, 1 - b, 70:71]).then_inc(S["lexp"], 1)
                stages(act, turn)

            @block.vector
            def _(dve):
                dve.wait_ge(S["const"], 48)

                def one(name, at, ins):
                    ins.then_inc(S[name], 1)
                    dve.wait_ge(S[name], at)

                def turn(c, b, i):
                    if has(c, 1):
                        o = 1 - b
                        if not early(c, 3):
                            dve.wait_ge(S["mix_turned"], c - 2)
                        dve.wait_ge(S["sig"], c)
                        for h in range(2):
                            cols = slice(h * 512, h * 512 + 512)
                            n = 2 * (c - 1) + h + 1
                            dve.wait_ge(S["y_done"], 2 * n - 1)
                            dve.tensor_tensor(mix[:, o, cols], y[:, 0, :], gates[:, o, cols], ALU.mult).then_inc(S["ga"], 1)
                            dve.wait_ge(S["y_done"], 2 * n)
                            dve.tensor_tensor(gb_part[:], y[:, 1, :], gates[:, o, D + h * 512:D + h * 512 + 512], ALU.mult).then_inc(S["gb"], 1)
                            dve.wait_ge(S["gb"], n)
                            one("mixed", n, dve.tensor_tensor(mix[:, o, cols], mix[:, o, cols], gb_part[:], ALU.add))
                    if has(c, 0):
                        s = lambda lo, n: st[:, b, lo:lo + n]
                        dve.wait_ge(S["sq"], c + 1)
                        dve.tensor_reduce(s(8, 8), sq[:].rearrange("p (h c) -> p h c", h=HEADS), AX.X, ALU.add).then_inc(S["sumsq"], 1)
                        dve.wait_ge(inputs[b], 80 * (i + 1))
                        m = att[:, b, :, GH * HD:GH * HD + GH]
                        den = att[:, b, :, GH * HD + GH:OUT_W]
                        one("m1", c + 1, dve.tensor_tensor(s(28, 4), m[:, 0, :], m[:, 1, :], ALU.max))
                        one("m2", c + 1, dve.tensor_tensor(s(28, 4), s(28, 4), m[:, 2, :], ALU.max))
                        e = s(16, 12).rearrange("p (g h) -> p g h", g=3)
                        dve.tensor_tensor(e, m, s(28, 4).unsqueeze(1).to_broadcast([P, 3, GH]), ALU.subtract).then_inc(S["dm"], 1)
                        dve.wait_ge(S["eatt"], c + 1)
                        ed = s(32, 12).rearrange("p (g h) -> p g h", g=3)
                        one("ed", c + 1, dve.tensor_tensor(ed, e, den, ALU.mult))
                        one("den", c + 1, dve.tensor_reduce(s(44, 4), ed.rearrange("p g h -> p h g"), AX.X, ALU.add))
                        one("rden", c + 1, dve.reciprocal(s(44, 4), s(44, 4)))
                        one("wgt", c + 1, dve.tensor_tensor(ed, e, s(44, 4).unsqueeze(1).to_broadcast([P, 3, GH]), ALU.mult))
                        for g in range(3):
                            last = dve.tensor_tensor(wv[:, g].rearrange("p (h c) -> p h c", h=GH), att[:, b, g, 0:GH * HD].rearrange("p (h c) -> p h c", h=GH),
                                                     s(32 + GH * g, GH).unsqueeze(2).to_broadcast([P, GH, HD]), ALU.mult)
                        one("wv", c + 1, last)
                        if not early(c, 2):
                            dve.wait_ge(S["on_turned"], c - 1)
                        dve.tensor_reduce(ob[:, b], wv[:].rearrange("p g c -> p c g"), AX.X, ALU.add).then_inc(S["ob_done"], 1)
                        dve.wait_ge(S["ob_done"], c + 1)
                    if has(c, 2):
                        if not early(c, 4):
                            dve.wait_ge(x2_stored[b], 16 * (i - 1))
                            dve.wait_ge(hn_stored[b], 16 * (i - 1))
                        dve.wait_ge(x_loaded[b], 16 * i)
                        for h in range(2):
                            cols = slice(h * 512, h * 512 + 512)
                            dve.wait_ge(S["out_done"], 2 * (c - 2) + h + 1)
                            dve.tensor_tensor(x2[:, b, cols], out[:, h, :], xin[:, b, cols], ALU.add).then_inc(S["x2"], 1)
                        dve.wait_ge(S["rstd_x"], c - 1)
                        if not early(c, 4):
                            dve.wait_ge(S["hn_turned"], c - 3)
                        dve.scalar_tensor_tensor(out=hn[:, b], in0=x2[:, b], scalar=st[:, b, 66:67], in1=fgain[:], op0=ALU.mult, op1=ALU.mult).then_inc(S["hn"], 1)
                    if has(c, 3):
                        o = 1 - b
                        dve.wait_ge(S["logits"], c - 2)
                        one("lmax", c - 2, dve.tensor_reduce(st[:, o, 68:69], logit[:, 0:EXPERTS], AX.X, ALU.max))
                        dve.tensor_scalar(st[:, o, 69:70], st[:, o, 68:69], -1.0, None, ALU.mult).then_inc(S["lneg"], 1)
                        dve.wait_ge(S["lexp"], c - 2)
                        one("lrec", c - 2, dve.reciprocal(st[:, o, 71:72], st[:, o, 70:71]))
                        dve.tensor_scalar(aff[:, bass.ds(c - 3, 1), :].rearrange("p a e -> p (a e)"), st[:, o, 72:88], st[:, o, 71:72], None, ALU.mult).then_inc(S["aff"], 1)
                stages(dve, turn)

                dve.wait_ge(S["aff_turned"], 1)
                for n, (dst, src) in enumerate(((afft[:, 0:TS].rearrange("e (t p) -> e t p", p=P), turned[0:EXPERTS]), (afft[:, TS:], out[0:EXPERTS, 0, 0:TP]))):
                    one("afft", n + 1, dve.tensor_copy(dst, src))
                n = 2
                for lo, size, at, cap in ((0, TS, 0, CAP_S), (TS, TP, CAP_S, CAP_P)):
                    seg = afft[:, lo:lo + size]
                    for r in range(cap // 8):
                        cols = slice(at + 8 * r, at + 8 * r + 8)
                        n += 1
                        one("afft", n, dve.max(out=val[:, cols], in_=seg))
                        dve.max_index(out=idx[:, cols], in_max=val[:, cols], in_values=seg)
                        n += 1
                        one("afft", n, dve.match_replace(out=seg, in_to_replace=val[:, cols], in_values=seg, imm_value=-1.0))
                dve.tensor_scalar(idx[:, CAP_S:], idx[:, CAP_S:], TS, None, ALU.add).then_inc(S["topk"], 1)


DE = 1024
FT = DE // P


def phase_experts(nc, io, dr, ident, pieces, pieces_ready):
    with ExitStack() as ctx:
        sb = lambda n, s, d=F32: ctx.enter_context(nc.sbuf_tensor(n, s, d))
        ps = lambda n, s: ctx.enter_context(nc.psum_tensor(n, s, F32))
        sem = ctx.enter_context(signals(nc))
        PIECES = ("gate0", "up0", "gate1", "up1", "down0", "down1")
        w = {n: pieces[n] if n in pieces else sb(f"ex_{n}", [P, KT, HALF]) for n in PIECES}
        gather_idx = [sb("ex_gidx_s", [CAP_S, 1], U32), sb("ex_gidx_p", [CAP_P, 1], U32)]
        scatter_idx = [sb("ex_sidx_s", [CAP_S, 1], U32), sb("ex_sidx_p", [CAP_P, 1], U32)]
        gain_s = sb("ex_gain_s", [CAP_S, EXPERTS])
        gain_p = sb("ex_gain_p", [CAP_P, EXPERTS])
        xs = sb("ex_xs", [CAP_S, D])
        xp = sb("ex_xp", [CAP_P, D])
        xt = sb("ex_xt", [P, KT, SLOTS])
        sg = sb("ex_sg", [P, 2, SLOTS])
        ht = sb("ex_ht", [P, FT, SLOTS])
        yt = sb("ex_yt", [P, KT, SLOTS])
        ys = sb("ex_ys", [CAP_S, D])
        yp = sb("ex_yp", [CAP_P, D])
        g_acc = ps("ex_g_acc", [P, 2, 512])
        u_acc = ps("ex_u_acc", [P, 2, 512])
        y_acc = ps("ex_y_acc", [P, 2, 512])
        turned = ps("ex_turned", [P, 2, 512])

        w_ready = {n: pieces_ready[n] if n in pieces else sem(f"ex_{n}_ready") for n in PIECES}
        gains_ready = sem("ex_gains_ready")
        gidx_ready = sem("ex_gidx_ready")
        sidx_ready = sem("ex_sidx_ready")
        gathered = sem("ex_gathered")
        turns = sem("ex_turns")
        scattered = sem("ex_scattered")
        x_turned = sem("ex_x_turned")
        xt_act, xt_dve = sem("ex_xt_act"), sem("ex_xt_dve")
        g_done, u_done = sem("ex_g_done"), sem("ex_u_done")
        silu_done, h_done = sem("ex_silu_done"), sem("ex_h_done")
        y_done = sem("ex_y_done")
        yt_act, yt_dve = sem("ex_yt_act"), sem("ex_yt_dve")
        y_turned = sem("ex_y_turned")
        ys_act, ys_dve = sem("ex_ys_act"), sem("ex_ys_dve")

        def experts(engine, body):
            body(0)
            with engine.Fori(1, EXPERTS - 1) as e:
                body(e)
            body(EXPERTS - 1)

        def last(e):
            return isinstance(e, int) and e == EXPERTS - 1

        with nc.Block() as block:
            @block.sync
            def _(sp):
                def weights(e):
                    for n, name in enumerate(PIECES):
                        if early(e, 1) and name in pieces:
                            continue
                        if not early(e, 1):
                            done, tiles = (u_done, FT) if n < 4 else (y_done, KT)
                            sp.wait_ge(done, tiles * (e - 1) + (tiles // 2 if name[-1] == "0" else tiles))
                        sp.dma_start(w[name][:], expert_piece(io, name, e)).then_inc(w_ready[name], 16)

                def indices(e, dst, ready):
                    for buf, (lo, hi) in zip(dst, ((0, CAP_S), (CAP_S, SLOTS))):
                        sp.dma_start(buf[:], dr["idx"][bass.ds(e, 1), lo:hi].rearrange("a n -> n a")).then_inc(ready, 16)

                indices(0, gather_idx, gidx_ready)
                weights(0)
                sp.dma_start(gain_s[:], dr["gate"][:, 0:CAP_S].rearrange("e n -> n e"), allow_slow_non_contiguous=True).then_inc(gains_ready, 16)
                sp.dma_start(gain_p[:], dr["gate"][:, CAP_S:].rearrange("e n -> n e"), allow_slow_non_contiguous=True).then_inc(gains_ready, 16)

                def turn(e):
                    if not last(e):
                        sp.wait_ge(gathered, 32 * (e + 1))
                        indices(e + 1, gather_idx, gidx_ready)
                    if not early(e, 1):
                        if not early(e, 2):
                            sp.wait_ge(scattered, 32 * (e - 1))
                        indices(e - 1, scatter_idx, sidx_ready)
                    if not last(e):
                        weights(e + 1)
                turn(0)
                turn(1)
                with sp.Fori(2, EXPERTS - 1) as e:
                    turn(e)
                turn(EXPERTS - 1)
                sp.wait_ge(scattered, 32 * (EXPERTS - 1))
                indices(EXPERTS - 1, scatter_idx, sidx_ready)

            @block.gpsimd
            def _(pool):
                def gather(e):
                    pool.wait_ge(gidx_ready, 32 * (e + 1))
                    if not early(e, 1):
                        pool.wait_ge(x_turned, 3 * e)
                    pool.sem_inc(turns, 1)
                    for buf, ix in ((xs, gather_idx[0]), (xp, gather_idx[1])):
                        pool.indirect_dma_start(out=buf[:], out_offset=None, in_=dr["hn"], in_offset=bass.IndirectOffsetOnAxis(ap=ix[:, 0:1], axis=0)).then_inc(gathered, 16)

                def scatter(e):
                    pool.wait_ge(sidx_ready, 32 * (e + 1))
                    pool.wait_ge(ys_act, 2 * (e + 1))
                    pool.wait_ge(ys_dve, 2 * (e + 1))
                    if not early(e, 1):
                        pool.wait_ge(scattered, 32 * e)
                    pool.sem_inc(turns, 1)
                    for buf, ix in ((ys, scatter_idx[0]), (yp, scatter_idx[1])):
                        pool.indirect_dma_start(out=dr["x2"], out_offset=bass.IndirectOffsetOnAxis(ap=ix[:, 0:1], axis=0), in_=buf[:], in_offset=None,
                                                compute_op=ALU.add).then_inc(scattered, 16)
                gather(0)
                gather(1)
                gather(2)
                scatter(0)
                with pool.Fori(2, EXPERTS - 1) as e:
                    gather(e + 1)
                    scatter(e - 1)
                scatter(EXPERTS - 2)
                scatter(EXPERTS - 1)
                pool.wait_ge(scattered, 32 * EXPERTS)

            @block.tensor
            def _(pe):
                def turn_in(e):
                    pe.wait_ge(gathered, 32 * (e + 1))
                    for k in range(KT):
                        bank = (turned[:, 0], turned[:, 1], y_acc[:, 1])[k // 3]
                        at = (k % 3) * SLOTS
                        pe.transpose(bank[:, at:at + CAP_S], xs[:, k * P:(k + 1) * P], ident[:])
                        mm = pe.transpose(bank[:, at + CAP_S:at + SLOTS], xp[:, k * P:(k + 1) * P], ident[0:CAP_P, 0:CAP_P])
                        if k in (2, 5, 7):
                            mm.then_inc(x_turned, 1)

                def turn_back(e, n):
                    slots = (slice(0, CAP_S), slice(CAP_S, SLOTS))[n]
                    if n:
                        pe.wait_ge(ys_act, 2 * e + 1)
                        pe.wait_ge(ys_dve, 2 * e + 1)
                    else:
                        pe.wait_ge(yt_act, 4 * (e + 1))
                        pe.wait_ge(yt_dve, 4 * (e + 1))
                    for k in range(KT):
                        mm = pe.transpose(turned[0:slots.stop - slots.start, k // 4, (k % 4) * P:(k % 4 + 1) * P], yt[:, k, slots], ident[:])
                    mm.then_inc(y_turned, 1)

                def turn(e):
                    pe.wait_ge(xt_act, 2 * (e + 1))
                    pe.wait_ge(xt_dve, e + 1)
                    for f in range(FT):
                        if f % 4 == 0:
                            pe.wait_ge(w_ready[f"gate{f // 4}"], 16 * (e + 1))
                        if f >= 2 or not early(e, 1):
                            pe.wait_ge(h_done, FT * e + f - 1)
                        for k in range(KT):
                            mm = pe.matmul(g_acc[:, f % 2, 0:SLOTS], w[f"gate{f // 4}"][:, k, (f % 4) * P:(f % 4 + 1) * P], xt[:, k, :], start=(k == 0), stop=(k == KT - 1))
                        mm.then_inc(g_done, 1)
                        if f % 4 == 0:
                            pe.wait_ge(w_ready[f"up{f // 4}"], 16 * (e + 1))
                        for k in range(KT):
                            mm = pe.matmul(u_acc[:, f % 2, 0:SLOTS], w[f"up{f // 4}"][:, k, (f % 4) * P:(f % 4 + 1) * P], xt[:, k, :], start=(k == 0), stop=(k == KT - 1))
                        mm.then_inc(u_done, 1)
                        if f == 1 and not early(e, 1):
                            turn_back(e - 1, 0)
                        if f == 4 and not early(e, 1):
                            turn_back(e - 1, 1)
                    if not last(e):
                        if not early(e, 1):
                            pe.wait_ge(ys_act, 2 * e)
                            pe.wait_ge(ys_dve, 2 * e)
                        turn_in(e + 1)
                    for d in range(KT):
                        if d % 4 == 0:
                            pe.wait_ge(w_ready[f"down{d // 4}"], 16 * (e + 1))
                        if d == 0:
                            pe.wait_ge(h_done, FT * (e + 1))
                        if d >= 2:
                            pe.wait_ge((yt_act, yt_dve)[d % 2], 4 * e + d // 2)
                        if d == 1:
                            pe.wait_ge(xt_act, 2 * (e + 2) if not last(e) else 2 * (e + 1))
                        for k in range(FT):
                            mm = pe.matmul(y_acc[:, d % 2, 0:SLOTS], w[f"down{d // 4}"][:, k, (d % 4) * P:(d % 4 + 1) * P], ht[:, k, :], start=(k == 0), stop=(k == FT - 1))
                        mm.then_inc(y_done, 1)

                turn_in(0)
                experts(pe, turn)
                turn_back(EXPERTS - 1, 0)
                turn_back(EXPERTS - 1, 1)

            @block.scalar
            def _(act):
                def x_out(e):
                    act.wait_ge(x_turned, 3 * e + 1)
                    act.copy(xt[:, 0:3, :], turned[:, 0, 0:3 * SLOTS].rearrange("p (k n) -> p k n", k=3)).then_inc(xt_act, 1)
                    act.wait_ge(x_turned, 3 * e + 3)
                    act.copy(xt[:, 6:8, :], y_acc[:, 1, 0:2 * SLOTS].rearrange("p (k n) -> p k n", k=2)).then_inc(xt_act, 1)

                def y_out(e, n):
                    act.wait_ge(gains_ready, 32)
                    act.wait_ge(y_turned, 2 * e + n + 1)
                    if n == 0 and not early(e, 1):
                        act.wait_ge(scattered, 32 * e)
                    rows, dst, gain = ((CAP_S, ys, gain_s), (CAP_P, yp, gain_p))[n]
                    act.activation(dst[:, 0:HALF], turned[0:rows, 0, :], ACT.Copy, scale=gain[:, bass.ds(e, 1)]).then_inc(ys_act, 1)

                def turn(e):
                    for f in range(FT):
                        act.wait_ge(g_done, FT * e + f + 1)
                        if f >= 2 or not early(e, 1):
                            act.wait_ge(h_done, FT * e + f - 1)
                        act.activation(sg[:, f % 2], g_acc[:, f % 2, 0:SLOTS], ACT.Silu).then_inc(silu_done, 1)
                        if f in (1, 4) and not early(e, 1):
                            y_out(e - 1, int(f == 4))
                    if not last(e):
                        x_out(e + 1)
                    for d in range(0, KT, 2):
                        act.wait_ge(y_done, KT * e + d + 1)
                        act.copy(yt[:, d, :], y_acc[:, 0, 0:SLOTS]).then_inc(yt_act, 1)
                x_out(0)
                experts(act, turn)
                y_out(EXPERTS - 1, 0)
                y_out(EXPERTS - 1, 1)

            @block.vector
            def _(dve):
                def x_out(e):
                    dve.wait_ge(x_turned, 3 * e + 2)
                    dve.tensor_copy(xt[:, 3:6, :], turned[:, 1, 0:3 * SLOTS].rearrange("p (k n) -> p k n", k=3)).then_inc(xt_dve, 1)

                def y_out(e, n):
                    dve.wait_ge(gains_ready, 32)
                    dve.wait_ge(y_turned, 2 * e + n + 1)
                    if n == 0 and not early(e, 1):
                        dve.wait_ge(scattered, 32 * e)
                    rows, dst, gain = ((CAP_S, ys, gain_s), (CAP_P, yp, gain_p))[n]
                    dve.tensor_scalar(dst[:, HALF:], turned[0:rows, 1, :], gain[:, bass.ds(e, 1)], None, ALU.mult).then_inc(ys_dve, 1)

                def turn(e):
                    for f in range(FT):
                        dve.wait_ge(silu_done, FT * e + f + 1)
                        dve.wait_ge(u_done, FT * e + f + 1)
                        dve.tensor_tensor(ht[:, f, :], u_acc[:, f % 2, 0:SLOTS], sg[:, f % 2], ALU.mult).then_inc(h_done, 1)
                        if f in (1, 4) and not early(e, 1):
                            y_out(e - 1, int(f == 4))
                    if not last(e):
                        x_out(e + 1)
                    for d in range(1, KT, 2):
                        dve.wait_ge(y_done, KT * e + d + 1)
                        dve.tensor_copy(yt[:, d, :], y_acc[:, 1, 0:SLOTS]).then_inc(yt_dve, 1)
                x_out(0)
                experts(dve, turn)
                y_out(EXPERTS - 1, 0)
                y_out(EXPERTS - 1, 1)


def phase_final(nc, io, dr, y):
    with ExitStack() as ctx:
        sb = lambda n, s, d=F32: ctx.enter_context(nc.sbuf_tensor(n, s, d))
        sem = ctx.enter_context(signals(nc))
        xall = sb("fn_x", [P, NT, D])
        sq = sb("fn_sq", [P, D])
        gain = sb("fn_gain", [P, D])
        ss = sb("fn_ss", [P, 3, NT])
        loaded = [sem("fn_loaded_a"), sem("fn_loaded_b")]
        gain_in = sem("fn_gain_in")
        sumsq, mean_done, inv_done, rstd_done, y_done, out = (sem(f"fn_{n}") for n in ("sumsq", "mean", "inv", "rstd", "y", "out"))
        H = NT // 2
        tiles = lambda a, h: a[h * H * P:(h + 1) * H * P].rearrange("(t p) c -> p t c", p=P)
        with nc.Block() as block:
            @block.sync
            def _(sp):
                for h in range(2):
                    sp.dma_start(xall[:, h * H:(h + 1) * H, :], tiles(dr["x2"], h)).then_inc(loaded[h], 16)
                sp.dma_start(gain[:], io["norm_final"].partition_broadcast(P)).then_inc(gain_in, 16)
                for t in range(NT):
                    sp.wait_ge(y_done, t + 1)
                    sp.dma_start(y[t * P:(t + 1) * P, :], xall[:, t, :]).then_inc(out, 16)
                sp.wait_ge(out, 16 * NT)

            @block.scalar
            def _(act):
                for t in range(NT):
                    if t % H == 0:
                        act.wait_ge(loaded[t // H], 16)
                    if t:
                        act.wait_ge(sumsq, t)
                    act.activation(sq[:], xall[:, t, :], ACT.Square, accum_out=ss[:, 0, t:t + 1]).then_inc(sumsq, 1)
                    if t % H == H - 1:
                        act.wait_ge(inv_done, t // H + 1)
                        act.activation(ss[:, 2, t - H + 1:t + 1], ss[:, 1, t - H + 1:t + 1], ACT.Sqrt).then_inc(rstd_done, 1)

            @block.vector
            def _(dve):
                dve.wait_ge(gain_in, 16)
                for h in range(2):
                    cols = slice(h * H, h * H + H)
                    dve.wait_ge(sumsq, H * (h + 1))
                    dve.tensor_scalar(ss[:, 1, cols], ss[:, 0, cols], 1.0 / D, EPS, ALU.mult, ALU.add).then_inc(mean_done, 1)
                    dve.wait_ge(mean_done, h + 1)
                    dve.reciprocal(ss[:, 1, cols], ss[:, 1, cols]).then_inc(inv_done, 1)
                    dve.wait_ge(rstd_done, h + 1)
                    for t in range(h * H, h * H + H):
                        dve.scalar_tensor_tensor(out=xall[:, t, :], in0=xall[:, t, :], scalar=ss[:, 2, t:t + 1], in1=gain[:], op0=ALU.mult, op1=ALU.mult).then_inc(y_done, 1)


def layer(nc, io, y):
    dram = lambda n, s, d=F32: nc.dram_tensor(n, s, d, kind="Internal").ap()
    dr = dict(
        qkv_ch=dram("qkv_ch", [STEPS, HD, A_TILES * P // HD, CH]), qkv_tok=dram("qkv_tok", [T, A_TILES * P]),
        qk_att=dram("qk_att", [A_TILES * P, QK_COLS]), proj_tok=dram("proj_tok", [T, TOK_COLS]),
        cols=dram("cols", [T, 2 * COLS]), rows=dram("rows", [2, STEPS, 2 * HEADS, CH]),
        v_att=dram("v_att", [3, V_ROWS, GH * HD]), att_out=dram("att_out", [T, 3 * OUT_W]),
        laq=dram("laq", [STEPS, P, 3 * NH * CH]), diag=dram("diag", [NH, STEPS, P, BLK]), blocks=dram("blocks", [2, NH, STEPS, P, BLK]),
        o_delta=dram("o_delta", [2, T, NH * HD]), x2=dram("x2", [T, D]), hn=dram("hn", [T, D]),
        idx=dram("idx", [EXPERTS, SLOTS], U32), gate=dram("gate", [EXPERTS, SLOTS]),
    )
    with nc.sbuf_tensor("identity", [P, P], F32) as ident:
        with nc.sbuf_tensor("normed", [P, KT, T], F32R) as normed, nc.sbuf_tensor("normed_rest", [P, KT, T], F32R) as normed_lo:
            phase_norm(nc, io, normed, normed_lo, ident)
            phase_channels(nc, io, dr, normed, normed_lo, ident)
            phase_tokens(nc, io, dr, normed, normed_lo)
        phase_decay(nc, io, dr, ident)
        phase_scores(nc, io, dr)
        phase_attention(nc, io, dr, ident)
        with ExitStack() as ctx:
            mixer, mixer_ready, load_mixer, pieces, pieces_ready, load_expert = shared_weights(nc, ctx, io)
            phase_delta(nc, io, dr, load_mixer)
            phase_merge(nc, io, dr, ident, mixer, mixer_ready, load_expert)
            phase_experts(nc, io, dr, ident, pieces, pieces_ready)
        phase_final(nc, io, dr, y)


def constants():
    i = np.arange(P)
    same = i[:, None] // CH == i[None] // CH
    tri = np.stack([same & (i[:, None] <= i[None]), same & (i[:, None] >= i[None]), same], 1)
    power = np.zeros((P, A_TILES))
    power[:, :2 * NH * HD // P] = -0.5
    f = lambda a: np.ascontiguousarray(a, np.float32)
    return dict(ident=f(np.eye(P)), tri=f(tri), norm_power=f(power), headsum=f(same), att_bias=attention_bias(), **delta_constants())


def laid_out(inputs):
    a = {n: np.asarray(v) for n, v in inputs.items()}
    tiled = lambda w, width: np.ascontiguousarray(w.reshape(KT, P, -1, width).transpose(2, 1, 0, 3))
    w_in = a["w_in"][0]
    qkv_a = A_TILES * P
    qk_b = 2 * 3 * GH * HD
    z_end = qkv_a + TOK_COLS - (3 * GH * HD + 2 * D)
    return dict(
        x=np.concatenate([a["x_sample"][0], a["x_prompt"][0]]),
        norm_mix=a["norm_mix"], norm_ffn=a["norm_ffn"], norm_final=a["norm_final"].reshape(1, D), a_norm=a["a_norm"],
        w_ch=tiled(np.concatenate([w_in[:, :qkv_a], w_in[:, z_end:z_end + qk_b]], 1), P),
        w_tok=tiled(np.concatenate([w_in[:, qkv_a:z_end], w_in[:, z_end + qk_b:]], 1), TOK_BLOCK),
        conv_w=np.ascontiguousarray(a["conv_w"][0].T.reshape(A_TILES, P, CONV).transpose(1, 0, 2)),
        a_log=a["a_log"].reshape(1, 2 * HEADS), dt_bias=a["dt_bias"].reshape(1, 2 * HEADS),
        w_proj_a=a["w_proj_a"][0], w_proj_b=a["w_proj_b"][0], w_out=a["w_out"][0], w_router=a["w_router"][0],
        w_gate=a["w_gate"][0], w_up=a["w_up"][0], w_down=a["w_down"][0],
    )


def kernel(**inputs):
    import concourse.bacc as bacc
    from concourse.bass_utils import run_bass_kernel_spmd

    nc = bacc.Bacc("TRN2", target_bir_lowering=False, num_devices=1)
    arrays = {f"in_{n}": np.ascontiguousarray(v) for n, v in {**laid_out(inputs), **constants()}.items()}
    io = {n[3:]: nc.dram_tensor(n, a.shape, mybir.dt.from_np(a.dtype), kind="ExternalInput").ap() for n, a in arrays.items()}
    y = nc.dram_tensor("y", [T, D], F32, kind="ExternalOutput").ap()
    layer(nc, io, y)
    got = run_bass_kernel_spmd(nc, [arrays], core_ids=[0]).results[0]["y"]
    return got[TS:].reshape(1, TP, D), got[:TS].reshape(1, TS, D)
```
